# Optimizing a Trainium2 kernel written in Bass

```python
import math
import jax, jax.numpy as jnp
from jax import lax
import numpy as np

D_MODEL = 1024
BATCH = 1
SEQ = 1024
DEPTH = 1

PLE_DIM = 256
C_RW = D_MODEL // 2
RW_HEAD = 64
RW_HEADS = C_RW // RW_HEAD
DECAY_LORA = 64
AAA_LORA = 64
GATE_LORA = 128
RW_COLS = 3 * C_RW + 2 * DECAY_LORA + 2 * AAA_LORA + GATE_LORA
RW_GN_EPS = RW_HEAD * 1e-5
C_DA = D_MODEL - C_RW
DA_HEADS = 4
DA_V_DIM = C_DA // DA_HEADS
DA_QK_DIM = DA_V_DIM // 2
DA_COLS = 3 * C_DA
IN_COLS = RW_COLS + DA_COLS
D_MIX = C_RW + C_DA
Q_BLOCK = 128
N_EXPERTS = 32
TOP_K = 4
D_FF = D_MODEL
SWIGLU_ALPHA = 1.702
SWIGLU_LIMIT = 7.0
EXPERT_BLOCK = 128
NORM_EPS = 1e-6

kernel_name = "hybrid_rwkv7_diffattn_moe_encoder"

def rmsnorm(x, g, eps=NORM_EPS):
    xf = x.astype(jnp.float32)
    y = xf * lax.rsqrt(jnp.mean(xf * xf, axis=-1, keepdims=True) + eps)
    return y * g.astype(jnp.float32)

def centred_shift(z):
    zp = jnp.pad(z, ((0, 0), (1, 1), (0, 0)))
    return 0.5 * (zp[:, :-2] + zp[:, 2:])

def rwkv7_bidirectional(z, mu, w0, w2, a0, a2, g2, k_k, k_a, r_k, ln_g, ln_b):
    B, T, _ = z.shape
    H, N = RW_HEADS, RW_HEAD
    z = z.astype(jnp.float32)
    z = z + (centred_shift(z) - z) * mu
    idx = [C_RW, 2 * C_RW, 3 * C_RW, 3 * C_RW + 2 * DECAY_LORA,
           3 * C_RW + 2 * DECAY_LORA + 2 * AAA_LORA]
    r, k, v, wd, ad, gd = jnp.split(z, idx, axis=-1)
    wd = wd.reshape(B, T, 2, DECAY_LORA)
    ad = ad.reshape(B, T, 2, AAA_LORA)
    w_log = -jax.nn.softplus(-(w0 + jnp.einsum('btdr,drc->btdc', jnp.tanh(wd), w2))) - 0.5
    decay = jnp.exp(-jnp.exp(w_log))
    a = jax.nn.sigmoid(a0 + jnp.einsum('btdr,drc->btdc', ad, a2))
    g = jax.nn.sigmoid(gd) @ g2
    kk = (k * k_k).reshape(B, T, H, N)
    kk = kk * lax.rsqrt(jnp.sum(kk * kk, axis=-1, keepdims=True) + 1e-12)
    kk = kk.reshape(B, T, C_RW)
    k_dir = k[:, :, None, :] * (1.0 + (a - 1.0) * k_a)
    b_dir = kk[:, :, None, :] * a

    def to_time_major(x_fwd, x_bwd):
        s = jnp.stack([x_fwd, jnp.flip(x_bwd, axis=1)], axis=0).astype(jnp.float32)
        return s.reshape(2, B, T, H, N).transpose(2, 0, 1, 3, 4)

    xs = (to_time_major(r, r),
          to_time_major(decay[:, :, 0], decay[:, :, 1]),
          to_time_major(k_dir[:, :, 0], k_dir[:, :, 1]),
          to_time_major(v, v),
          to_time_major(-kk, -kk),
          to_time_major(b_dir[:, :, 0], b_dir[:, :, 1]))

    def step(S, inp):
        r_t, w_t, k_t, v_t, a_t, b_t = inp
        sa = jnp.einsum('dbhvk,dbhk->dbhv', S, a_t)
        S = S * w_t[..., None, :] + sa[..., None] * b_t[..., None, :] + v_t[..., None] * k_t[..., None, :]
        y = jnp.einsum('dbhvk,dbhk->dbhv', S, r_t)
        return S, y

    S0 = jnp.zeros((2, B, H, N, N), jnp.float32)
    _, ys = lax.scan(step, S0, xs)
    y = ys[:, 0] + jnp.flip(ys[:, 1], axis=0)
    y = y.transpose(1, 0, 2, 3)
    mean = jnp.mean(y, axis=-1, keepdims=True)
    var = jnp.mean(jnp.square(y - mean), axis=-1, keepdims=True)
    y = (y - mean) * lax.rsqrt(var + RW_GN_EPS) * ln_g + ln_b
    k_bonus = jnp.mean(k_dir, axis=2).reshape(B, T, H, N)
    rh = r.reshape(B, T, H, N)
    vh = v.reshape(B, T, H, N)
    bonus = jnp.sum(rh * k_bonus * r_k, axis=-1, keepdims=True) * vh
    return (y + bonus).reshape(B, T, C_RW) * g

def diff_attention(zq, zk, zv, q_norm_g, k_norm_g, lq1, lk1, lq2, lk2, subln_g, lambda_init):
    B, T, _ = zq.shape
    H, D, E = DA_HEADS, DA_QK_DIM, DA_V_DIM
    q = rmsnorm(zq.reshape(B, T, H, 2, D), q_norm_g)
    k = rmsnorm(zk.reshape(B, T, H, 2, D), k_norm_g)
    v = zv.astype(jnp.float32).reshape(B, T, H, E)
    lq1, lk1, lq2, lk2 = (t.astype(jnp.float32) for t in (lq1, lk1, lq2, lk2))
    lam = jnp.exp(jnp.sum(lq1 * lk1)) - jnp.exp(jnp.sum(lq2 * lk2)) + lambda_init
    scale = 1.0 / math.sqrt(D)
    slopes = 2.0 ** (-8.0 * jnp.arange(1, H + 1, dtype=jnp.float32) / H)
    n_blocks = T // Q_BLOCK
    qb = q.reshape(B, n_blocks, Q_BLOCK, H, 2, D).transpose(1, 0, 2, 3, 4, 5)
    pos_k = jnp.arange(T, dtype=jnp.int32)

    def block(args):
        q_blk, bi = args
        pos_q = bi * Q_BLOCK + jnp.arange(Q_BLOCK, dtype=jnp.int32)
        dist = jnp.abs(pos_q[:, None] - pos_k[None, :]).astype(jnp.float32)
        s = jnp.einsum('bqhcd,bkhcd->bhcqk', q_blk, k) * scale
        s = s - slopes[:, None, None, None] * dist
        pm = jax.nn.softmax(s, axis=-1)
        attn = pm[:, :, 0] - lam * pm[:, :, 1]
        return jnp.einsum('bhqk,bkhe->bqhe', attn, v)

    o = lax.map(block, (qb, jnp.arange(n_blocks, dtype=jnp.int32)))
    o = o.transpose(1, 0, 2, 3, 4).reshape(B, T, H, E)
    o = rmsnorm(o, subln_g) * (1.0 - lambda_init)
    return o.reshape(B, T, H * E)

def routed_experts(xs, ids, gates, w1, b1, w2, b2):
    Tn = xs.shape[0]
    M = Tn * TOP_K
    e_flat = ids.reshape(M)
    g_flat = gates.reshape(M)
    order = jnp.argsort(e_flat)
    se = e_flat[order]
    stok = (order // TOP_K).astype(jnp.int32)
    sg = g_flat[order]
    counts = jnp.bincount(e_flat, length=N_EXPERTS)
    padded = (counts + EXPERT_BLOCK - 1) // EXPERT_BLOCK * EXPERT_BLOCK
    pend = jnp.cumsum(padded)
    pstart = pend - padded
    cstart = jnp.cumsum(counts) - counts
    dest = pstart[se] + jnp.arange(M, dtype=jnp.int32) - cstart[se]
    n_blk = (M + N_EXPERTS * (EXPERT_BLOCK - 1) + EXPERT_BLOCK - 1) // EXPERT_BLOCK
    P = n_blk * EXPERT_BLOCK
    row_tok = jnp.zeros((P,), jnp.int32).at[dest].set(stok)
    row_gate = jnp.zeros((P,), jnp.float32).at[dest].set(sg.astype(jnp.float32))
    blk_start = jnp.arange(n_blk, dtype=pend.dtype) * EXPERT_BLOCK
    blk_e = jnp.minimum(jnp.searchsorted(pend, blk_start, side='right'), N_EXPERTS - 1)
    xb = xs[row_tok].reshape(n_blk, EXPERT_BLOCK, xs.shape[-1])

    def expert_block(args):
        x_blk, e = args
        hcat = x_blk @ w1[e] + b1[e]
        glu = jnp.minimum(hcat[:, :D_FF], SWIGLU_LIMIT)
        lin = jnp.clip(hcat[:, D_FF:], -SWIGLU_LIMIT, SWIGLU_LIMIT)
        act = glu * jax.nn.sigmoid(SWIGLU_ALPHA * glu) * (lin + 1.0)
        return (act @ w2[e] + b2[e]).astype(jnp.float32)

    yb = lax.map(expert_block, (xb, blk_e)).reshape(P, -1)
    return jnp.zeros((Tn, yb.shape[-1]), jnp.float32).at[row_tok].add(yb * row_gate[:, None])

def moe(xn, w_router, b_router, w1, b1, w2, b2):
    logits = (xn @ w_router + b_router).astype(jnp.float32)
    vals, idx = lax.top_k(logits, TOP_K)
    gates = jax.nn.softmax(vals, axis=-1)

    def per_seq(args):
        xs, ids, gs = args
        return routed_experts(xs, ids, gs, w1, b1, w2, b2)

    return lax.map(per_seq, (xn, idx.astype(jnp.int32), gates))

def setup_inputs(seed: int = 0) -> dict:
    key = jax.random.key(seed)
    ks = iter(jax.random.split(key, 48))
    L = DEPTH
    f32 = jnp.float32

    def nrm(shape, scale):
        return jax.random.normal(next(ks), shape, f32) * scale

    def gain(shape):
        return 1.0 + nrm(shape, 0.02)

    return {
        "x": nrm((BATCH, SEQ, D_MODEL), 1.0),
        "p": nrm((DEPTH, BATCH, SEQ, PLE_DIM), 1.0),
        "norm_mix_g": gain((L, D_MODEL)),
        "w_in": nrm((L, D_MODEL, IN_COLS), D_MODEL ** -0.5),
        "rw_mu": jax.random.uniform(next(ks), (L, RW_COLS), f32, 0.0, 1.0),
        "rw_w0": jax.random.uniform(next(ks), (L, 2, C_RW), f32, -6.0, -1.0),
        "rw_w2": nrm((L, 2, DECAY_LORA, C_RW), 0.1 * DECAY_LORA ** -0.5),
        "rw_a0": nrm((L, 2, C_RW), 0.1),
        "rw_a2": nrm((L, 2, AAA_LORA, C_RW), 0.1 * AAA_LORA ** -0.5),
        "rw_g2": nrm((L, GATE_LORA, C_RW), GATE_LORA ** -0.5),
        "rw_k_k": 0.85 + nrm((L, C_RW), 0.02),
        "rw_k_a": gain((L, C_RW)),
        "rw_r_k": nrm((L, RW_HEADS, RW_HEAD), 0.1),
        "rw_ln_g": gain((L, RW_HEADS, RW_HEAD)),
        "rw_ln_b": nrm((L, RW_HEADS, RW_HEAD), 0.01),
        "da_q_norm_g": gain((L, DA_QK_DIM)),
        "da_k_norm_g": gain((L, DA_QK_DIM)),
        "da_lq1": nrm((L, DA_QK_DIM), 0.1),
        "da_lk1": nrm((L, DA_QK_DIM), 0.1),
        "da_lq2": nrm((L, DA_QK_DIM), 0.1),
        "da_lk2": nrm((L, DA_QK_DIM), 0.1),
        "da_subln_g": gain((L, DA_V_DIM)),
        "w_out": nrm((L, D_MIX, D_MODEL), D_MIX ** -0.5),
        "norm_ffn_g": gain((L, D_MODEL)),
        "w_router": nrm((L, D_MODEL, N_EXPERTS), D_MODEL ** -0.5),
        "b_router": nrm((L, N_EXPERTS), 0.01),
        "w1": nrm((L, N_EXPERTS, D_MODEL, 2 * D_FF), D_MODEL ** -0.5),
        "b1": nrm((L, N_EXPERTS, 2 * D_FF), 0.01),
        "w2": nrm((L, N_EXPERTS, D_FF, D_MODEL), D_FF ** -0.5),
        "b2": nrm((L, N_EXPERTS, D_MODEL), 0.01),
        "w_ple": nrm((L, PLE_DIM, D_MODEL), PLE_DIM ** -0.5),
        "ple_norm_g": gain((L, D_MODEL)),
        "w_ple_gate": nrm((L, D_MODEL, D_MODEL), D_MODEL ** -0.5),
    }

def reference(x, p, norm_mix_g, w_in, rw_mu, rw_w0, rw_w2, rw_a0, rw_a2, rw_g2,
              rw_k_k, rw_k_a, rw_r_k, rw_ln_g, rw_ln_b, da_q_norm_g, da_k_norm_g,
              da_lq1, da_lk1, da_lq2, da_lk2, da_subln_g, w_out, norm_ffn_g,
              w_router, b_router, w1, b1, w2, b2, w_ple, ple_norm_g, w_ple_gate):
    h = x.astype(jnp.float32)
    for i in range(DEPTH):
        lambda_init = 0.8 - 0.6 * math.exp(-0.3 * i)
        u = rmsnorm(h, norm_mix_g[i]).astype(x.dtype)
        z = u @ w_in[i]
        z_rw = z[..., :RW_COLS]
        z_q = z[..., RW_COLS:RW_COLS + C_DA]
        z_k = z[..., RW_COLS + C_DA:RW_COLS + 2 * C_DA]
        z_v = z[..., RW_COLS + 2 * C_DA:]
        o_rw = rwkv7_bidirectional(z_rw, rw_mu[i], rw_w0[i], rw_w2[i], rw_a0[i], rw_a2[i],
                                   rw_g2[i], rw_k_k[i], rw_k_a[i], rw_r_k[i],
                                   rw_ln_g[i], rw_ln_b[i])
        o_da = diff_attention(z_q, z_k, z_v, da_q_norm_g[i], da_k_norm_g[i],
                              da_lq1[i], da_lk1[i], da_lq2[i], da_lk2[i],
                              da_subln_g[i], lambda_init)
        o = jnp.concatenate([o_rw, o_da], axis=-1).astype(x.dtype)
        h = h + (o @ w_out[i]).astype(jnp.float32)
        m = rmsnorm(h, norm_ffn_g[i]).astype(x.dtype)
        h = h + moe(m, w_router[i], b_router[i], w1[i], b1[i], w2[i], b2[i])
        e = rmsnorm(p[i] @ w_ple[i], ple_norm_g[i])
        gate = jax.nn.sigmoid((h.astype(x.dtype) @ w_ple_gate[i]).astype(jnp.float32))
        h = h + e * gate
    return h.astype(x.dtype)


_drawn_inputs = setup_inputs


def setup_inputs(seed=0):
    import zlib

    import numpy as np

    out = dict(_drawn_inputs(seed))
    spreads = {}
    factors = {'rw_w2': 8.0,
     'rw_k_a': 2.959,
     'rw_ln_g': 9.854,
     'rw_ln_b': 14.93,
     'da_lk2': 8.466,
     'b1': 25.387,
     'b2': 28.935,
     'ple_norm_g': 23.008,
     'rw_k_k': 2.873,
     'da_q_norm_g': 5.399,
     'da_k_norm_g': 4.635,
     'da_lq1': 2.671,
     'da_lk1': 4.235,
     'da_subln_g': 5.104,
     'norm_ffn_g': 2.969,
     'b_router': 4.158}
    for name, (base, spread) in spreads.items():
        noise = np.random.default_rng([zlib.crc32(name.encode()), seed]).standard_normal(out[name].shape)
        drawn = base * np.exp(spread * noise) if base else spread * noise
        out[name] = __import__('jax').numpy.asarray(drawn.astype(out[name].dtype))
    for name, factor in factors.items():
        out[name] = (out[name] * factor).astype(out[name].dtype)
    return out
```

```python
import math
from contextlib import ExitStack

import concourse.bass as bass
from concourse import mybir
from concourse.alu_op_type import AluOpType as ALU

F32 = mybir.dt.float32
BF16 = mybir.dt.bfloat16
U32 = mybir.dt.uint32
I32 = mybir.dt.int32
ACT = mybir.ActivationFunctionType
AX = mybir.AxisListType

P = 128
T, D = 1024, 1024
NT = T // P
ND = D // P
HALF = 512
C_RW = D // 2
RW_TILES = C_RW // P
HEAD = 64
CHUNK = 64
NCH = T // CHUNK
LORA = 64
RW_COLS = 3 * C_RW + 4 * LORA + 128
C_DA = D - C_RW
DA_HEADS = 4
IN_COLS = RW_COLS + 3 * C_DA
IN_TILES = IN_COLS // P
EXPERTS, TOP_K, D_FF = 32, 4, D
PLE = 256
BLOCKS = (T * TOP_K + EXPERTS * P) // P
ROWS = (BLOCKS + T // P) * P
NORM_EPS = 1e-6
RW_GN_EPS = HEAD * 1e-5
LAMBDA_INIT = 0.8 - 0.6 * math.exp(0.0)
DECAY = math.exp(-0.5)


def row(ap, i, n=1):
    return ap[bass.ds(i, n)]


class Steps:

    def __init__(self, text):
        self.names = text.split()
        self.n = len(self.names)

    def __call__(self, name, i=0):
        return self.names.index(name) + 1 + i * self.n


class Line:

    def __init__(self, eng, sem, steps, i=0, base=0):
        self.eng, self.sem, self.steps, self.i, self.base, self.at = eng, sem, steps, i, base, 0

    def __call__(self, name, instruction):
        assert self.steps.names[self.at] == name, (name, self.steps.names[self.at])
        self.at += 1
        instruction.then_inc(self.sem, 1)
        self.eng.wait_ge(self.sem, self.steps(name, self.i) + self.base)


def constants(nc, k):
    with nc.semaphore("const_made") as made, nc.Block() as block:

        @block.gpsimd
        def _(pool):
            n = 0

            def select(t, pattern, mult, base, op, fill):
                nonlocal n
                pool.wait_ge(made, n)
                pool.affine_select(out=t, in_=t, compare_op=op, fill=fill, base=base,
                                   pattern=pattern, channel_multiplier=mult).then_inc(made, 1)
                n += 1

            def fill(t, v):
                nonlocal n
                pool.memset(t, v).then_inc(made, 1)
                n += 1

            def blocks(t, size):
                v = t.rearrange("p (b s) -> p b s", s=size)
                m = P // size
                select(v, [[-size, m], [0, size]], 1, 0, ALU.is_ge, 0.0)
                select(v, [[size, m], [0, size]], -1, size - 1, ALU.is_ge, 0.0)

            fill(k.ident[:], 0.0)
            select(k.ident[:], [[-1, P]], 1, 0, ALU.not_equal, 1.0)
            fill(k.ones[:], 1.0)
            fill(k.zeros[:], 0.0)
            fill(k.head_ones[:], 1.0)
            blocks(k.head_ones[:], HEAD)
            fill(k.before[:], 1.0)
            select(k.before[:], [[1, P]], -1, 0, ALU.is_gt, 0.0)
            for d in range(2):
                s = 1 - 2 * d
                for kind, op in ((0, ALU.is_gt), (1, ALU.is_ge)):
                    fill(k.causal[:, d, kind, :], 1.0)
                    select(k.causal[:, d, kind, :], [[s, P]], -s, 0, op, 0.0)
                    blocks(k.causal[:, d, kind, :], CHUNK)
                    fill(k.causal[:, d, 2 + kind, :], 1.0)
                    select(k.causal[:, d, 2 + kind, :], [[s, P]], -s, 0, op, 0.0)
                    blocks(k.causal[:, d, 2 + kind, :], CHUNK)
            for level, size in enumerate((16, 32, 64)):
                fill(k.near[:, level, :], 1.0)
                blocks(k.near[:, level, :], size)
            for level in (2, 1):
                pool.wait_ge(made, n)
                pool.tensor_tensor(k.near[:, level, :], k.near[:, level, :], k.near[:, level - 1, :],
                                   ALU.subtract).then_inc(made, 1)
                n += 1
            fill(k.chunk_col[:], 1.0)
            v = k.chunk_col[:]
            select(v[:, 0:1], [[0, 1]], -1, CHUNK - 1, ALU.is_ge, 0.0)
            select(v[:, 1:2], [[0, 1]], 1, -CHUNK, ALU.is_ge, 0.0)
            fill(k.scan_keep[:], 1.0)
            v = k.scan_keep[:].rearrange("p (c s) -> p c s", s=CHUNK)
            select(v, [[0, NCH], [1, CHUNK]], 0, 0, ALU.not_equal, 0.0)
            fill(k.eps[:, 0:1], NORM_EPS)
            fill(k.eps[:, 1:2], 1e-12)
            fill(k.eps[:, 2:3], RW_GN_EPS)
            pool.wait_ge(made, n)


def normed_columns(nc, k, x, gain, uT):
    with ExitStack() as ctx:
        sb = lambda name, shape, dt=F32: ctx.enter_context(nc.sbuf_tensor(name, shape, dt))
        sem = lambda name: ctx.enter_context(nc.semaphore(name))
        xt = [sb(f"xt{s}", [P, D]) for s in range(2)]
        xn = [sb(f"xn{s}", [P, D]) for s in range(2)]
        sq = [sb(f"sq{s}", [P, D]) for s in range(2)]
        ssq = sb("ssq", [P, 2, 4])
        gcol = sb("gcol", [P, ND])
        ps = [ctx.enter_context(nc.psum_tensor(f"tp{s}", [P, D], F32)) for s in range(2)]
        x_loaded = [sem(f"x_loaded{s}") for s in range(2)]
        gain_loaded = sem("gain_loaded")
        act_done, dve_done, transposed = sem("a_done"), sem("v_done"), sem("transposed")
        A = Steps("ssq0 root0 ssq1 root1")
        V = Steps("inv0 xn0 out0 inv1 xn1 out1")
        block = ctx.enter_context(nc.Block())
        PAIRS = NT // 2

        @block.sync
        def _(sp):
            with nc.allow_non_contiguous_dma(reason="gain columns"):
                sp.dma_start(gcol[:], gain.rearrange("(n p) -> p n", p=P)).then_inc(gain_loaded, 16)
            sp.wait_ge(gain_loaded, 16)
            with sp.Fori(0, PAIRS) as j:
                for s in range(2):
                    first = sp.snap(j * 2 * P + s * P)
                    sp.wait_ge(dve_done, j * V.n)
                    sp.dma_start(xt[s][:], row(x, first, P)).then_inc(x_loaded[s], 16)

        @block.scalar
        def _(act):
            with act.Fori(0, PAIRS) as j:
                for s in range(2):
                    act.wait_ge(x_loaded[s], j * 16 + 16)
                    act.wait_ge(dve_done, j * V.n)
                    nc.scalar.activation(sq[s][:], xt[s][:], ACT.Square,
                                         accum_out=ssq[:, s, 0:1]).then_inc(act_done, 1)
                    act.wait_ge(act_done, A(f"ssq{s}", j))
                    nc.scalar.activation(ssq[:, s, 1:2], ssq[:, s, 0:1], ACT.Sqrt, bias=k.eps[:, 0:1],
                                         scale=1.0 / D).then_inc(act_done, 1)

        @block.vector
        def _(dve):
            with dve.Fori(0, PAIRS) as j:
                for s in range(2):
                    dve.wait_ge(act_done, A(f"root{s}", j))
                    nc.vector.reciprocal(ssq[:, s, 2:3], ssq[:, s, 1:2]).then_inc(dve_done, 1)
                    dve.wait_ge(dve_done, V(f"inv{s}", j))
                    dve.wait_ge(transposed, j * 2)
                    nc.vector.tensor_scalar(xn[s][:], xt[s][:], ssq[:, s, 2:3], None,
                                            ALU.mult).then_inc(dve_done, 1)
                    dve.wait_ge(transposed, j * 2 + s + 1)
                    nc.vector.tensor_tensor(
                        uT[:, :, bass.ds(j * 2 * P + s * P, P)],
                        ps[s][:].rearrange("p (n t) -> p n t", t=P),
                        gcol[:].unsqueeze(2).to_broadcast([P, ND, P]), ALU.mult).then_inc(dve_done, 1)
            dve.wait_ge(gain_loaded, 16)

        @block.tensor
        def _(pe):
            with pe.Fori(0, PAIRS) as j:
                for s in range(2):
                    pe.wait_ge(dve_done, V(f"xn{s}", j))
                    for n in range(ND):
                        last = nc.tensor.transpose(ps[s][:, n * P:(n + 1) * P], xn[s][:, n * P:(n + 1) * P],
                                                   k.ident[:])
                    last.then_inc(transposed, 1)


def project_in(nc, k, uT, w_in, zT):
    R = 3
    with ExitStack() as ctx:
        sb = lambda name, shape, dt=F32: ctx.enter_context(nc.sbuf_tensor(name, shape, dt))
        sem = lambda name: ctx.enter_context(nc.semaphore(name))
        w = [sb(f"win{s}", [P, ND, P]) for s in range(R)]
        z = [sb(f"z{s}", [P, T]) for s in range(R)]
        ps = [ctx.enter_context(nc.psum_tensor(f"zp{s}", [P, T], F32)) for s in range(R)]
        w_loaded = [sem(f"w_loaded{s}") for s in range(R)]
        z_stored = [sem(f"z_stored{s}") for s in range(R)]
        multiplied = [sem(f"multiplied{s}") for s in range(R)]
        copied = [sem(f"copied{s}") for s in range(R)]
        block = ctx.enter_context(nc.Block())
        w_view = w_in.rearrange("(kt p) n -> p kt n", p=P)

        @block.sync
        def _(sp):
            with sp.Fori(0, IN_TILES // R) as j:
                for s in range(R):
                    first = sp.snap(j * R * P + s * P)
                    sp.wait_ge(multiplied[s], j)
                    sp.dma_start(w[s][:], w_view[:, :, bass.ds(first, P)]).then_inc(w_loaded[s], 16)

        @block.gpsimd
        def _(pool):
            with pool.Fori(0, IN_TILES // R) as j:
                for s in range(R):
                    pool.wait_ge(copied[s], j * 2 + 2)
                    pool.dma_start(row(zT, j * R * P + s * P, P), z[s][:]).then_inc(z_stored[s], 16)
            for s in range(R):
                pool.wait_ge(z_stored[s], 16 * (IN_TILES // R))

        @block.tensor
        def _(pe):
            with pe.Fori(0, IN_TILES // R) as j:
                for s in range(R):
                    pe.wait_ge(w_loaded[s], j * 16 + 16)
                    pe.wait_ge(copied[s], j * 2)
                    for h in range(2):
                        for kt in range(ND):
                            last = nc.tensor.matmul(ps[s][:, h * HALF:(h + 1) * HALF], w[s][:, kt, :],
                                                    uT[:, kt, h * HALF:(h + 1) * HALF],
                                                    start=(kt == 0), stop=(kt == ND - 1))
                    last.then_inc(multiplied[s], 1)

        def copies(eng, copy, half):
            with eng.Fori(0, IN_TILES // R) as j:
                for s in range(R):
                    eng.wait_ge(multiplied[s], j + 1)
                    eng.wait_ge(z_stored[s], j * 16)
                    cols = slice(half * HALF, (half + 1) * HALF)
                    copy(z[s][:, cols], ps[s][:, cols]).then_inc(copied[s], 1)

        @block.scalar
        def _(act):
            copies(act, nc.scalar.copy, 0)

        @block.vector
        def _(dve):
            copies(dve, nc.vector.tensor_copy, 1)


def rwkv_prepare(nc, k, zT, mu, w0, w2, a0, a2, k_k, k_a, r_k, ops, vals, bonus, gate_in, end_decay):
    with ExitStack() as ctx:
        sb = lambda name, shape, dt=F32: ctx.enter_context(nc.sbuf_tensor(name, shape, dt))
        sem = lambda name: ctx.enter_context(nc.semaphore(name))
        low = [sb(f"low{i}", [P, T + 2]) for i in range(3)]
        zin = [sb(f"zin{i}", [P, T + 2]) for i in range(3)]
        rkv = [sb(f"rkv{i}", [P, T]) for i in range(3)]
        mixc = sb("mixc", [P, 3, RW_COLS // P])
        par = sb("par", [P, 4, 5 + 3])
        parv = sb("parv", [P, 8, 4])
        lw_w = [sb(f"lora{i}", [P, P]) for i in range(4)]
        tmp = [sb(f"tmp{i}", [P, T]) for i in range(3)]
        kk = sb("kk", [P, T])
        lwt = sb("lwt", [P, T])
        rate = sb("rate", [P, T])
        acc = sb("accl", [P, T])
        inc = sb("inc", [P, T])
        exc = sb("exc", [P, T])
        kdir = [sb(f"kdir{d}", [P, T]) for d in range(2)]
        res = sb("res", [P, 4, T])
        dec = sb("dec", [P, NCH])
        tot = sb("tot", [P, NCH])
        psA = ctx.enter_context(nc.psum_tensor("psA", [P, T], F32))
        psB = ctx.enter_context(nc.psum_tensor("psB", [P, T], F32))
        psC = ctx.enter_context(nc.psum_tensor("psC", [P, T], F32))
        par_loaded, lora_loaded = sem("par_loaded"), sem("lora_loaded")
        low_loaded, z_loaded = sem("low_loaded"), sem("z_loaded")
        edge, acts, dves, pes = sem("edge"), sem("acts"), sem("dves"), sem("pes")
        stored, res_stored = sem("stored"), sem("res_stored")
        kept = sem("kept")
        low_stored = sem("low_stored")

        V0 = Steps("one_minus half s0 m0 o0 s1 m1 o1 s2 m2 o2 omka")
        A0 = Steps("tanh sig")
        V = Steps("sr mr rr sk mk rk sv mv rv kkr kkinv kk "
                  "lw0 scan0 inc0 exc0 m0 kd0 a0 r0 bb0 b0 k0 "
                  "lw1 scan1 tot1 exc1 inc1 m1 kd1 a1 r1 bb1 b1 k1 "
                  "kb q0 q1 bv")
        A = Steps("sq root sw0 sa0 ex0 in0 en0 dc0 sw1 sa1 ex1 in1 en1 dc1")
        M = Steps("norm w0 a0 w1 a1 bonus")
        block = ctx.enter_context(nc.Block())
        mu_v = mu.rearrange("(n p) -> p n", p=P)

        @block.sync
        def _(sp):
            with nc.allow_non_contiguous_dma(reason="per-channel parameters as columns"):
                sp.dma_start(mixc[:, 0, :], mu_v).then_inc(par_loaded, 16)
                for d in range(2):
                    sp.dma_start(parv[:, 0 + d, :], w0[d].rearrange("(n p) -> p n", p=P)).then_inc(par_loaded, 16)
                    sp.dma_start(parv[:, 2 + d, :], a0[d].rearrange("(n p) -> p n", p=P)).then_inc(par_loaded, 16)
                for i, v in enumerate((k_k, k_a, r_k)):
                    sp.dma_start(parv[:, 4 + i, :], v.rearrange("(n p) -> p n", p=P)).then_inc(par_loaded, 16)
            sp.wait_ge(edge, 2)
            for i in range(3):
                n = 3 * RW_TILES + i
                sp.dma_start(low[i][:, 1:T + 1], zT[n * P:(n + 1) * P, :]).then_inc(low_loaded, 16)
            with sp.Fori(0, RW_TILES) as c:
                first = sp.snap(c * P)
                sources = [row(zT[i * C_RW:(i + 1) * C_RW], first, P) for i in range(3)]
                sp.wait_ge(dves, V0.n + c * V.n)
                for i in range(3):
                    sp.dma_start(zin[i][:, 1:T + 1], sources[i]).then_inc(z_loaded, 16)

        @block.gpsimd
        def _(pool):
            for t in low + zin:
                pool.memset(t[:, 0:1], 0.0)
                last = pool.memset(t[:, T + 1:T + 2], 0.0)
            last.then_inc(edge, 1)
            for t in lw_w:
                last = pool.memset(t[:], 0.0)
            last.then_inc(edge, 1)
            pool.wait_ge(acts, A0("sig"))
            pool.dma_start(gate_in, low[2][:, 1:T + 1]).then_inc(low_stored, 16)
            pool.wait_ge(low_stored, 16)
            with pool.Fori(0, RW_TILES) as c:
                for d in range(2):
                    pool.wait_ge(dves, V(f"k{d}", c) + V0.n)
                    pool.wait_ge(edge, 2)
                    pool.dma_start(row(ops[d], c * P, P), res[:]).then_inc(res_stored, 16)
                    pool.wait_ge(acts, A(f"dc{d}", c) + A0.n)
                    pool.wait_ge(edge, 2)
                    pool.dma_start(row(end_decay[d], c * P, P), dec[:]).then_inc(stored, 16)
                pool.wait_ge(dves, V("bv", c) + V0.n)
                pool.wait_ge(edge, 2)
                pool.dma_start(row(vals, c * P, P), rkv[2][:]).then_inc(kept, 16)
                pool.dma_start(row(bonus, c * P, P), tmp[2][:]).then_inc(kept, 16)

            for s in (res_stored, stored, kept):
                pool.wait_ge(s, 32 * RW_TILES)

        def shift(line, names, src, out, scr, n):
            line(names[0], nc.vector.tensor_tensor(scr[:], src[:, 0:T], src[:, 2:T + 2], ALU.add))
            line(names[1], nc.vector.tensor_scalar(scr[:], scr[:], mixc[:, 2, n], None, ALU.mult))
            line(names[2], nc.vector.scalar_tensor_tensor(out=out, in0=src[:, 1:T + 1], scalar=mixc[:, 1, n],
                                                          in1=scr[:], op0=ALU.mult, op1=ALU.add))

        @block.vector
        def _(dve):
            line = Line(dve, dves, V0)
            dve.wait_ge(par_loaded, 16 * 8)
            line("one_minus", nc.vector.tensor_scalar(mixc[:, 1, :], mixc[:, 0, :], -1.0, 1.0, ALU.mult, ALU.add))
            line("half", nc.vector.tensor_scalar(mixc[:, 2, :], mixc[:, 0, :], 0.5, None, ALU.mult))
            dve.wait_ge(low_loaded, 48)
            for i in range(3):
                n = 3 * RW_TILES + i
                shift(line, (f"s{i}", f"m{i}", f"o{i}"), low[i], low[i][:, 1:T + 1], tmp[0], slice(n, n + 1))
            line("omka", nc.vector.tensor_scalar(parv[:, 7, :], parv[:, 5, :], -1.0, 1.0, ALU.mult, ALU.add))
            with dve.Fori(0, RW_TILES) as c:
                line = Line(dve, dves, V, c, V0.n)
                mul = lambda out, x, y: nc.vector.tensor_tensor(out, x, y, ALU.mult)
                col = lambda j: parv[:, j, bass.ds(c, 1)]
                dve.wait_ge(z_loaded, c * 48 + 48)
                dve.wait_ge(kept, c * 32)
                for i, x in enumerate("rkv"):
                    shift(line, (f"s{x}", f"m{x}", f"r{x}"), zin[i], rkv[i][:], tmp[0], bass.ds(c + i * RW_TILES, 1))
                r, ky, v = rkv
                line("kkr", nc.vector.tensor_scalar(tmp[1][:], ky[:], col(4), None, ALU.mult))
                dve.wait_ge(acts, A0.n + A("root", c))
                line("kkinv", nc.vector.reciprocal(tmp[0][:], tmp[0][:]))
                line("kk", mul(kk[:], tmp[1][:], tmp[0][:]))
                for d in range(2):
                    dve.wait_ge(acts, A0.n + A(f"sw{d}", c))
                    line(f"lw{d}", nc.vector.tensor_scalar(lwt[:], lwt[:], -DECAY, None, ALU.mult))
                    line(f"scan{d}", nc.vector.tensor_tensor_scan(acc[:], k.scan_keep[:], lwt[:], 0.0,
                                                                  ALU.mult, ALU.add))
                    if d == 0:
                        line("inc0", nc.vector.tensor_copy(inc[:], acc[:]))
                        line("exc0", nc.vector.tensor_tensor(exc[:], acc[:], lwt[:], ALU.subtract))
                    else:
                        av = acc[:].rearrange("p (c s) -> p c s", s=CHUNK)
                        line("tot1", nc.vector.tensor_copy(tot[:], av[:, :, CHUNK - 1]))
                        line("exc1", nc.vector.tensor_tensor(exc[:].rearrange("p (c s) -> p c s", s=CHUNK),
                                                             tot[:].unsqueeze(2).to_broadcast([P, NCH, CHUNK]), av,
                                                             ALU.subtract))
                        line("inc1", nc.vector.tensor_tensor(inc[:], exc[:], lwt[:], ALU.add))
                    dve.wait_ge(acts, A0.n + A(f"sa{d}", c))
                    line(f"m{d}", nc.vector.tensor_scalar(tmp[0][:], rate[:], col(5), col(7), ALU.mult, ALU.add))
                    line(f"kd{d}", mul(kdir[d][:], tmp[0][:], ky[:]))
                    dve.wait_ge(res_stored, c * 32 + d * 16)
                    dve.wait_ge(acts, A0.n + A(f"ex{d}", c))
                    line(f"a{d}", nc.vector.scalar_tensor_tensor(out=res[:, 0, :], in0=exc[:], scalar=-1.0,
                                                                 in1=kk[:], op0=ALU.mult, op1=ALU.mult))
                    dve.wait_ge(acts, A0.n + A(f"en{d}", c))
                    line(f"r{d}", mul(res[:, 1, :], r[:], tmp[1][:]))
                    line(f"bb{d}", mul(tmp[0][:], kk[:], rate[:]))
                    line(f"b{d}", mul(res[:, 2, :], tmp[0][:], tmp[2][:]))
                    line(f"k{d}", mul(res[:, 3, :], kdir[d][:], tmp[2][:]))
                line("kb", nc.vector.tensor_tensor(tmp[0][:], kdir[0][:], kdir[1][:], ALU.add))
                line("q0", mul(tmp[0][:], tmp[0][:], r[:]))
                line("q1", nc.vector.tensor_scalar(tmp[0][:], tmp[0][:], col(6), 0.5, ALU.mult, ALU.mult))
                dve.wait_ge(pes, M("bonus", c))
                line("bv", mul(tmp[2][:], psC[:], v[:]))

        @block.scalar
        def _(act):
            line = Line(act, acts, A0)
            act.wait_ge(dves, V0("omka"))
            line("tanh", nc.scalar.activation(low[0][:, 1:T + 1], low[0][:, 1:T + 1], ACT.Tanh))
            line("sig", nc.scalar.activation(low[2][:, 1:T + 1], low[2][:, 1:T + 1], ACT.Sigmoid))
            with act.Fori(0, RW_TILES) as c:
                act.wait_ge(edge, 2)
                act.wait_ge(pes, M.n * c)
                for d in range(2):
                    half = slice(d * LORA, (d + 1) * LORA)
                    act.dma_start(lw_w[d][half, :], w2[d][:, bass.ds(c * P, P)]).then_inc(lora_loaded, 16)
                    act.dma_start(lw_w[2 + d][half, :], a2[d][:, bass.ds(c * P, P)]).then_inc(lora_loaded, 16)
                line = Line(act, acts, A, c, A0.n)
                vdone = lambda name: V0.n + V(name, c)
                col = lambda j: parv[:, j, bass.ds(c, 1)]
                act.wait_ge(dves, vdone("kkr"))
                line("sq", nc.scalar.activation(tmp[2][:], tmp[1][:], ACT.Square))
                act.wait_ge(pes, M("norm", c))
                line("root", nc.scalar.activation(tmp[0][:], psC[:], ACT.Sqrt, bias=k.eps[:, 1:2]))
                for d in range(2):
                    act.wait_ge(pes, M(f"w{d}", c))
                    if d == 1:
                        act.wait_ge(dves, vdone("k0"))
                    line(f"sw{d}", nc.scalar.activation(lwt[:], psA[:], ACT.Sigmoid, bias=col(d)))
                    act.wait_ge(pes, M(f"a{d}", c))
                    line(f"sa{d}", nc.scalar.activation(rate[:], psB[:], ACT.Sigmoid, bias=col(2 + d)))
                    act.wait_ge(dves, vdone(f"m{d}"))
                    line(f"ex{d}", nc.scalar.activation(exc[:], exc[:], ACT.Exp))
                    line(f"in{d}", nc.scalar.activation(tmp[1][:], inc[:], ACT.Exp))
                    line(f"en{d}", nc.scalar.activation(tmp[2][:], inc[:], ACT.Exp, scale=-1.0))
                    act.wait_ge(stored, c * 32 + d * 16)
                    end = CHUNK - 1 if d == 0 else 0
                    line(f"dc{d}", nc.scalar.activation(
                        dec[:], inc[:].rearrange("p (c s) -> p c s", s=CHUNK)[:, :, end], ACT.Exp))

        @block.tensor
        def _(pe):
            def both(ps, lhsT, rhs):
                for h in range(2):
                    last = nc.tensor.matmul(ps[:, h * HALF:(h + 1) * HALF], lhsT, rhs[:, h * HALF:(h + 1) * HALF],
                                            start=True, stop=True)
                return last

            with pe.Fori(0, RW_TILES) as c:
                pe.wait_ge(acts, A0.n + A("sq", c))
                both(psC, k.head_ones[:], tmp[2][:]).then_inc(pes, 1)
                pe.wait_ge(lora_loaded, c * 64 + 64)
                for d in range(2):
                    if d == 1:
                        pe.wait_ge(acts, A0.n + A("sa0", c))
                    both(psA, lw_w[d][:], low[0][:, 1:T + 1]).then_inc(pes, 1)
                    both(psB, lw_w[2 + d][:], low[1][:, 1:T + 1]).then_inc(pes, 1)
                pe.wait_ge(dves, V0.n + V("q1", c))
                both(psC, k.head_ones[:], tmp[0][:]).then_inc(pes, 1)


def rwkv_scan(nc, k, ops, vals, end_decay, y, yb=None):
    PAIRS = T // P
    with ExitStack() as ctx:
        sb = lambda name, shape, dt=F32: ctx.enter_context(nc.sbuf_tensor(name, shape, dt))
        sem = lambda name: ctx.enter_context(nc.semaphore(name))
        dirs, slots = range(2), range(2)
        opt = [[sb(f"opt{s}{d}", [P, 4, P]) for d in dirs] for s in slots]
        byhead = [[sb(f"byhead{s}{d}", [P, 4, P]) for d in dirs] for s in slots]
        vc = [[sb(f"vc{s}{d}", [P, P]) for d in dirs] for s in slots]
        ended = [[sb(f"ended{s}{d}", [P, 2]) for d in dirs] for s in slots]
        yo = [sb(f"yo{s}", [P, 2, P]) for s in slots]
        vt = sb("vt", [P, 2, P])
        bk = sb("bk", [P, 2, 2, 2, P])
        xa = sb("xa", [P, 2, 2, 2, HEAD])
        kj = sb("kj", [P, 2, 4, P])
        bj = sb("bj", [P, 2, 4, P])
        U = lambda name: sb(name, [P, 4, P])
        E0, X0, X1, X2, X3, X4, X5 = (U(f"X_{n}") for n in "e012345")
        D0, N1, N2, D1, E1, D2, E2, D3, Z1, Z2, T3, T4 = (U(f"N_{n}") for n in range(12))
        ua = sb("ua", [P, 2, 2, 2, HEAD])
        ya = sb("ya", [P, 2, 2, 2, HEAD])
        mt = sb("mt", [P, 2, 2, P])
        rt = [[sb(f"rt{d}{c}", [P, P]) for c in range(2)] for d in dirs]
        st = [[sb(f"st{d}{n}", [P, P]) for n in range(2)] for d in dirs]
        pb = [ctx.enter_context(nc.psum_tensor(f"pb{n}", [P, HALF], F32)) for n in range(8)]
        loaded = [sem(f"unit_loaded{s}") for s in slots]
        y_stored = [sem(f"y_stored{s}") for s in slots]
        yb_zeroed = sem("yb_zeroed")
        zeroed, cleared = sem("zeroed"), sem("cleared")
        acts, dves, pes = sem("s_acts"), sem("s_dves"), sem("s_pes")
        A = Steps("ta0 tv0 b00 b01 ta1 tv1 b10 b11 d1 d2 e2 d3 t3 t4 xv ua0 ua1 ya0 ya1")
        V = Steps("kj0 kj1 bj0 bj1 e0 x0 d0 n1 n2 e1 x1 x2 x3 z1 x4 z2 x5 mt rt00 rt01 rt10 rt11 "
                  "mid0 mid1 end0 end1 y0 y1")
        M = Steps("tm0 tm1 kj0 kj1 bj0 bj1 dt d1 e1 d2 e2 x1 d3 x2 x3 z1 t3 x4 z2 t4 x5 xv ua mt yr rt "
                  "mid0 mid1 end0 end1 y0 y1")
        by_unit = lambda ps, d: ps[:, d * 2 * P:(d + 1) * 2 * P].rearrange("p (h k e) -> p h k e", h=2, k=2)
        quad = lambda ps: ps[:].rearrange("p (u n) -> p u n", u=4)
        four = lambda m: m.unsqueeze(1).to_broadcast([P, 4, P])
        block = ctx.enter_context(nc.Block())

        def rounds(eng, body):
            with eng.Fori(0, RW_TILES) as c:
                with eng.Fori(0, PAIRS // 2) as j:
                    for s in slots:
                        body(s, c * PAIRS + j * 2 + s)

        @block.sync
        def _(sp):
            sp.wait_ge(zeroed, 1)
            with sp.Fori(0, RW_TILES) as c:
                with sp.Fori(0, PAIRS // 2) as j:
                    for s in slots:
                        chan = sp.snap(c * P)
                        t0 = (sp.snap(j * (2 * P) + s * P), sp.snap(j * (-2 * P) + (PAIRS - 1 - s) * P))
                        ch0 = (sp.snap(j * 4 + s * 2), sp.snap(j * -4 + (PAIRS - 1 - s) * 2))
                        sp.wait_ge(y_stored[s], (c * (PAIRS // 2) + j) * 32)
                        for d in dirs:
                            tok = bass.ds(t0[d], P)
                            src = row(ops[d], chan, P)[:, :, tok]
                            sp.dma_start(opt[s][d][:], src).then_inc(loaded[s], 16)
                            for h in range(2):
                                rows = slice(h * HEAD, (h + 1) * HEAD)
                                sp.dma_start(byhead[s][d][rows, 2 * h:2 * h + 2, :],
                                             row(ops[d, h * HEAD:], chan, HEAD)[:, 0:2, tok]).then_inc(loaded[s], 16)
                            sp.dma_start(vc[s][d][:], row(vals, chan, P)[:, tok]).then_inc(loaded[s], 16)
                            sp.dma_start(ended[s][d][:],
                                         row(end_decay[d], chan, P)[:, bass.ds(ch0[d], 2)]).then_inc(loaded[s], 16)

        @block.gpsimd
        def _(pool):
            for s in slots:
                for d in dirs:
                    pool.memset(byhead[s][d][:], 0.0)
            for d in dirs:
                for c in range(2):
                    last = pool.memset(rt[d][c][:], 0.0)
            last.then_inc(zeroed, 1)
            with pool.Fori(0, RW_TILES) as c:
                with pool.Fori(0, PAIRS // 2) as j:
                    for s in slots:
                        i = c * PAIRS + j * 2 + s
                        pool.wait_ge(dves, V("y1", i))
                        for d in dirs:
                            t0 = j * (2 * P) + s * P if d == 0 else j * (-2 * P) + (PAIRS - 1 - s) * P
                            pool.dma_start(row(y[d], t0, P)[:, bass.ds(c * P, P)], yo[s][:, d, :]).then_inc(y_stored[s], 16)
            for s in slots:
                pool.wait_ge(y_stored[s], 32 * RW_TILES * PAIRS // 2)

        @block.scalar
        def _(act):
            if yb is not None:
                act.dma_start(yb.rearrange("(n p) d -> p n d", p=P),
                              k.zeros[:].unsqueeze(1).to_broadcast([P, ROWS // P, D])).then_inc(yb_zeroed, 16)

            def body(s, i):
                line = Line(act, acts, A, i)
                act.wait_ge(dves, V.n * i)
                for d in dirs:
                    ps = quad(pb[d])
                    act.wait_ge(pes, M(f"tm{d}", i))
                    line(f"ta{d}", nc.scalar.copy(xa[:, d, :, 1, :], ps[:, 0, :].rearrange("p (h e) -> p h e", h=2)))
                    line(f"tv{d}", nc.scalar.copy(vt[:, d, :], ps[:, 3, :]))
                    for c in range(2):
                        line(f"b{d}{c}", nc.scalar.activation(bk[:, d, c, :, :], ps[:, 1:3, :], ACT.Copy,
                                                              scale=k.chunk_col[:, c:c + 1]))
                act.wait_ge(pes, M("d1", i))
                line("d1", nc.scalar.copy(D1[:], quad(pb[7])))
                act.wait_ge(pes, M("d2", i))
                line("d2", nc.scalar.copy(D2[:], quad(pb[1])))
                act.wait_ge(pes, M("e2", i))
                line("e2", nc.scalar.copy(E2[:], quad(pb[2])))
                act.wait_ge(pes, M("d3", i))
                line("d3", nc.scalar.copy(D3[:], quad(pb[4])))
                act.wait_ge(pes, M("t3", i))
                line("t3", nc.scalar.copy(T3[:], quad(pb[0])))
                act.wait_ge(pes, M("t4", i))
                line("t4", nc.scalar.copy(T4[:], quad(pb[3])))
                act.wait_ge(pes, M("xv", i))
                line("xv", nc.scalar.copy(xa[:, :, :, 0, :],
                                          pb[5][:, 0:4 * HEAD].rearrange("p (d h e) -> p d h e", d=2, h=2)))
                act.wait_ge(pes, M("ua", i))
                for d in dirs:
                    line(f"ua{d}", nc.scalar.copy(ua[:, d, :, :, :].rearrange("p k h e -> p h k e"),
                                                  by_unit(pb[6], d)))
                act.wait_ge(pes, M("yr", i))
                for d in dirs:
                    line(f"ya{d}", nc.scalar.copy(ya[:, d, :, :, :].rearrange("p k h e -> p h k e"),
                                                  by_unit(pb[0], d)))

            rounds(act, body)
            if yb is not None:
                act.wait_ge(yb_zeroed, 16)

        @block.vector
        def _(dve):
            def masked(out, ps, mask):
                return nc.vector.tensor_tensor(out, ps, mask, ALU.mult)

            def added(out, ps, x):
                return nc.vector.tensor_tensor(out[:], quad(ps), x[:], ALU.add)

            def body(s, i):
                line = Line(dve, dves, V, i)
                for n, t in enumerate((kj, bj)):
                    for d in dirs:
                        nm = f"{'kb'[n]}j{d}"
                        dve.wait_ge(pes, M(nm, i))
                        line(nm, masked(t[:, d, :, :], quad(pb[2 + 2 * n + d]), k.causal[:, d, :, :]))
                near = lambda n: four(k.near[:, n, :])
                e_all = bj[:].rearrange("p d (h k) i -> p d h k i", k=2)[:, :, :, 0, :]
                u4 = lambda t: t[:].rearrange("p (d h) i -> p d h i", d=2)
                line("e0", masked(u4(E0), e_all, k.near[:, 0, :].unsqueeze(1).unsqueeze(1).to_broadcast([P, 2, 2, P])))
                line("x0", nc.vector.tensor_tensor(X0[:], E0[:], four(k.ident[:]), ALU.add))
                dve.wait_ge(pes, M("dt", i))
                line("d0", masked(D0[:], quad(pb[6]), near(0)))
                line("n1", masked(N1[:], quad(pb[6]), near(1)))
                line("n2", masked(N2[:], quad(pb[6]), near(2)))
                dve.wait_ge(pes, M("e1", i))
                line("e1", nc.vector.tensor_copy(E1[:], quad(pb[0])))
                for nm, out, ps, x in (("x1", X1, pb[3], X0), ("x2", X2, pb[5], X1), ("x3", X3, pb[6], X2)):
                    dve.wait_ge(pes, M(nm, i))
                    line(nm, added(out, ps, x))
                dve.wait_ge(pes, M("z1", i))
                line("z1", nc.vector.tensor_copy(Z1[:], quad(pb[7])))
                dve.wait_ge(pes, M("x4", i))
                line("x4", added(X4, pb[1], X3))
                dve.wait_ge(pes, M("z2", i))
                line("z2", nc.vector.tensor_copy(Z2[:], quad(pb[2])))
                dve.wait_ge(pes, M("x5", i))
                line("x5", added(X5, pb[4], X4))
                dve.wait_ge(pes, M("mt", i))
                line("mt", masked(mt[:].rearrange("p d c n -> p (d c) n"), quad(pb[7]), four(k.head_ones[:])))
                dve.wait_ge(pes, M("rt", i))
                for d in dirs:
                    for c in range(2):
                        cols = slice(c * CHUNK, (c + 1) * CHUNK)
                        line(f"rt{d}{c}", nc.vector.tensor_tensor(
                            rt[d][c][:, cols], pb[1][:, d * P + c * CHUNK:d * P + (c + 1) * CHUNK],
                            opt[s][d][:, 1, cols], ALU.add))
                for n, nm in enumerate(("mid", "end")):
                    for d in dirs:
                        c = n if d == 0 else 1 - n
                        dve.wait_ge(pes, M("mid1", i) if n == 0 else M("y1", i))
                        line(f"{nm}{d}", nc.vector.scalar_tensor_tensor(
                            out=st[d][1 - n][:], in0=pb[2 if n == 0 else 5][:, d * P:(d + 1) * P],
                            scalar=ended[s][d][:, c:c + 1], in1=k.head_ones[:], op0=ALU.mult, op1=ALU.mult))
                dve.wait_ge(y_stored[s], stores(s, i))
                dve.wait_ge(acts, A("ya1", i))
                for d in dirs:
                    dve.wait_ge(pes, M(f"y{d}", i))
                    line(f"y{d}", nc.vector.tensor_tensor(
                        yo[s][:, d, :], pb[3 + d][:, 0:P],
                        ya[:, d, 0, :, :].rearrange("p h e -> p (h e)"), ALU.add))

            with dve.Fori(0, RW_TILES) as c:
                dve.wait_ge(pes, c * PAIRS * M.n)
                dve.wait_ge(dves, c * PAIRS * V.n)
                for d in dirs:
                    last = nc.vector.memset(st[d][0][:], 0.0)
                    last.then_inc(cleared, 1)
                with dve.Fori(0, PAIRS // 2) as j:
                    for s in slots:
                        stores = lambda s, i: (c * (PAIRS // 2) + j) * 32
                        body(s, c * PAIRS + j * 2 + s)

        @block.tensor
        def _(pe):
            mm = lambda out, lhsT, rhs, start=True, stop=True: nc.tensor.matmul(
                out, lhsT, rhs, start=start, stop=stop)

            def body(s, i, first, cleared_by):
                pe.wait_ge(loaded[s], first)
                pe.wait_ge(acts, A.n * i)
                pe.wait_ge(dves, V.n * i)
                for d in dirs:
                    for n, src in enumerate((opt[s][d][:, 0, :], opt[s][d][:, 2, :], opt[s][d][:, 3, :], vc[s][d][:])):
                        last = nc.tensor.transpose(pb[d][:, n * P:(n + 1) * P], src, k.ident[:])
                    last.then_inc(pes, 1)
                for n in range(2):
                    for d in dirs:
                        mm(pb[2 + 2 * n + d][:], opt[s][d][:, 3 - n, :],
                           byhead[s][d][:].rearrange("p m i -> p (m i)")).then_inc(pes, 1)

                def each(ps, lhsT, rhs, width=P):
                    for u in range(4):
                        last = mm(pb[ps][:, u * width:(u + 1) * width], lhsT(u), rhs(u))
                    last.then_inc(pes, 1)

                def turned(ps, src):
                    for u in range(4):
                        last = nc.tensor.transpose(pb[ps][:, u * P:(u + 1) * P], src(u), k.ident[:])
                    last.then_inc(pes, 1)

                of = lambda t: (lambda u: t[:, u, :])
                pe.wait_ge(dves, V("bj1", i))
                turned(6, lambda u: bj[:, u // 2, 2 * (u % 2), :])
                pe.wait_ge(dves, V("d0", i))
                each(7, of(E0), of(D0))
                pe.wait_ge(acts, A("b11", i))
                each(0, of(D0), of(E0))
                pe.wait_ge(dves, V("e1", i))
                pe.wait_ge(acts, A("d1", i))
                each(1, of(E1), of(D1))
                each(2, of(D1), of(E1))
                each(3, of(D1), of(X0))
                pe.wait_ge(acts, A("e2", i))
                each(4, of(E2), of(D2))
                pe.wait_ge(dves, V("x1", i))
                each(5, of(D2), of(X1))
                pe.wait_ge(acts, A("d3", i))
                pe.wait_ge(dves, V("x2", i))
                each(6, of(D3), of(X2))
                pe.wait_ge(dves, V("x3", i))
                each(7, of(N1), of(X3))
                turned(0, of(X3))
                pe.wait_ge(acts, A("t3", i))
                pe.wait_ge(dves, V("z1", i))
                each(1, of(T3), of(Z1))
                pe.wait_ge(dves, V("x4", i))
                each(2, of(N2), of(X4))
                turned(3, of(X4))
                pe.wait_ge(acts, A("t4", i))
                pe.wait_ge(dves, V("z2", i))
                each(4, of(T4), of(Z2))
                each(5, lambda u: kj[:, u // 2, 2 * (u % 2), :],
                     lambda u: vt[:, u // 2, (u % 2) * HEAD:(u % 2 + 1) * HEAD], HEAD)
                pe.wait_ge(dves, V("x5", i))
                pe.wait_ge(acts, A("xv", i))
                each(6, of(X5), lambda u: xa[:, u // 2, u % 2, :, :].rearrange("p k e -> p (k e)"))
                pe.wait_ge(acts, A("ua1", i))
                flat = lambda t: t.rearrange("p h e -> p (h e)")
                for d in dirs:
                    last = mm(pb[7][:, d * 2 * P:(d + 1) * 2 * P], flat(ua[:, d, 1, :, :]), bk[:, d, :, 0, :])
                last.then_inc(pes, 1)
                for u in range(4):
                    d, h = u // 2, u % 2
                    mm(pb[0][:, u * P:(u + 1) * P], bj[:, d, 2 * h + 1, :], ua[:, d, :, h, :], True, False)
                    last = mm(pb[0][:, u * P:u * P + HEAD], kj[:, d, 2 * h + 1, :],
                              vt[:, d, h * HEAD:(h + 1) * HEAD], False, True)
                last.then_inc(pes, 1)
                pe.wait_ge(acts, A("ya1", i))
                for d in dirs:
                    last = nc.tensor.transpose(pb[1][:, d * P:(d + 1) * P], flat(ya[:, d, 1, :, :]), k.ident[:])
                last.then_inc(pes, 1)

                def state(ps, n):
                    for d in dirs:
                        c = n if d == 0 else 1 - n
                        out = pb[ps][:, d * P:(d + 1) * P]
                        mm(out, bk[:, d, c, 0, :], flat(ua[:, d, 0, :, :]), True, False)
                        mm(out, bk[:, d, c, 1, :], vt[:, d, :], False, False)
                        mm(out, k.ident[:], st[d][n][:], False, False)
                        mm(out, mt[:, d, c, :], st[d][n][:], False, True).then_inc(pes, 1)

                pe.wait_ge(dves, V("mt", i))
                pe.wait_ge(cleared, cleared_by)
                state(2, 0)
                pe.wait_ge(dves, V("mid1", i))
                state(5, 1)
                for d in dirs:
                    mm(pb[3 + d][:, 0:P], rt[d][d][:], st[d][0][:], True, False)
                    mm(pb[3 + d][:, 0:P], rt[d][1 - d][:], st[d][1][:], False, True).then_inc(pes, 1)

            with pe.Fori(0, RW_TILES) as c:
                with pe.Fori(0, PAIRS // 2) as j:
                    for s in slots:
                        body(s, c * PAIRS + j * 2 + s, (c * (PAIRS // 2) + j) * 160 + 160, c * 2 + 2)


E_DA = C_DA // DA_HEADS
QK = E_DA // 2


def differential_attention(nc, k, zT, q_gain, k_gain, lq1, lk1, lq2, lk2, sub_gain, oT):
    QT = NT
    with ExitStack() as ctx:
        sb = lambda name, shape, dt=F32: ctx.enter_context(nc.sbuf_tensor(name, shape, dt))
        sem = lambda name: ctx.enter_context(nc.semaphore(name))
        maps = range(2)
        zq, zk, zv = (sb(f"a{n}", [P, T]) for n in ("zq", "zk", "zv"))
        sq = sb("asq", [P, T])
        inv = sb("ainv", [P, T])
        qm = [sb(f"qm{m}", [P, T]) for m in maps]
        kn = sb("kn", [P, T])
        vt = sb("avt", [P, NT, E_DA])
        gains = sb("gains", [P, 3])
        lam_in = sb("lam_in", [P, 4, QK])
        lam = sb("lam", [P, 8])
        far = sb("far", [P, 2 * T - P], I32)
        dist = sb("dist", [P, 2 * T - P])
        slope = sb("slope", [P, 2 * T - P])
        sc = [sb(f"sc{m}", [P, T]) for m in maps]
        pr = [sb(f"pr{m}", [P, T]) for m in maps]
        at = sb("at", [P, T])
        aT = sb("aT", [P, NT, P])
        mx = sb("amx", [P, 2])
        nmx = sb("anmx", [P, 2])
        sm = sb("asm", [P, 2])
        rs = sb("ars", [P, 4])
        carrier = sb("carrier", [P, 1])
        o_sb = sb("o_sb", [P, E_DA])
        o_sq = sb("o_sq", [P, E_DA])
        oc = sb("oc", [P, T])
        ps = [ctx.enter_context(nc.psum_tensor(f"sp{m}", [P, T], F32)) for m in maps]
        tp = ctx.enter_context(nc.psum_tensor("atp", [P, T], F32))
        op = ctx.enter_context(nc.psum_tensor("aop", [P, HALF], F32))
        ot = ctx.enter_context(nc.psum_tensor("aot", [P, HALF], F32))
        par, zl, made = sem("apar"), sem("azl"), sem("amade")
        acts, dves, pes, kept = sem("a_acts"), sem("a_dves"), sem("a_pes"), sem("a_kept")
        A0 = Steps("e0 e1 gq")
        V0 = Steps("p0 p1 fcopy fneg dist lamd lamn")
        A = Steps("slope sqq rq sqk rk v0 v1 " + " ".join(
            f"ex0_{t} ex1_{t} at0_{t} at1_{t} osq_{t} ort_{t} oT_{t}" for t in range(QT)))
        V = Steps("iq q0 q1 ik kn " + " ".join(
            f"s0_{t} n0_{t} s1_{t} n1_{t} rs_{t} c1_{t} a0_{t} a1_{t} oc_{t} orc_{t} on_{t}" for t in range(QT)))
        M = Steps("nq nk v " + " ".join(f"s0_{t} s1_{t} at_{t} o_{t} oT_{t}" for t in range(QT)))
        block = ctx.enter_context(nc.Block())

        @block.sync
        def _(sp):
            with nc.allow_non_contiguous_dma(reason="gains as columns"):
                for m in maps:
                    rows = slice(m * QK, (m + 1) * QK)
                    sp.dma_start(gains[rows, 0:1], q_gain.rearrange("(p o) -> p o", o=1)).then_inc(par, 16)
                    sp.dma_start(gains[rows, 1:2], k_gain.rearrange("(p o) -> p o", o=1)).then_inc(par, 16)
                sp.dma_start(gains[:, 2:3], sub_gain.rearrange("(p o) -> p o", o=1)).then_inc(par, 16)
            for i, v in enumerate((lq1, lk1, lq2, lk2)):
                sp.dma_start(lam_in[:, i, :], v.rearrange("(o n) -> o n", o=1).to_broadcast([P, QK])).then_inc(par, 16)
            with sp.Fori(0, DA_HEADS) as h:
                first = sp.snap(h * P)
                sp.wait_ge(kept, h * 16)
                for i, t in enumerate((zq, zk, zv)):
                    base = RW_COLS + i * C_DA
                    sp.dma_start(t[:], row(zT[base:base + C_DA], first, P)).then_inc(zl, 16)

        @block.gpsimd
        def _(pool):
            pool.memset(qm[0][:], 0.0)
            pool.memset(qm[1][:], 0.0)
            pool.iota(far[:], [[1, 2 * T - P]], base=-(T - P), channel_multiplier=-1).then_inc(made, 1)
            with pool.Fori(0, DA_HEADS) as h:
                pool.wait_ge(acts, A0.n + A(f"oT_{QT - 1}", h))
                pool.dma_start(row(oT, h * P + C_RW, P), oc[:]).then_inc(kept, 16)
            pool.wait_ge(kept, 16 * DA_HEADS)

        @block.vector
        def _(dve):
            line = Line(dve, dves, V0)
            dve.wait_ge(par, 16 * 9)
            for m in maps:
                line(f"p{m}", nc.vector.tensor_tensor_reduce(
                    lam_in[:, 2 * m, :], lam_in[:, 2 * m, :], lam_in[:, 2 * m + 1, :], 1.0, 0.0,
                    ALU.mult, ALU.add, lam[:, m:m + 1]))
            dve.wait_ge(made, 1)
            line("fcopy", nc.vector.tensor_copy(dist[:], far[:]))
            line("fneg", nc.vector.tensor_scalar(slope[:], dist[:], -1.0, None, ALU.mult))
            line("dist", nc.vector.tensor_tensor(dist[:], dist[:], slope[:], ALU.min))
            dve.wait_ge(acts, A0("e1"))
            line("lamd", nc.vector.tensor_tensor(lam[:, 4:5], lam[:, 3:4], lam[:, 2:3], ALU.subtract))
            line("lamn", nc.vector.tensor_scalar(lam[:, 5:6], lam[:, 4:5], -LAMBDA_INIT, None, ALU.add))
            with dve.Fori(0, DA_HEADS) as h:
                line = Line(dve, dves, V, h, V0.n)
                dve.wait_ge(acts, A0.n + A("rq", h))
                line("iq", nc.vector.reciprocal(inv[:], inv[:]))
                for m in maps:
                    rows = slice(m * QK, (m + 1) * QK)
                    line(f"q{m}", nc.vector.scalar_tensor_tensor(
                        out=qm[m][rows, :], in0=zq[rows, :], scalar=gains[rows, 0:1], in1=inv[rows, :],
                        op0=ALU.mult, op1=ALU.mult))
                dve.wait_ge(acts, A0.n + A("rk", h))
                line("ik", nc.vector.reciprocal(sq[:], sq[:]))
                line("kn", nc.vector.scalar_tensor_tensor(out=kn[:], in0=zk[:], scalar=gains[:, 1:2], in1=sq[:],
                                                          op0=ALU.mult, op1=ALU.mult))
                dve.wait_ge(acts, A0.n + A("v1", h))
                for t in range(QT):
                    at0 = (T - P) - t * P
                    for m in maps:
                        dve.wait_ge(pes, M(f"s{m}_{t}", h))
                        nc.vector.memset(carrier[:], 0.0)
                        line(f"s{m}_{t}", nc.vector.tensor_tensor_reduce(
                            sc[m][:], ps[m][:], dist[:, at0:at0 + T], 1.0, -3.0e38, ALU.add, ALU.max,
                            mx[:, m:m + 1]))
                        line(f"n{m}_{t}", nc.vector.tensor_scalar(nmx[:, m:m + 1], mx[:, m:m + 1], -1.0, None,
                                                                  ALU.mult))
                    dve.wait_ge(acts, A0.n + A(f"ex1_{t}", h))
                    line(f"rs_{t}", nc.vector.reciprocal(rs[:, 0:2], sm[:]))
                    line(f"c1_{t}", nc.vector.tensor_scalar(rs[:, 2:3], rs[:, 1:2], lam[:, 5:6], None, ALU.mult))
                    line(f"a0_{t}", nc.vector.tensor_scalar(pr[0][:], pr[0][:], rs[:, 0:1], None, ALU.mult))
                    line(f"a1_{t}", nc.vector.scalar_tensor_tensor(out=at[:], in0=pr[1][:], scalar=rs[:, 2:3],
                                                                   in1=pr[0][:], op0=ALU.mult, op1=ALU.add))
                    dve.wait_ge(pes, M(f"o_{t}", h))
                    line(f"oc_{t}", nc.vector.tensor_copy(o_sb[:], op[:, 0:E_DA]))
                    dve.wait_ge(acts, A0.n + A(f"ort_{t}", h))
                    line(f"orc_{t}", nc.vector.reciprocal(rs[:, 3:4], rs[:, 3:4]))
                    line(f"on_{t}", nc.vector.tensor_scalar(o_sb[:], o_sb[:], rs[:, 3:4], 1.0 - LAMBDA_INIT,
                                                            ALU.mult, ALU.mult))

        @block.scalar
        def _(act):
            line = Line(act, acts, A0)
            act.wait_ge(dves, V0("p1"))
            for m in maps:
                line(f"e{m}", nc.scalar.activation(lam[:, 2 + m:3 + m], lam[:, m:m + 1], ACT.Exp))
            line("gq", nc.scalar.mul(gains[:, 0:1], gains[:, 0:1], QK ** -0.5))
            with act.Fori(0, DA_HEADS) as h:
                line = Line(act, acts, A, h, A0.n)
                vdone = lambda name: V0.n + V(name, h)
                act.wait_ge(dves, V0.n + h * V.n)
                line("slope", nc.scalar.mul(dist[:], dist[:], 0.25))
                act.wait_ge(zl, h * 48 + 48)
                line("sqq", nc.scalar.activation(sq[:], zq[:], ACT.Square))
                act.wait_ge(pes, M("nq", h))
                line("rq", nc.scalar.activation(inv[:], ps[0][:], ACT.Sqrt, bias=k.eps[:, 0:1], scale=1.0 / QK))
                line("sqk", nc.scalar.activation(at[:], zk[:], ACT.Square))
                act.wait_ge(pes, M("nk", h))
                line("rk", nc.scalar.activation(sq[:], ps[1][:], ACT.Sqrt, bias=k.eps[:, 0:1], scale=1.0 / QK))
                act.wait_ge(pes, M("v", h))
                for n in range(2):
                    line(f"v{n}", nc.scalar.copy(vt[:].rearrange("p n e -> p (n e)")[:, n * HALF:(n + 1) * HALF],
                                                 tp[:, n * HALF:(n + 1) * HALF]))
                for t in range(QT):
                    for m in maps:
                        act.wait_ge(dves, vdone(f"n{m}_{t}"))
                        line(f"ex{m}_{t}", nc.scalar.activation(pr[m][:], sc[m][:], ACT.Exp, bias=nmx[:, m:m + 1],
                                                                accum_out=sm[:, m:m + 1]))
                    act.wait_ge(pes, M(f"at_{t}", h))
                    for n in range(2):
                        line(f"at{n}_{t}", nc.scalar.copy(
                            aT[:].rearrange("p n e -> p (n e)")[:, n * HALF:(n + 1) * HALF],
                            tp[:, n * HALF:(n + 1) * HALF]))
                    act.wait_ge(dves, vdone(f"oc_{t}"))
                    line(f"osq_{t}", nc.scalar.activation(o_sq[:], o_sb[:], ACT.Square, accum_out=rs[:, 3:4]))
                    line(f"ort_{t}", nc.scalar.activation(rs[:, 3:4], rs[:, 3:4], ACT.Sqrt, bias=k.eps[:, 0:1],
                                                          scale=1.0 / E_DA))
                    act.wait_ge(pes, M(f"oT_{t}", h))
                    act.wait_ge(kept, h * 16)
                    line(f"oT_{t}", nc.scalar.mul(oc[:, t * P:(t + 1) * P], ot[:, 0:P], gains[:, 2:3]))

        @block.tensor
        def _(pe):
            with pe.Fori(0, DA_HEADS) as h:
                adone = lambda name: A0.n + A(name, h)
                vdone = lambda name: V0.n + V(name, h)

                def both(out, lhsT, rhs):
                    for n in range(2):
                        last = nc.tensor.matmul(out[:, n * HALF:(n + 1) * HALF], lhsT,
                                                rhs[:, n * HALF:(n + 1) * HALF], start=True, stop=True)
                    last.then_inc(pes, 1)

                pe.wait_ge(acts, adone("sqq"))
                both(ps[0], k.head_ones[:], sq)
                pe.wait_ge(acts, adone("sqk"))
                both(ps[1], k.head_ones[:], at)
                for n in range(NT):
                    last = nc.tensor.transpose(tp[:, n * P:(n + 1) * P], zv[:, n * P:(n + 1) * P], k.ident[:])
                last.then_inc(pes, 1)
                pe.wait_ge(dves, vdone("kn"))
                for t in range(QT):
                    for m in maps:
                        if t:
                            pe.wait_ge(dves, vdone(f"s{m}_{t - 1}"))
                        both(ps[m], qm[m][:, t * P:(t + 1) * P], kn)
                    pe.wait_ge(dves, vdone(f"a1_{t}"))
                    for n in range(NT):
                        last = nc.tensor.transpose(tp[:, n * P:(n + 1) * P], at[:, n * P:(n + 1) * P], k.ident[:])
                    last.then_inc(pes, 1)
                    pe.wait_ge(acts, adone(f"at1_{t}"))
                    for n in range(NT):
                        last = nc.tensor.matmul(op[:, 0:E_DA], aT[:, n, :], vt[:, n, :],
                                                start=(n == 0), stop=(n == NT - 1))
                    last.then_inc(pes, 1)
                    pe.wait_ge(dves, vdone(f"on_{t}"))
                    nc.tensor.transpose(ot[:, 0:P], o_sb[:], k.ident[:]).then_inc(pes, 1)


def finish_rwkv(nc, k, y, bonus, gate_in, g2, ln_g, ln_b, oT):
    with ExitStack() as ctx:
        sb = lambda name, shape, dt=F32: ctx.enter_context(nc.sbuf_tensor(name, shape, dt))
        sem = lambda name: ctx.enter_context(nc.semaphore(name))
        slots = range(2)
        yf = [sb(f"yf{s}", [P, NT, P]) for s in slots]
        yb = [sb(f"yb{s}", [P, NT, P]) for s in slots]
        yc = sb("ycent", [P, NT, P])
        bv = [sb(f"bvt{s}", [P, T]) for s in slots]
        g2s = sb("g2s", [P, C_RW])
        gin = sb("gins", [P, T])
        gains = sb("lngains", [P, 2, RW_TILES])
        stat = sb("gnstat", [P, 3, NT * 2])
        oc = [sb(f"orw{s}", [P, T]) for s in slots]
        tp = [ctx.enter_context(nc.psum_tensor(f"gtp{s}", [P, T], F32)) for s in slots]
        gp = [ctx.enter_context(nc.psum_tensor(f"ggp{s}", [P, T], F32)) for s in slots]
        once, y_loaded = sem("once"), [sem(f"y_in{s}") for s in slots]
        o_stored = [sem(f"o_out{s}") for s in slots]
        acts, dves, pes = sem("g_acts"), sem("g_dves"), sem("g_pes")
        A = Steps("root0 root1")
        V = Steps(" ".join(f"sum{s} mean{s} meand{s} cent{s} sq{s} var{s} inv{s} norm{s} aff{s} bon{s} gate{s}" for s in slots))
        M = Steps("gate0 turn0 gate1 turn1")
        LOOPS = RW_TILES // 2
        block = ctx.enter_context(nc.Block())

        @block.sync
        def _(sp):
            with nc.allow_non_contiguous_dma(reason="gains as columns"):
                sp.dma_start(gains[:, 0, :], ln_g.rearrange("(n p) -> p n", p=P)).then_inc(once, 16)
                sp.dma_start(gains[:, 1, :], ln_b.rearrange("(n p) -> p n", p=P)).then_inc(once, 16)
            sp.dma_start(g2s[:], g2).then_inc(once, 16)
            sp.dma_start(gin[:], gate_in).then_inc(once, 16)
            for c in range(RW_TILES):
                s = c % 2
                if c >= 2:
                    sp.wait_ge(dves, V(f"gate{s}", c // 2 - 1))
                chan = slice(c * P, (c + 1) * P)
                for d, t in ((0, yf), (1, yb)):
                    sp.dma_start(t[s][:], y[d][:, chan].rearrange("(n p) c -> p n c", p=P)).then_inc(y_loaded[s], 16)
                sp.dma_start(bv[s][:], bonus[chan, :]).then_inc(y_loaded[s], 16)

        @block.gpsimd
        def _(pool):
            for c in range(RW_TILES):
                s = c % 2
                pool.wait_ge(dves, V(f"gate{s}", c // 2))
                pool.dma_start(oT[c * P:(c + 1) * P, :], oc[s][:]).then_inc(o_stored[s], 16)
            for s in slots:
                pool.wait_ge(o_stored[s], 16 * LOOPS)

        @block.scalar
        def _(act):
            with act.Fori(0, LOOPS) as j:
                line = Line(act, acts, A, j)
                for s in slots:
                    act.wait_ge(dves, V(f"var{s}", j))
                    line(f"root{s}", nc.scalar.activation(stat[:, 2, :], stat[:, 1, :], ACT.Sqrt,
                                                          bias=k.eps[:, 2:3], scale=1.0 / HEAD))

        @block.vector
        def _(dve):
            dve.wait_ge(once, 64)
            with dve.Fori(0, LOOPS) as j:
                line = Line(dve, dves, V, j)
                for s in slots:
                    heads = lambda t: t[:].rearrange("p n (h e) -> p (n h) e", e=HEAD)
                    wide = lambda i: stat[:, i, :].unsqueeze(2).to_broadcast([P, NT * 2, HEAD])
                    col = lambda i: gains[:, i, bass.ds(j * 2 + s, 1)]
                    flat = lambda t: t[:].rearrange("p n c -> p (n c)")
                    dve.wait_ge(y_loaded[s], j * 48 + 48)
                    line(f"sum{s}", nc.vector.tensor_tensor(flat(yf[s]), flat(yf[s]), flat(yb[s]), ALU.add))
                    line(f"mean{s}", nc.vector.tensor_reduce(stat[:, 0, :], heads(yf[s]), AX.X, ALU.add))
                    line(f"meand{s}", nc.vector.tensor_scalar(stat[:, 0, :], stat[:, 0, :], 1.0 / HEAD, None, ALU.mult))
                    line(f"cent{s}", nc.vector.tensor_tensor(heads(yc), heads(yf[s]), wide(0), ALU.subtract))
                    line(f"sq{s}", nc.vector.tensor_tensor(flat(yb[s]), flat(yc), flat(yc), ALU.mult))
                    line(f"var{s}", nc.vector.tensor_reduce(stat[:, 1, :], heads(yb[s]), AX.X, ALU.add))
                    dve.wait_ge(acts, A(f"root{s}", j))
                    line(f"inv{s}", nc.vector.reciprocal(stat[:, 2, :], stat[:, 2, :]))
                    line(f"norm{s}", nc.vector.tensor_tensor(heads(yf[s]), heads(yc), wide(2), ALU.mult))
                    dve.wait_ge(pes, M(f"turn{s}", j))
                    dve.wait_ge(o_stored[s], j * 16)
                    line(f"aff{s}", nc.vector.tensor_scalar(oc[s][:], tp[s][:], col(0), col(1), ALU.mult, ALU.add))
                    line(f"bon{s}", nc.vector.tensor_tensor(oc[s][:], oc[s][:], bv[s][:], ALU.add))
                    line(f"gate{s}", nc.vector.tensor_tensor(oc[s][:], oc[s][:], gp[s][:], ALU.mult))

        @block.tensor
        def _(pe):
            pe.wait_ge(once, 64)
            for c in range(RW_TILES):
                s, j = c % 2, c // 2
                if j:
                    pe.wait_ge(dves, V(f"gate{s}", j - 1))
                for h in range(2):
                    last = nc.tensor.matmul(gp[s][:, h * HALF:(h + 1) * HALF], g2s[:, c * P:(c + 1) * P],
                                            gin[:, h * HALF:(h + 1) * HALF], start=True, stop=True)
                last.then_inc(pes, 1)
                pe.wait_ge(dves, V(f"norm{s}", j))
                for n in range(NT):
                    last = nc.tensor.transpose(tp[s][:, n * P:(n + 1) * P], yf[s][:, n, :], k.ident[:])
                last.then_inc(pes, 1)


def mix_out_and_route(nc, k, x, oT, w_out, ffn_gain, w_router, b_router, h1, m, chosen, gates):
    with ExitStack() as ctx:
        sb = lambda name, shape, dt=F32: ctx.enter_context(nc.sbuf_tensor(name, shape, dt))
        sem = lambda name: ctx.enter_context(nc.semaphore(name))
        slots = range(2)
        wo = sb("wo", [P, ND, D])
        wr = sb("wr", [P, ND, EXPERTS])
        br = sb("br", [P, EXPERTS])
        gb = sb("gb", [P, D])
        expert = sb("expert", [P, EXPERTS], I32)
        expertf = sb("expertf", [P, EXPERTS])
        ot = [sb(f"ot{s}", [P, ND, P]) for s in slots]
        xt = [sb(f"xin{s}", [P, D]) for s in slots]
        ht = [sb(f"ht{s}", [P, D]) for s in slots]
        mt = [sb(f"mtok{s}", [P, D]) for s in slots]
        mT = [sb(f"mT{s}", [P, ND, P]) for s in slots]
        carrier = sb("rcarrier", [P, 1])
        sq = sb("hsq", [P, D])
        st = [sb(f"hst{s}", [P, 2]) for s in slots]
        lg = [sb(f"lg{s}", [P, EXPERTS]) for s in slots]
        top = [sb(f"top{s}", [P, 8]) for s in slots]
        ix = [sb(f"ix{s}", [P, 8], U32) for s in slots]
        ixf = [sb(f"ixf{s}", [P, 8]) for s in slots]
        gt = [sb(f"gt{s}", [P, 4]) for s in slots]
        hp = [ctx.enter_context(nc.psum_tensor(f"hp{s}", [P, D], F32)) for s in slots]
        tp = ctx.enter_context(nc.psum_tensor("mtp", [P, D], F32))
        lp = [ctx.enter_context(nc.psum_tensor(f"lp{s}", [P, HALF], F32)) for s in slots]
        once, made = sem("r_once"), sem("r_made")
        loaded = [sem(f"r_loaded{s}") for s in slots]
        stored = [sem(f"r_stored{s}") for s in slots]
        acts, dves, pes = sem("r_acts"), sem("r_dves"), sem("r_pes")
        V0 = Steps("expertf")
        A = Steps(" ".join(f"sq{s} root{s} mTa{s} mTb{s} exp{s}" for s in slots))
        V = Steps(" ".join(f"h{s} inv{s} m{s} logit{s} max{s} idx{s} idf{s} neg{s} hot0{s} hot1{s} hot2{s} hot3{s} "
                           f"inve{s} gate{s}" for s in slots))
        M = Steps(" ".join(f"h{s} turn{s} logit{s}" for s in slots))
        LOOPS = NT // 2
        block = ctx.enter_context(nc.Block())
        oT_v = oT.rearrange("(n p) t -> p n t", p=P)

        @block.sync
        def _(sp):
            sp.dma_start(wr[:], w_router.rearrange("(n p) e -> p n e", p=P)).then_inc(once, 16)
            sp.dma_start(br[:], b_router.rearrange("(o e) -> o e", o=1).to_broadcast([P, EXPERTS])).then_inc(once, 16)
            sp.dma_start(gb[:], ffn_gain.rearrange("(o e) -> o e", o=1).to_broadcast([P, D])).then_inc(once, 16)
            sp.dma_start(wo[:], w_out.rearrange("(n p) e -> p n e", p=P)).then_inc(once, 16)
            with sp.Fori(0, LOOPS) as j:
                for s in slots:
                    first = sp.snap(j * 2 * P + s * P)
                    sp.wait_ge(stored[s], j * 32)
                    sp.dma_start(ot[s][:], oT_v[:, :, bass.ds(first, P)]).then_inc(loaded[s], 16)
                    sp.dma_start(xt[s][:], row(x, first, P)).then_inc(loaded[s], 16)

        @block.gpsimd
        def _(pool):
            pool.iota(expert[:], [[1, EXPERTS]], base=0, channel_multiplier=0).then_inc(made, 1)
            with pool.Fori(0, LOOPS) as j:
                for s in slots:
                    first = j * 2 * P + s * P
                    pool.wait_ge(dves, V0.n + V(f"m{s}", j))
                    pool.dma_start(row(h1, first, P), ht[s][:]).then_inc(stored[s], 16)
                    pool.dma_start(row(m, first, P), mt[s][:]).then_inc(stored[s], 16)
            for s in slots:
                pool.wait_ge(stored[s], 32 * LOOPS)

        @block.scalar
        def _(act):
            with act.Fori(0, LOOPS) as j:
                line = Line(act, acts, A, j)
                vdone = lambda name: V0.n + V(name, j)
                for s in slots:
                    act.wait_ge(dves, vdone(f"h{s}"))
                    line(f"sq{s}", nc.scalar.activation(sq[:], ht[s][:], ACT.Square, accum_out=st[s][:, 0:1]))
                    line(f"root{s}", nc.scalar.activation(st[s][:, 1:2], st[s][:, 0:1], ACT.Sqrt,
                                                          bias=k.eps[:, 0:1], scale=1.0 / D))
                    act.wait_ge(pes, M(f"turn{s}", j))
                    for n in range(2):
                        line(f"mT{'ab'[n]}{s}", nc.scalar.copy(
                            mT[s][:].rearrange("p n t -> p (n t)")[:, n * HALF:(n + 1) * HALF],
                            tp[:, n * HALF:(n + 1) * HALF]))
                    act.wait_ge(dves, vdone(f"neg{s}"))
                    line(f"exp{s}", nc.scalar.activation(gt[s][:], top[s][:, 0:4], ACT.Exp, bias=ixf[s][:, 7:8],
                                                         accum_out=ixf[s][:, 6:7]))

        @block.vector
        def _(dve):
            line = Line(dve, dves, V0)
            dve.wait_ge(made, 1)
            line("expertf", nc.vector.tensor_copy(expertf[:], expert[:]))
            dve.wait_ge(once, 64)
            with dve.Fori(0, LOOPS) as j:
                line = Line(dve, dves, V, j, V0.n)
                for s in slots:
                    tile = bass.ds(j * 2 + s, 1)
                    dve.wait_ge(pes, M(f"h{s}", j))
                    dve.wait_ge(loaded[s], j * 32 + 32)
                    line(f"h{s}", nc.vector.tensor_tensor(ht[s][:], hp[s][:], xt[s][:], ALU.add))
                    dve.wait_ge(acts, A(f"root{s}", j))
                    line(f"inv{s}", nc.vector.reciprocal(st[s][:, 0:1], st[s][:, 1:2]))
                    line(f"m{s}", nc.vector.scalar_tensor_tensor(out=mt[s][:], in0=ht[s][:], scalar=st[s][:, 0:1],
                                                                 in1=gb[:], op0=ALU.mult, op1=ALU.mult))
                    dve.wait_ge(pes, M(f"logit{s}", j))
                    line(f"logit{s}", nc.vector.tensor_tensor(lg[s][:], lp[s][:, 0:EXPERTS], br[:], ALU.add))
                    nc.vector.memset(carrier[:], 0.0)
                    line(f"max{s}", nc.vector.max(top[s][:], lg[s][:]))
                    nc.vector.memset(carrier[:], 0.0)
                    line(f"idx{s}", nc.vector.max_index(ix[s][:], top[s][:], lg[s][:]))
                    line(f"idf{s}", nc.vector.tensor_copy(ixf[s][:], ix[s][:]))
                    line(f"neg{s}", nc.vector.tensor_scalar(ixf[s][:, 7:8], top[s][:, 0:1], -1.0, None, ALU.mult))
                    for q in range(TOP_K):
                        line(f"hot{q}{s}", nc.vector.tensor_scalar(
                            chosen[:, tile, q, :].rearrange("p a e -> p (a e)"), expertf[:], ixf[s][:, q:q + 1],
                            None, ALU.is_equal))
                    dve.wait_ge(acts, A(f"exp{s}", j))
                    line(f"inve{s}", nc.vector.reciprocal(ixf[s][:, 6:7], ixf[s][:, 6:7]))
                    line(f"gate{s}", nc.vector.tensor_scalar(
                        gates[:, tile, :].rearrange("p a q -> p (a q)"), gt[s][:], ixf[s][:, 6:7], None, ALU.mult))

        @block.tensor
        def _(pe):
            pe.wait_ge(once, 64)
            with pe.Fori(0, LOOPS) as j:
                for s in slots:
                    pe.wait_ge(loaded[s], j * 32 + 32)
                    for h in range(2):
                        for n in range(ND):
                            last = nc.tensor.matmul(hp[s][:, h * HALF:(h + 1) * HALF], ot[s][:, n, :],
                                                    wo[:, n, h * HALF:(h + 1) * HALF],
                                                    start=(n == 0), stop=(n == ND - 1))
                    last.then_inc(pes, 1)
                    pe.wait_ge(dves, V0.n + V(f"m{s}", j))
                    for n in range(ND):
                        last = nc.tensor.transpose(tp[:, n * P:(n + 1) * P], mt[s][:, n * P:(n + 1) * P], k.ident[:])
                    last.then_inc(pes, 1)
                    pe.wait_ge(acts, A(f"mTb{s}", j))
                    for n in range(ND):
                        last = nc.tensor.matmul(lp[s][:, 0:EXPERTS], mT[s][:, n, :], wr[:, n, :],
                                                start=(n == 0), stop=(n == ND - 1))
                    last.then_inc(pes, 1)


def place_rows(nc, k, chosen, row_of, table, row_token):
    with ExitStack() as ctx:
        sb = lambda name, shape, dt=F32: ctx.enter_context(nc.sbuf_tensor(name, shape, dt))
        sem = lambda name: ctx.enter_context(nc.semaphore(name))
        mask = sb("pmask", [P, NT, EXPERTS])
        m1 = sb("pmask1", [P, NT, EXPERTS])
        cnt = sb("pcnt", [P, EXPERTS])
        nb = sb("pnb", [P, EXPERTS])
        ge = sb("pge", [P, EXPERTS])
        incl = sb("pincl", [P, EXPERTS])
        start = sb("pstart", [P, EXPERTS])
        rank = sb("prank", [P, NT, EXPERTS])
        prod = sb("pprod", [P, NT, TOP_K, EXPERTS])
        dest = sb("pdest", [P, NT * TOP_K])
        token = sb("ptoken", [P, NT], I32)
        zero = sb("pzero", [P, ROWS // P], I32)
        rp = ctx.enter_context(nc.psum_tensor("rp", [P, HALF], F32))
        cp = ctx.enter_context(nc.psum_tensor("cp", [P, HALF], F32))
        dves, pes, made, zeroed, scattered = (sem(f"p_{n}") for n in "dves pes made zeroed scattered".split())
        V = Steps("m0 m1 m cnt one " + " ".join(f"ge{n} nb{n}" for n in range(1, T // P)) +
                  " incl first tab0 tab1 start rank prod dest cast")
        block = ctx.enter_context(nc.Block())

        @block.vector
        def _(dve):
            line = Line(dve, dves, V)
            tt = lambda o, a, b, op: nc.vector.tensor_tensor(o, a, b, op)
            line("m0", tt(mask[:], chosen[:, :, 0, :], chosen[:, :, 1, :], ALU.add))
            line("m1", tt(m1[:], chosen[:, :, 2, :], chosen[:, :, 3, :], ALU.add))
            line("m", tt(mask[:], mask[:], m1[:], ALU.add))
            dve.wait_ge(pes, 1)
            line("cnt", nc.vector.tensor_copy(cnt[:], cp[:, 0:EXPERTS]))
            line("one", nc.vector.memset(nb[:], 1.0))
            for n in range(1, T // P):
                line(f"ge{n}", nc.vector.tensor_scalar(ge[:], cnt[:], float(n * P), None, ALU.is_gt))
                line(f"nb{n}", tt(nb[:], nb[:], ge[:], ALU.add))
            line("incl", nc.vector.tensor_tensor_scan(incl[:], k.ones[:, 0:EXPERTS], nb[:], 0.0, ALU.mult, ALU.add))
            line("first", tt(start[:], incl[:], nb[:], ALU.subtract))
            line("tab0", nc.vector.tensor_copy(table[:, 0, :], start[:]))
            line("tab1", nc.vector.tensor_copy(table[:, 1, :], nb[:]))
            line("start", nc.vector.tensor_scalar(start[:], start[:], float(P), None, ALU.mult))
            dve.wait_ge(pes, 2)
            line("rank", tt(rank[:], rp[:, 0:NT * EXPERTS].rearrange("p (t e) -> p t e", e=EXPERTS),
                            start[:].unsqueeze(1).to_broadcast([P, NT, EXPERTS]), ALU.add))
            line("prod", tt(prod[:], chosen[:], rank[:].unsqueeze(2).to_broadcast([P, NT, TOP_K, EXPERTS]), ALU.mult))
            line("dest", nc.vector.tensor_reduce(dest[:], prod[:].rearrange("p t q e -> p (t q) e"), AX.X, ALU.add))
            line("cast", nc.vector.tensor_copy(row_of[:], dest[:]))

        @block.tensor
        def _(pe):
            pe.wait_ge(dves, V("m"))
            for t in range(NT):
                last = nc.tensor.matmul(cp[:, 0:EXPERTS], k.ones[:], mask[:, t, :], start=(t == 0), stop=(t == NT - 1))
            last.then_inc(pes, 1)
            for t in range(NT):
                out = rp[:, t * EXPERTS:(t + 1) * EXPERTS]
                for u in range(t):
                    nc.tensor.matmul(out, k.ones[:], mask[:, u, :], start=(u == 0), stop=False)
                last = nc.tensor.matmul(out, k.before[:], mask[:, t, :], start=(t == 0), stop=True)
            last.then_inc(pes, 1)

        @block.gpsimd
        def _(pool):
            pool.memset(zero[:], 0).then_inc(made, 1)
            pool.iota(token[:], [[P, NT]], base=0, channel_multiplier=1).then_inc(made, 1)
            pool.wait_ge(made, 2)
            pool.dma_start(row_token.rearrange("(p n) o -> p (n o)", p=P), zero[:]).then_inc(zeroed, 16)
            pool.wait_ge(zeroed, 16)
            pool.wait_ge(dves, V("cast"))
            for t in range(NT):
                for q in range(TOP_K):
                    i = t * TOP_K + q
                    pool.indirect_dma_start(row_token, bass.IndirectOffsetOnAxis(ap=row_of[:, i:i + 1], axis=0),
                                            token[:, t:t + 1], None).then_inc(scattered, 16)
            pool.wait_ge(scattered, 16 * NT * TOP_K)


LIMIT, ALPHA = 7.0, 1.702
PARTS = 3


def split_biases(nc, b1, b2, biases):
    F = 2 * D_FF + D
    with ExitStack() as ctx:
        sb = lambda name, shape, dt=F32: ctx.enter_context(nc.sbuf_tensor(name, shape, dt))
        rest = sb("brest", [EXPERTS, F])
        part = [sb(f"bpart{i}", [EXPERTS, F], BF16) for i in range(PARTS)]
        loaded, split, stored = (ctx.enter_context(nc.semaphore(f"b_{n}")) for n in ("loaded", "split", "stored"))
        V = Steps("part0 rest1 part1 rest2 part2")
        block = ctx.enter_context(nc.Block())

        @block.sync
        def _(sp):
            sp.dma_start(rest[:, 0:2 * D_FF], b1).then_inc(loaded, 16)
            sp.dma_start(rest[:, 2 * D_FF:F], b2).then_inc(loaded, 16)
            for i in range(PARTS):
                sp.wait_ge(split, V(f"part{i}"))
                sp.dma_start(biases[:, i, :], part[i][:]).then_inc(stored, 16)
            sp.wait_ge(stored, 16 * PARTS)

        @block.vector
        def _(dve):
            line = Line(dve, split, V)
            dve.wait_ge(loaded, 32)
            for i in range(PARTS):
                if i:
                    line(f"rest{i}", nc.vector.tensor_tensor(rest[:], rest[:], part[i - 1][:], ALU.subtract))
                line(f"part{i}", nc.vector.tensor_copy(part[i][:], rest[:]))


def expert_rows(nc, k, m, row_token, table, w1, w2, biases, yb):
    SLOTS = 6
    order = (0, 2, 1, 3)
    Q = ND // 2
    with ExitStack() as ctx:
        sb = lambda name, shape, dt=F32: ctx.enter_context(nc.sbuf_tensor(name, shape, dt))
        sem = lambda name: ctx.enter_context(nc.semaphore(name))
        w = [sb(f"wslot{c}", [P, ND, HALF]) for c in range(SLOTS)]
        bias = [sb(f"bslot{c}", [PARTS, HALF], BF16) for c in range(SLOTS)]
        ones = sb("bones", [PARTS, P], BF16)
        idx = sb("gidx", [P, 1], U32)
        xg = sb("xg", [P, D])
        xT = sb("xT", [P, ND, P])
        glu = [sb(f"glu{h}", [P, HALF]) for h in range(2)]
        lin = [sb(f"lin{h}", [P, HALF]) for h in range(2)]
        sig = [sb(f"sig{h}", [P, HALF]) for h in range(2)]
        act_t = sb("actt", [P, D_FF])
        aT = sb("aTt", [P, ND, P])
        yo = sb("yo", [P, D])
        tp = [ctx.enter_context(nc.psum_tensor(f"etp{h}", [P, HALF], F32)) for h in range(2)]
        hc = [ctx.enter_context(nc.psum_tensor(f"hc{c}", [P, HALF], F32)) for c in range(SLOTS)]
        w_loaded = [sem(f"w_in{c}") for c in range(SLOTS)]
        used = [sem(f"used{c}") for c in range(SLOTS)]
        idx_loaded, gathered, y_stored, passed = sem("idx_in"), sem("gathered"), sem("y_out"), sem("e_passed")
        x_turned = sem("x_turned")
        act_turned = sem("act_turned")
        x_low, x_high = sem("x_low"), sem("x_high")
        act_copied = sem("act_copied")
        sigmoid_done, ones_made = sem("sigmoid_done"), sem("ones_made")
        y_low, y_high, passed_act = sem("y_low"), sem("y_high"), sem("act_passed")
        dves = sem("e_dves")
        V = Steps("glu0 lin0 mul0 act0 glu1 lin1 mul1 act1")
        flat = lambda t: t.rearrange("p n t -> p (n t)")
        block = ctx.enter_context(nc.Block())

        def blocks(eng, body):
            with eng.Fori(0, EXPERTS) as e:
                first = eng.value_load(table[0:1, 0, bass.ds(e, 1)], min_val=0, max_val=BLOCKS - 1)
                count = eng.value_load(table[0:1, 1, bass.ds(e, 1)], min_val=1, max_val=T // P)
                with eng.Fori(0, count) as b:
                    body(first + b, e)

        @block.sync
        def _(sp):
            def load(c, e):
                src, chunk = (w1, order[c]) if c < 4 else (w2, c - 4)
                cols = slice(chunk * HALF, (chunk + 1) * HALF)
                sp.dma_start(w[c][:], row(src, e).rearrange("o (n p) f -> p (o n) f", p=P)[:, :, cols]
                             ).then_inc(w_loaded[c], 16)
                bcols = slice(cols.start + (0 if c < 4 else 2 * D_FF), cols.stop + (0 if c < 4 else 2 * D_FF))
                sp.dma_start(bias[c][:], row(biases, e).rearrange("o s f -> (o s) f")[:, bcols]
                             ).then_inc(w_loaded[c], 16)

            for c in range(SLOTS):
                load(c, 0)
            with sp.Fori(1, EXPERTS) as e:
                first = sp.value_load(table[0:1, 0, bass.ds(e, 1)], min_val=0, max_val=BLOCKS - 1)
                for c in range(SLOTS):
                    sp.wait_ge(used[c], first)
                    load(c, e)

        @block.gpsimd
        def _(pool):
            def fetch(n):
                pool.dma_start(idx[:], row(row_token, n * P, P)).then_inc(idx_loaded, 16)
                pool.wait_ge(idx_loaded, n * 16 + 16)
                pool.sem_inc(passed, 1)
                pool.indirect_dma_start(xg[:], None, m, bass.IndirectOffsetOnAxis(ap=idx[:, 0:1], axis=0)
                                        ).then_inc(gathered, 16)

            def body(n, e):
                pool.wait_ge(x_turned, n * 2 + 2)
                fetch(n + 1)

            pool.memset(ones[:], 1.0).then_inc(ones_made, 1)
            fetch(0)
            blocks(pool, body)
            last = pool.value_load(table[0:1, 0, EXPERTS - 1:EXPERTS], min_val=0, max_val=BLOCKS - 1)
            more = pool.value_load(table[0:1, 1, EXPERTS - 1:EXPERTS], min_val=1, max_val=T // P)
            pool.wait_ge(gathered, (last + more) * 16 + 16)
            pool.sem_inc(passed, 1)

        @block.scalar
        def _(act):
            def copy_x(n):
                act.wait_ge(x_turned, n * 2 + 2)
                nc.scalar.copy(flat(xT[:, 0:Q, :]), tp[0][:]).then_inc(x_low, 1)

            def sigmoid(h, n):
                act.wait_ge(dves, V(f"glu{h}", n))
                nc.scalar.activation(sig[h][:], glu[h][:], ACT.Sigmoid, scale=ALPHA).then_inc(sigmoid_done, 1)

            def copy_act(h, n):
                act.wait_ge(act_turned, n * 2 + 1 + h)
                nc.scalar.copy(flat(aT[:, Q * h:Q * h + Q, :]), tp[h][:]).then_inc(act_copied, 1)

            def body(n, e):
                sigmoid(0, n)
                copy_act(0, n)
                sigmoid(1, n)
                copy_x(n + 1)
                copy_act(1, n)
                act.wait_ge(used[5], n + 1)
                nc.scalar.copy(yo[:, HALF:D], hc[5][:]).then_inc(y_high, 1)
                act.wait_ge(y_high, n + 1)
                act.wait_ge(y_low, n + 1)
                act.dma_start(row(yb, n * P, P), yo[:]).then_inc(y_stored, 16)
                act.wait_ge(y_stored, n * 16 + 16)
                act.sem_inc(passed_act, 1)

            copy_x(0)
            blocks(act, body)

        @block.vector
        def _(dve):
            def copy_x(n):
                dve.wait_ge(x_turned, n * 2 + 1)
                nc.vector.tensor_copy(flat(xT[:, Q:ND, :]), tp[1][:]).then_inc(x_high, 1)

            def body(n, e):
                line = Line(dve, dves, V, n)
                for h in range(2):
                    dve.wait_ge(used[2 * h], n + 1)
                    line(f"glu{h}", nc.vector.tensor_scalar(glu[h][:], hc[2 * h][:], LIMIT, None, ALU.min))
                    dve.wait_ge(used[2 * h + 1], n + 1)
                    line(f"lin{h}", nc.vector.tensor_scalar(lin[h][:], hc[2 * h + 1][:], LIMIT, -LIMIT,
                                                            ALU.min, ALU.max))
                    line(f"mul{h}", nc.vector.scalar_tensor_tensor(out=lin[h][:], in0=lin[h][:], scalar=1.0,
                                                                   in1=glu[h][:], op0=ALU.add, op1=ALU.mult))
                    dve.wait_ge(sigmoid_done, n * 2 + 1 + h)
                    line(f"act{h}", nc.vector.tensor_tensor(act_t[:, h * HALF:(h + 1) * HALF], lin[h][:], sig[h][:],
                                                            ALU.mult))
                copy_x(n + 1)
                dve.wait_ge(used[4], n + 1)
                nc.vector.tensor_copy(yo[:, 0:HALF], hc[4][:]).then_inc(y_low, 1)

            copy_x(0)
            blocks(dve, body)

        @block.tensor
        def _(pe):
            def turn(src, h):
                for q in range(Q):
                    last = nc.tensor.transpose(tp[h][:, q * P:(q + 1) * P],
                                               src[:, (Q * h + q) * P:(Q * h + q + 1) * P], k.ident[:])
                return last

            def turn_x(n):
                pe.wait_ge(gathered, n * 16 + 16)
                turn(xg, 1).then_inc(x_turned, 1)
                turn(xg, 0).then_inc(x_turned, 1)

            def bias_rows(c, e):
                pe.wait_ge(w_loaded[c], e * 32 + 32)
                nc.tensor.matmul(hc[c][:], ones[:], bias[c][:], start=True, stop=False)

            def part(c, lhsT, q):
                return nc.tensor.matmul(hc[c][:], lhsT[:, q, :], w[c][:, q, :], start=False, stop=(q == ND - 1))

            def product(c, lhsT, e):
                bias_rows(c, e)
                for q in range(ND):
                    last = part(c, lhsT, q)
                last.then_inc(used[c], 1)

            def body(n, e):
                pe.wait_ge(x_low, n + 1)
                pe.wait_ge(x_high, n + 1)
                for c in range(3):
                    product(c, xT, e)
                pe.wait_ge(dves, V("act0", n))
                turn(act_t, 0).then_inc(act_turned, 1)
                product(3, xT, e)
                pe.wait_ge(act_copied, n * 2 + 1)
                turn_x(n + 1)
                for c in (4, 5):
                    bias_rows(c, e)
                for q in range(Q - 1):
                    for c in (4, 5):
                        part(c, aT, q)
                pe.wait_ge(dves, V("act1", n))
                pe.wait_ge(x_high, n + 2)
                turn(act_t, 1).then_inc(act_turned, 1)
                for c in (4, 5):
                    part(c, aT, Q - 1)
                pe.wait_ge(act_copied, n * 2 + 2)
                for c in (4, 5):
                    for q in range(Q, ND):
                        last = part(c, aT, q)
                    last.then_inc(used[c], 1)

            pe.wait_ge(ones_made, 1)
            turn_x(0)
            blocks(pe, body)


def finish(nc, k, h1, yb, row_of, gates, p, w_ple, ple_gain, w_gate, out):
    NP = PLE // P
    with ExitStack() as ctx:
        sb = lambda name, shape, dt=F32: ctx.enter_context(nc.sbuf_tensor(name, shape, dt))
        sem = lambda name: ctx.enter_context(nc.semaphore(name))
        slots = range(2)
        wg = sb("wgate", [P, ND, D])
        wp = sb("wple", [P, NP, D])
        gb = sb("pgain", [P, D])
        ht = [sb(f"fh{s}", [P, D]) for s in slots]
        pt = [sb(f"fp{s}", [P, PLE]) for s in slots]
        rows = [[sb(f"frow{s}{q}", [P, D]) for q in range(TOP_K)] for s in slots]
        ix = [sb(f"fix{s}", [P, TOP_K], U32) for s in slots]
        hT = [sb(f"fhT{s}", [P, ND, P]) for s in slots]
        pT = [sb(f"fpT{s}", [P, NP, P]) for s in slots]
        sg = sb("fsig", [P, D])
        es = sb("fe", [P, D])
        sq = sb("fsq", [P, D])
        st = sb("fst", [P, 2])
        ot = [sb(f"fo{s}", [P, D]) for s in slots]
        tp = ctx.enter_context(nc.psum_tensor("ftp", [P, D], F32))
        pp = ctx.enter_context(nc.psum_tensor("fpp", [P, HALF], F32))
        ep = ctx.enter_context(nc.psum_tensor("fep", [P, D], F32))
        gp = ctx.enter_context(nc.psum_tensor("fgp", [P, D], F32))
        once, passed = sem("f_once"), sem("f_passed")
        loaded = [sem(f"f_loaded{s}") for s in slots]
        fetched = [sem(f"f_rows{s}") for s in slots]
        stored = [sem(f"f_stored{s}") for s in slots]
        acts, dves, pes = sem("f_acts"), sem("f_dves"), sem("f_pes")
        A = Steps(" ".join(f"pT{s} sq{s} root{s} ha{s} hb{s} sig{s}" for s in slots))
        V = Steps(" ".join(f"ix{s} " + " ".join(f"r{q}{s}" for q in range(TOP_K)) + f" inv{s} e{s} g{s} out{s}"
                           for s in slots))
        M = Steps(" ".join(f"pT{s} e{s} hT{s} g{s}" for s in slots))
        LOOPS = NT // 2
        block = ctx.enter_context(nc.Block())

        @block.sync
        def _(sp):
            sp.dma_start(wp[:], w_ple.rearrange("(n p) e -> p n e", p=P)).then_inc(once, 16)
            sp.dma_start(gb[:], ple_gain.rearrange("(o e) -> o e", o=1).to_broadcast([P, D])).then_inc(once, 16)
            sp.dma_start(wg[:], w_gate.rearrange("(n p) e -> p n e", p=P)).then_inc(once, 16)
            with sp.Fori(0, LOOPS) as j:
                for s in slots:
                    first = sp.snap(j * 2 * P + s * P)
                    sp.wait_ge(stored[s], j * 16)
                    sp.dma_start(ht[s][:], row(h1, first, P)).then_inc(loaded[s], 16)
                    sp.dma_start(pt[s][:], row(p, first, P)).then_inc(loaded[s], 16)

        @block.gpsimd
        def _(pool):
            with pool.Fori(0, LOOPS) as j:
                for s in slots:
                    pool.wait_ge(dves, V(f"ix{s}", j))
                    pool.sem_inc(passed, 1)
                    for q in range(TOP_K):
                        pool.indirect_dma_start(rows[s][q][:], None, yb,
                                                bass.IndirectOffsetOnAxis(ap=ix[s][:, q:q + 1], axis=0)
                                                ).then_inc(fetched[s], 16)

        @block.scalar
        def _(act):
            with act.Fori(0, LOOPS) as j:
                line = Line(act, acts, A, j)
                for s in slots:
                    act.wait_ge(pes, M(f"pT{s}", j))
                    line(f"pT{s}", nc.scalar.copy(pT[s][:].rearrange("p n t -> p (n t)"), pp[:, 0:PLE]))
                    act.wait_ge(pes, M(f"e{s}", j))
                    line(f"sq{s}", nc.scalar.activation(sq[:], ep[:], ACT.Square, accum_out=st[:, 0:1]))
                    line(f"root{s}", nc.scalar.activation(st[:, 0:1], st[:, 0:1], ACT.Sqrt, bias=k.eps[:, 0:1],
                                                          scale=1.0 / D))
                    act.wait_ge(pes, M(f"hT{s}", j))
                    for n in range(2):
                        line(f"h{'ab'[n]}{s}", nc.scalar.copy(
                            hT[s][:].rearrange("p n t -> p (n t)")[:, n * HALF:(n + 1) * HALF],
                            tp[:, n * HALF:(n + 1) * HALF]))
                    act.wait_ge(pes, M(f"g{s}", j))
                    line(f"sig{s}", nc.scalar.activation(sg[:], gp[:], ACT.Sigmoid))
                    act.wait_ge(dves, V(f"out{s}", j))
                    act.dma_start(row(out, j * 2 * P + s * P, P), ot[s][:]).then_inc(stored[s], 16)
            for s in slots:
                act.wait_ge(stored[s], 16 * LOOPS)

        @block.vector
        def _(dve):
            dve.wait_ge(once, 48)
            with dve.Fori(0, LOOPS) as j:
                line = Line(dve, dves, V, j)
                for s in slots:
                    dve.wait_ge(fetched[s], j * 64)
                    line(f"ix{s}", nc.vector.tensor_copy(ix[s][:], row_of[:, bass.ds((j * 2 + s) * TOP_K, TOP_K)]))
                    dve.wait_ge(loaded[s], j * 32 + 32)
                    dve.wait_ge(fetched[s], j * 64 + 64)
                    for q in range(TOP_K):
                        line(f"r{q}{s}", nc.vector.scalar_tensor_tensor(
                            out=ht[s][:], in0=rows[s][q][:],
                            scalar=gates[:, bass.ds(j * 2 + s, 1), q:q + 1].rearrange("p a q -> p (a q)"),
                            in1=ht[s][:], op0=ALU.mult, op1=ALU.add))
                    dve.wait_ge(acts, A(f"root{s}", j))
                    line(f"inv{s}", nc.vector.reciprocal(st[:, 1:2], st[:, 0:1]))
                    line(f"e{s}", nc.vector.scalar_tensor_tensor(out=es[:], in0=ep[:], scalar=st[:, 1:2], in1=gb[:],
                                                                 op0=ALU.mult, op1=ALU.mult))
                    dve.wait_ge(acts, A(f"sig{s}", j))
                    line(f"g{s}", nc.vector.tensor_tensor(es[:], es[:], sg[:], ALU.mult))
                    dve.wait_ge(stored[s], j * 16)
                    line(f"out{s}", nc.vector.tensor_tensor(ot[s][:], es[:], ht[s][:], ALU.add))

        @block.tensor
        def _(pe):
            pe.wait_ge(once, 48)
            with pe.Fori(0, LOOPS) as j:
                for s in slots:
                    pe.wait_ge(loaded[s], j * 32 + 32)
                    pe.wait_ge(dves, V.n * j if s == 0 else V("out0", j))
                    for n in range(NP):
                        last = nc.tensor.transpose(pp[:, n * P:(n + 1) * P], pt[s][:, n * P:(n + 1) * P], k.ident[:])
                    last.then_inc(pes, 1)
                    pe.wait_ge(acts, A(f"pT{s}", j))
                    for h in range(2):
                        for n in range(NP):
                            last = nc.tensor.matmul(ep[:, h * HALF:(h + 1) * HALF], pT[s][:, n, :],
                                                    wp[:, n, h * HALF:(h + 1) * HALF], start=(n == 0), stop=(n == NP - 1))
                    last.then_inc(pes, 1)
                    pe.wait_ge(dves, V(f"r{TOP_K - 1}{s}", j))
                    for n in range(ND):
                        last = nc.tensor.transpose(tp[:, n * P:(n + 1) * P], ht[s][:, n * P:(n + 1) * P], k.ident[:])
                    last.then_inc(pes, 1)
                    pe.wait_ge(acts, A(f"hb{s}", j))
                    for h in range(2):
                        for n in range(ND):
                            last = nc.tensor.matmul(gp[:, h * HALF:(h + 1) * HALF], hT[s][:, n, :],
                                                    wg[:, n, h * HALF:(h + 1) * HALF], start=(n == 0), stop=(n == ND - 1))
                    last.then_inc(pes, 1)


def build_layer(nc, x, p, norm_mix_g, w_in, rw_mu, rw_w0, rw_w2, rw_a0, rw_a2, rw_g2, rw_k_k, rw_k_a, rw_r_k,
                rw_ln_g, rw_ln_b, da_q_norm_g, da_k_norm_g, da_lq1, da_lk1, da_lq2, da_lk2, da_subln_g, w_out,
                norm_ffn_g, w_router, b_router, w1, b1, w2, b2, w_ple, ple_norm_g, w_ple_gate, out):
    scratch = lambda name, shape, dt=F32: nc.dram_tensor(name, shape, dt, kind="Internal").ap()
    zT = scratch("zT", [IN_COLS, T])
    ops = scratch("scan_ops", [2, C_RW, 4, T])
    vals = scratch("scan_vals", [C_RW, T])
    bonus = scratch("bonus", [C_RW, T])
    gate_in = scratch("gate_in", [P, T])
    end_decay = scratch("end_decay", [2, C_RW, NCH])
    y = scratch("scan_y", [2, T, C_RW])
    oT = scratch("mixed", [D, T])
    h1 = scratch("h1", [T, D])
    m = scratch("ffn_in", [T, D])
    row_token = scratch("row_token", [ROWS, 1], U32)
    yb = scratch("expert_out", [ROWS, D])
    biases = scratch("biases", [EXPERTS, PARTS, 2 * D_FF + D], BF16)
    flat = lambda ap: ap.rearrange("h n -> (h n)")
    x, p, out = x[0], p[0, 0], out[0]
    with ExitStack() as ctx:
        sb = lambda name, shape, dt=F32: ctx.enter_context(nc.sbuf_tensor(name, shape, dt))

        class k:
            ident, ones, head_ones, before = (sb(n, [P, P]) for n in ("ident", "ones", "head_ones", "before"))
            zeros = sb("zeros", [P, D])
            causal = sb("causal", [P, 2, 4, P])
            near = sb("near", [P, 3, P])
            chunk_col = sb("chunk_col", [P, 2])
            scan_keep = sb("scan_keep", [P, T])
            eps = sb("eps", [P, 3])

        chosen = sb("chosen", [P, NT, TOP_K, EXPERTS])
        gates = sb("gates", [P, NT, TOP_K])
        row_of = sb("row_of", [P, NT * TOP_K], U32)
        table = sb("table", [P, 2, EXPERTS], I32)
        constants(nc, k)
        split_biases(nc, b1[0], b2[0], biases)
        with nc.sbuf_tensor("uT", [P, ND, T], F32) as uT:
            normed_columns(nc, k, x, norm_mix_g[0], uT)
            project_in(nc, k, uT, w_in[0], zT)
        rwkv_prepare(nc, k, zT, rw_mu[0], rw_w0[0], rw_w2[0], rw_a0[0], rw_a2[0], rw_k_k[0], rw_k_a[0],
                     flat(rw_r_k[0]), ops, vals, bonus, gate_in, end_decay)
        rwkv_scan(nc, k, ops, vals, end_decay, y, yb)
        differential_attention(nc, k, zT, da_q_norm_g[0], da_k_norm_g[0], da_lq1[0], da_lk1[0], da_lq2[0],
                               da_lk2[0], da_subln_g[0], oT)
        finish_rwkv(nc, k, y, bonus, gate_in, rw_g2[0], flat(rw_ln_g[0]), flat(rw_ln_b[0]), oT)
        mix_out_and_route(nc, k, x, oT, w_out[0], norm_ffn_g[0], w_router[0], b_router[0], h1, m, chosen, gates)
        place_rows(nc, k, chosen, row_of, table, row_token)
        expert_rows(nc, k, m, row_token, table, w1[0], w2[0], biases, yb)
        finish(nc, k, h1, yb, row_of, gates, p, w_ple[0], ple_norm_g[0], w_ple_gate[0], out)


INPUTS = ("x p norm_mix_g w_in rw_mu rw_w0 rw_w2 rw_a0 rw_a2 rw_g2 rw_k_k rw_k_a rw_r_k rw_ln_g rw_ln_b "
          "da_q_norm_g da_k_norm_g da_lq1 da_lk1 da_lq2 da_lk2 da_subln_g w_out norm_ffn_g w_router b_router "
          "w1 b1 w2 b2 w_ple ple_norm_g w_ple_gate").split()


def kernel(**inputs):
    import numpy as np
    import concourse.bacc as bacc
    from concourse.bass_utils import run_bass_kernel_spmd

    nc = bacc.Bacc("TRN2", target_bir_lowering=False, num_devices=1)
    arrays, args = {}, []
    for name in INPUTS:
        a = np.ascontiguousarray(inputs[name])
        arrays[f"in_{name}"] = a
        args.append(nc.dram_tensor(f"in_{name}", a.shape, mybir.dt.from_np(a.dtype), kind="ExternalInput").ap())
    args.append(nc.dram_tensor("out_h", (1, T, D), F32, kind="ExternalOutput").ap())
    build_layer(nc, *args)
    r = run_bass_kernel_spmd(nc, [arrays], core_ids=[0])
    return r.results[0]["out_h"]
```

```python
import math
from contextlib import ExitStack

import concourse.bass as bass
from concourse import mybir
from concourse.alu_op_type import AluOpType as ALU

F32 = mybir.dt.float32
BF16 = mybir.dt.bfloat16
U32 = mybir.dt.uint32
I32 = mybir.dt.int32
ACT = mybir.ActivationFunctionType
AX = mybir.AxisListType

P = 128
T, D = 1024, 1024
NT = T // P
ND = D // P
HALF = 512
C_RW = D // 2
RW_TILES = C_RW // P
HEAD = 64
CHUNK = 64
NCH = T // CHUNK
LORA = 64
RW_COLS = 3 * C_RW + 4 * LORA + 128
C_DA = D - C_RW
DA_HEADS = 4
IN_COLS = RW_COLS + 3 * C_DA
IN_TILES = IN_COLS // P
EXPERTS, TOP_K, D_FF = 32, 4, D
PLE = 256
BLOCKS = (T * TOP_K + EXPERTS * P) // P
ROWS = (BLOCKS + T // P) * P
NORM_EPS = 1e-6
RW_GN_EPS = HEAD * 1e-5
LAMBDA_INIT = 0.8 - 0.6 * math.exp(0.0)
DECAY = math.exp(-0.5)


def row(ap, i, n=1):
    return ap[bass.ds(i, n)]


class Steps:

    def __init__(self, text):
        self.names = text.split()
        self.n = len(self.names)

    def __call__(self, name, i=0):
        return self.names.index(name) + 1 + i * self.n


class Line:

    def __init__(self, eng, sem, steps, i=0, base=0):
        self.eng, self.sem, self.steps, self.i, self.base, self.at = eng, sem, steps, i, base, 0

    def __call__(self, name, instruction):
        assert self.steps.names[self.at] == name, (name, self.steps.names[self.at])
        self.at += 1
        instruction.then_inc(self.sem, 1)
        self.eng.wait_ge(self.sem, self.steps(name, self.i) + self.base)


def constants(nc, k):
    with nc.semaphore("const_made") as made, nc.Block() as block:

        @block.gpsimd
        def _(pool):
            n = 0

            def select(t, pattern, mult, base, op, fill):
                nonlocal n
                pool.wait_ge(made, n)
                pool.affine_select(out=t, in_=t, compare_op=op, fill=fill, base=base,
                                   pattern=pattern, channel_multiplier=mult).then_inc(made, 1)
                n += 1

            def fill(t, v):
                nonlocal n
                pool.memset(t, v).then_inc(made, 1)
                n += 1

            def blocks(t, size):
                v = t.rearrange("p (b s) -> p b s", s=size)
                m = P // size
                select(v, [[-size, m], [0, size]], 1, 0, ALU.is_ge, 0.0)
                select(v, [[size, m], [0, size]], -1, size - 1, ALU.is_ge, 0.0)

            fill(k.ident[:], 0.0)
            select(k.ident[:], [[-1, P]], 1, 0, ALU.not_equal, 1.0)
            fill(k.ones[:], 1.0)
            fill(k.zeros[:], 0.0)
            fill(k.head_ones[:], 1.0)
            blocks(k.head_ones[:], HEAD)
            fill(k.before[:], 1.0)
            select(k.before[:], [[1, P]], -1, 0, ALU.is_gt, 0.0)
            for d in range(2):
                s = 1 - 2 * d
                for kind, op in ((0, ALU.is_gt), (1, ALU.is_ge)):
                    fill(k.causal[:, d, kind, :], 1.0)
                    select(k.causal[:, d, kind, :], [[s, P]], -s, 0, op, 0.0)
                    blocks(k.causal[:, d, kind, :], CHUNK)
                    fill(k.causal[:, d, 2 + kind, :], 1.0)
                    select(k.causal[:, d, 2 + kind, :], [[s, P]], -s, 0, op, 0.0)
                    blocks(k.causal[:, d, 2 + kind, :], CHUNK)
            for level, size in enumerate((16, 32, 64)):
                fill(k.near[:, level, :], 1.0)
                blocks(k.near[:, level, :], size)
            for level in (2, 1):
                pool.wait_ge(made, n)
                pool.tensor_tensor(k.near[:, level, :], k.near[:, level, :], k.near[:, level - 1, :],
                                   ALU.subtract).then_inc(made, 1)
                n += 1
            fill(k.chunk_col[:], 1.0)
            v = k.chunk_col[:]
            select(v[:, 0:1], [[0, 1]], -1, CHUNK - 1, ALU.is_ge, 0.0)
            select(v[:, 1:2], [[0, 1]], 1, -CHUNK, ALU.is_ge, 0.0)
            fill(k.scan_keep[:], 1.0)
            v = k.scan_keep[:].rearrange("p (c s) -> p c s", s=CHUNK)
            select(v, [[0, NCH], [1, CHUNK]], 0, 0, ALU.not_equal, 0.0)
            fill(k.eps[:, 0:1], NORM_EPS)
            fill(k.eps[:, 1:2], 1e-12)
            fill(k.eps[:, 2:3], RW_GN_EPS)
            pool.wait_ge(made, n)


def normed_columns(nc, k, x, gain, uT):
    with ExitStack() as ctx:
        sb = lambda name, shape, dt=F32: ctx.enter_context(nc.sbuf_tensor(name, shape, dt))
        sem = lambda name: ctx.enter_context(nc.semaphore(name))
        xt = [sb(f"xt{s}", [P, D]) for s in range(2)]
        xn = [sb(f"xn{s}", [P, D]) for s in range(2)]
        sq = [sb(f"sq{s}", [P, D]) for s in range(2)]
        ssq = sb("ssq", [P, 2, 4])
        gcol = sb("gcol", [P, ND])
        ps = [ctx.enter_context(nc.psum_tensor(f"tp{s}", [P, D], F32)) for s in range(2)]
        x_loaded = [sem(f"x_loaded{s}") for s in range(2)]
        gain_loaded = sem("gain_loaded")
        act_done, dve_done, transposed = sem("a_done"), sem("v_done"), sem("transposed")
        A = Steps("ssq0 root0 ssq1 root1")
        V = Steps("inv0 xn0 out0 inv1 xn1 out1")
        block = ctx.enter_context(nc.Block())
        PAIRS = NT // 2

        @block.sync
        def _(sp):
            with nc.allow_non_contiguous_dma(reason="gain columns"):
                sp.dma_start(gcol[:], gain.rearrange("(n p) -> p n", p=P)).then_inc(gain_loaded, 16)
            sp.wait_ge(gain_loaded, 16)
            with sp.Fori(0, PAIRS) as j:
                for s in range(2):
                    first = sp.snap(j * 2 * P + s * P)
                    sp.wait_ge(dve_done, j * V.n)
                    sp.dma_start(xt[s][:], row(x, first, P)).then_inc(x_loaded[s], 16)

        @block.scalar
        def _(act):
            with act.Fori(0, PAIRS) as j:
                for s in range(2):
                    act.wait_ge(x_loaded[s], j * 16 + 16)
                    act.wait_ge(dve_done, j * V.n)
                    nc.scalar.activation(sq[s][:], xt[s][:], ACT.Square,
                                         accum_out=ssq[:, s, 0:1]).then_inc(act_done, 1)
                    act.wait_ge(act_done, A(f"ssq{s}", j))
                    nc.scalar.activation(ssq[:, s, 1:2], ssq[:, s, 0:1], ACT.Sqrt, bias=k.eps[:, 0:1],
                                         scale=1.0 / D).then_inc(act_done, 1)

        @block.vector
        def _(dve):
            with dve.Fori(0, PAIRS) as j:
                for s in range(2):
                    dve.wait_ge(act_done, A(f"root{s}", j))
                    nc.vector.reciprocal(ssq[:, s, 2:3], ssq[:, s, 1:2]).then_inc(dve_done, 1)
                    dve.wait_ge(dve_done, V(f"inv{s}", j))
                    dve.wait_ge(transposed, j * 2)
                    nc.vector.tensor_scalar(xn[s][:], xt[s][:], ssq[:, s, 2:3], None,
                                            ALU.mult).then_inc(dve_done, 1)
                    dve.wait_ge(transposed, j * 2 + s + 1)
                    nc.vector.tensor_tensor(
                        uT[:, :, bass.ds(j * 2 * P + s * P, P)],
                        ps[s][:].rearrange("p (n t) -> p n t", t=P),
                        gcol[:].unsqueeze(2).to_broadcast([P, ND, P]), ALU.mult).then_inc(dve_done, 1)
            dve.wait_ge(gain_loaded, 16)

        @block.tensor
        def _(pe):
            with pe.Fori(0, PAIRS) as j:
                for s in range(2):
                    pe.wait_ge(dve_done, V(f"xn{s}", j))
                    for n in range(ND):
                        last = nc.tensor.transpose(ps[s][:, n * P:(n + 1) * P], xn[s][:, n * P:(n + 1) * P],
                                                   k.ident[:])
                    last.then_inc(transposed, 1)


def project_in(nc, k, uT, w_in, zT):
    R = 3
    with ExitStack() as ctx:
        sb = lambda name, shape, dt=F32: ctx.enter_context(nc.sbuf_tensor(name, shape, dt))
        sem = lambda name: ctx.enter_context(nc.semaphore(name))
        w = [sb(f"win{s}", [P, ND, P]) for s in range(R)]
        z = [sb(f"z{s}", [P, T]) for s in range(R)]
        ps = [ctx.enter_context(nc.psum_tensor(f"zp{s}", [P, T], F32)) for s in range(R)]
        w_loaded = [sem(f"w_loaded{s}") for s in range(R)]
        z_stored = [sem(f"z_stored{s}") for s in range(R)]
        multiplied = [sem(f"multiplied{s}") for s in range(R)]
        copied = [sem(f"copied{s}") for s in range(R)]
        block = ctx.enter_context(nc.Block())
        w_view = w_in.rearrange("(kt p) n -> p kt n", p=P)

        @block.sync
        def _(sp):
            with sp.Fori(0, IN_TILES // R) as j:
                for s in range(R):
                    first = sp.snap(j * R * P + s * P)
                    sp.wait_ge(multiplied[s], j)
                    sp.dma_start(w[s][:], w_view[:, :, bass.ds(first, P)]).then_inc(w_loaded[s], 16)

        @block.gpsimd
        def _(pool):
            with pool.Fori(0, IN_TILES // R) as j:
                for s in range(R):
                    pool.wait_ge(copied[s], j * 2 + 2)
                    pool.dma_start(row(zT, j * R * P + s * P, P), z[s][:]).then_inc(z_stored[s], 16)
            for s in range(R):
                pool.wait_ge(z_stored[s], 16 * (IN_TILES // R))

        @block.tensor
        def _(pe):
            with pe.Fori(0, IN_TILES // R) as j:
                for s in range(R):
                    pe.wait_ge(w_loaded[s], j * 16 + 16)
                    pe.wait_ge(copied[s], j * 2)
                    for h in range(2):
                        for kt in range(ND):
                            last = nc.tensor.matmul(ps[s][:, h * HALF:(h + 1) * HALF], w[s][:, kt, :],
                                                    uT[:, kt, h * HALF:(h + 1) * HALF],
                                                    start=(kt == 0), stop=(kt == ND - 1))
                    last.then_inc(multiplied[s], 1)

        def copies(eng, copy, half):
            with eng.Fori(0, IN_TILES // R) as j:
                for s in range(R):
                    eng.wait_ge(multiplied[s], j + 1)
                    eng.wait_ge(z_stored[s], j * 16)
                    cols = slice(half * HALF, (half + 1) * HALF)
                    copy(z[s][:, cols], ps[s][:, cols]).then_inc(copied[s], 1)

        @block.scalar
        def _(act):
            copies(act, nc.scalar.copy, 0)

        @block.vector
        def _(dve):
            copies(dve, nc.vector.tensor_copy, 1)


def rwkv_prepare(nc, k, zT, mu, w0, w2, a0, a2, k_k, k_a, r_k, ops, vals, bonus, gate_in, end_decay):
    with ExitStack() as ctx:
        sb = lambda name, shape, dt=F32: ctx.enter_context(nc.sbuf_tensor(name, shape, dt))
        sem = lambda name: ctx.enter_context(nc.semaphore(name))
        low = [sb(f"low{i}", [P, T + 2]) for i in range(3)]
        zin = [sb(f"zin{i}", [P, T + 2]) for i in range(3)]
        rkv = [sb(f"rkv{i}", [P, T]) for i in range(3)]
        mixc = sb("mixc", [P, 3, RW_COLS // P])
        par = sb("par", [P, 4, 5 + 3])
        parv = sb("parv", [P, 8, 4])
        lw_w = [sb(f"lora{i}", [P, P]) for i in range(4)]
        tmp = [sb(f"tmp{i}", [P, T]) for i in range(3)]
        kk = sb("kk", [P, T])
        lwt = sb("lwt", [P, T])
        rate = sb("rate", [P, T])
        acc = sb("accl", [P, T])
        inc = sb("inc", [P, T])
        exc = sb("exc", [P, T])
        kdir = [sb(f"kdir{d}", [P, T]) for d in range(2)]
        res = sb("res", [P, 4, T])
        dec = sb("dec", [P, NCH])
        tot = sb("tot", [P, NCH])
        psA = ctx.enter_context(nc.psum_tensor("psA", [P, T], F32))
        psB = ctx.enter_context(nc.psum_tensor("psB", [P, T], F32))
        psC = ctx.enter_context(nc.psum_tensor("psC", [P, T], F32))
        par_loaded, lora_loaded = sem("par_loaded"), sem("lora_loaded")
        low_loaded, z_loaded = sem("low_loaded"), sem("z_loaded")
        edge, acts, dves, pes = sem("edge"), sem("acts"), sem("dves"), sem("pes")
        stored, res_stored = sem("stored"), sem("res_stored")
        kept, cut, passed = sem("kept"), sem("decay_cut"), sem("w_passed")
        low_stored = sem("low_stored")

        V0 = Steps("one_minus half s0 m0 o0 s1 m1 o1 s2 m2 o2 omka")
        A0 = Steps("tanh sig")
        V = Steps("sr mr rr sk mk rk sv mv rv kkr kkinv kk "
                  "lw0 scan0 inc0 exc0 m0 kd0 a0 r0 bb0 b0 k0 "
                  "lw1 scan1 tot1 exc1 inc1 m1 kd1 a1 r1 bb1 b1 k1 "
                  "kb q0 q1 bv")
        A = Steps("sq root sw0 sa0 ex0 in0 en0 dc0 sw1 sa1 ex1 in1 en1 dc1")
        M = Steps("norm w0 a0 w1 a1 bonus")
        block = ctx.enter_context(nc.Block())
        mu_v = mu.rearrange("(n p) -> p n", p=P)

        @block.sync
        def _(sp):
            with nc.allow_non_contiguous_dma(reason="per-channel parameters as columns"):
                sp.dma_start(mixc[:, 0, :], mu_v).then_inc(par_loaded, 16)
                for d in range(2):
                    sp.dma_start(parv[:, 0 + d, :], w0[d].rearrange("(n p) -> p n", p=P)).then_inc(par_loaded, 16)
                    sp.dma_start(parv[:, 2 + d, :], a0[d].rearrange("(n p) -> p n", p=P)).then_inc(par_loaded, 16)
                for i, v in enumerate((k_k, k_a, r_k)):
                    sp.dma_start(parv[:, 4 + i, :], v.rearrange("(n p) -> p n", p=P)).then_inc(par_loaded, 16)
            sp.wait_ge(edge, 2)
            for i in range(3):
                n = 3 * RW_TILES + i
                sp.dma_start(low[i][:, 1:T + 1], zT[n * P:(n + 1) * P, :]).then_inc(low_loaded, 16)
            with sp.Fori(0, RW_TILES) as c:
                first = sp.snap(c * P)
                sources = [row(zT[i * C_RW:(i + 1) * C_RW], first, P) for i in range(3)]
                sp.wait_ge(dves, V0.n + c * V.n)
                for i in range(3):
                    sp.dma_start(zin[i][:, 1:T + 1], sources[i]).then_inc(z_loaded, 16)

        @block.gpsimd
        def _(pool):
            for t in low + zin:
                pool.memset(t[:, 0:1], 0.0)
                last = pool.memset(t[:, T + 1:T + 2], 0.0)
            last.then_inc(edge, 1)
            for t in lw_w:
                last = pool.memset(t[:], 0.0)
            last.then_inc(edge, 1)
            pool.wait_ge(acts, A0("sig"))
            pool.dma_start(gate_in, low[2][:, 1:T + 1]).then_inc(low_stored, 16)
            pool.wait_ge(low_stored, 16)
            with pool.Fori(0, RW_TILES) as c:
                for d in range(2):
                    pool.wait_ge(dves, V(f"k{d}", c) + V0.n)
                    pool.wait_ge(edge, 2)
                    pool.dma_start(row(ops[d], c * P, P), res[:]).then_inc(res_stored, 16)
                    pool.wait_ge(acts, A(f"dc{d}", c) + A0.n)
                    pool.sem_inc(passed, 1)
                    last = (NCH - 1) * (1 - d)
                    pool.memset(dec[:, last:last + 1], 0.0).then_inc(cut, 1)
                    pool.wait_ge(cut, c * 2 + d + 1)
                    pool.dma_start(row(end_decay[d], c * P, P), dec[:]).then_inc(stored, 16)
                pool.wait_ge(dves, V("bv", c) + V0.n)
                pool.wait_ge(edge, 2)
                pool.dma_start(row(vals, c * P, P), rkv[2][:]).then_inc(kept, 16)
                pool.dma_start(row(bonus, c * P, P), tmp[2][:]).then_inc(kept, 16)

            for s in (res_stored, stored, kept):
                pool.wait_ge(s, 32 * RW_TILES)

        def shift(line, names, src, out, scr, n):
            line(names[0], nc.vector.tensor_tensor(scr[:], src[:, 0:T], src[:, 2:T + 2], ALU.add))
            line(names[1], nc.vector.tensor_scalar(scr[:], scr[:], mixc[:, 2, n], None, ALU.mult))
            line(names[2], nc.vector.scalar_tensor_tensor(out=out, in0=src[:, 1:T + 1], scalar=mixc[:, 1, n],
                                                          in1=scr[:], op0=ALU.mult, op1=ALU.add))

        @block.vector
        def _(dve):
            line = Line(dve, dves, V0)
            dve.wait_ge(par_loaded, 16 * 8)
            line("one_minus", nc.vector.tensor_scalar(mixc[:, 1, :], mixc[:, 0, :], -1.0, 1.0, ALU.mult, ALU.add))
            line("half", nc.vector.tensor_scalar(mixc[:, 2, :], mixc[:, 0, :], 0.5, None, ALU.mult))
            dve.wait_ge(low_loaded, 48)
            for i in range(3):
                n = 3 * RW_TILES + i
                shift(line, (f"s{i}", f"m{i}", f"o{i}"), low[i], low[i][:, 1:T + 1], tmp[0], slice(n, n + 1))
            line("omka", nc.vector.tensor_scalar(parv[:, 7, :], parv[:, 5, :], -1.0, 1.0, ALU.mult, ALU.add))
            with dve.Fori(0, RW_TILES) as c:
                line = Line(dve, dves, V, c, V0.n)
                mul = lambda out, x, y: nc.vector.tensor_tensor(out, x, y, ALU.mult)
                col = lambda j: parv[:, j, bass.ds(c, 1)]
                dve.wait_ge(z_loaded, c * 48 + 48)
                dve.wait_ge(kept, c * 32)
                for i, x in enumerate("rkv"):
                    shift(line, (f"s{x}", f"m{x}", f"r{x}"), zin[i], rkv[i][:], tmp[0], bass.ds(c + i * RW_TILES, 1))
                r, ky, v = rkv
                line("kkr", nc.vector.tensor_scalar(tmp[1][:], ky[:], col(4), None, ALU.mult))
                dve.wait_ge(acts, A0.n + A("root", c))
                line("kkinv", nc.vector.reciprocal(tmp[0][:], tmp[0][:]))
                line("kk", mul(kk[:], tmp[1][:], tmp[0][:]))
                for d in range(2):
                    dve.wait_ge(acts, A0.n + A(f"sw{d}", c))
                    line(f"lw{d}", nc.vector.tensor_scalar(lwt[:], lwt[:], -DECAY, None, ALU.mult))
                    line(f"scan{d}", nc.vector.tensor_tensor_scan(acc[:], k.scan_keep[:], lwt[:], 0.0,
                                                                  ALU.mult, ALU.add))
                    if d == 0:
                        line("inc0", nc.vector.tensor_copy(inc[:], acc[:]))
                        line("exc0", nc.vector.tensor_tensor(exc[:], acc[:], lwt[:], ALU.subtract))
                    else:
                        av = acc[:].rearrange("p (c s) -> p c s", s=CHUNK)
                        line("tot1", nc.vector.tensor_copy(tot[:], av[:, :, CHUNK - 1]))
                        line("exc1", nc.vector.tensor_tensor(exc[:].rearrange("p (c s) -> p c s", s=CHUNK),
                                                             tot[:].unsqueeze(2).to_broadcast([P, NCH, CHUNK]), av,
                                                             ALU.subtract))
                        line("inc1", nc.vector.tensor_tensor(inc[:], exc[:], lwt[:], ALU.add))
                    dve.wait_ge(acts, A0.n + A(f"sa{d}", c))
                    line(f"m{d}", nc.vector.tensor_scalar(tmp[0][:], rate[:], col(5), col(7), ALU.mult, ALU.add))
                    line(f"kd{d}", mul(kdir[d][:], tmp[0][:], ky[:]))
                    dve.wait_ge(res_stored, c * 32 + d * 16)
                    dve.wait_ge(acts, A0.n + A(f"ex{d}", c))
                    line(f"a{d}", nc.vector.scalar_tensor_tensor(out=res[:, 0, :], in0=exc[:], scalar=-1.0,
                                                                 in1=kk[:], op0=ALU.mult, op1=ALU.mult))
                    dve.wait_ge(acts, A0.n + A(f"en{d}", c))
                    line(f"r{d}", mul(res[:, 1, :], r[:], tmp[1][:]))
                    line(f"bb{d}", mul(tmp[0][:], kk[:], rate[:]))
                    line(f"b{d}", mul(res[:, 2, :], tmp[0][:], tmp[2][:]))
                    line(f"k{d}", mul(res[:, 3, :], kdir[d][:], tmp[2][:]))
                line("kb", nc.vector.tensor_tensor(tmp[0][:], kdir[0][:], kdir[1][:], ALU.add))
                line("q0", mul(tmp[0][:], tmp[0][:], r[:]))
                line("q1", nc.vector.tensor_scalar(tmp[0][:], tmp[0][:], col(6), 0.5, ALU.mult, ALU.mult))
                dve.wait_ge(pes, M("bonus", c))
                line("bv", mul(tmp[2][:], psC[:], v[:]))

        @block.scalar
        def _(act):
            line = Line(act, acts, A0)
            act.wait_ge(dves, V0("omka"))
            line("tanh", nc.scalar.activation(low[0][:, 1:T + 1], low[0][:, 1:T + 1], ACT.Tanh))
            line("sig", nc.scalar.activation(low[2][:, 1:T + 1], low[2][:, 1:T + 1], ACT.Sigmoid))
            with act.Fori(0, RW_TILES) as c:
                act.wait_ge(edge, 2)
                act.wait_ge(pes, M.n * c)
                for d in range(2):
                    half = slice(d * LORA, (d + 1) * LORA)
                    act.dma_start(lw_w[d][half, :], w2[d][:, bass.ds(c * P, P)]).then_inc(lora_loaded, 16)
                    act.dma_start(lw_w[2 + d][half, :], a2[d][:, bass.ds(c * P, P)]).then_inc(lora_loaded, 16)
                line = Line(act, acts, A, c, A0.n)
                vdone = lambda name: V0.n + V(name, c)
                col = lambda j: parv[:, j, bass.ds(c, 1)]
                act.wait_ge(dves, vdone("kkr"))
                line("sq", nc.scalar.activation(tmp[2][:], tmp[1][:], ACT.Square))
                act.wait_ge(pes, M("norm", c))
                line("root", nc.scalar.activation(tmp[0][:], psC[:], ACT.Sqrt, bias=k.eps[:, 1:2]))
                for d in range(2):
                    act.wait_ge(pes, M(f"w{d}", c))
                    if d == 1:
                        act.wait_ge(dves, vdone("k0"))
                    line(f"sw{d}", nc.scalar.activation(lwt[:], psA[:], ACT.Sigmoid, bias=col(d)))
                    act.wait_ge(pes, M(f"a{d}", c))
                    line(f"sa{d}", nc.scalar.activation(rate[:], psB[:], ACT.Sigmoid, bias=col(2 + d)))
                    act.wait_ge(dves, vdone(f"m{d}"))
                    line(f"ex{d}", nc.scalar.activation(exc[:], exc[:], ACT.Exp))
                    line(f"in{d}", nc.scalar.activation(tmp[1][:], inc[:], ACT.Exp))
                    line(f"en{d}", nc.scalar.activation(tmp[2][:], inc[:], ACT.Exp, scale=-1.0))
                    act.wait_ge(stored, c * 32 + d * 16)
                    end = CHUNK - 1 if d == 0 else 0
                    line(f"dc{d}", nc.scalar.activation(
                        dec[:], inc[:].rearrange("p (c s) -> p c s", s=CHUNK)[:, :, end], ACT.Exp))

        @block.tensor
        def _(pe):
            def both(ps, lhsT, rhs):
                for h in range(2):
                    last = nc.tensor.matmul(ps[:, h * HALF:(h + 1) * HALF], lhsT, rhs[:, h * HALF:(h + 1) * HALF],
                                            start=True, stop=True)
                return last

            with pe.Fori(0, RW_TILES) as c:
                pe.wait_ge(acts, A0.n + A("sq", c))
                both(psC, k.head_ones[:], tmp[2][:]).then_inc(pes, 1)
                pe.wait_ge(lora_loaded, c * 64 + 64)
                for d in range(2):
                    if d == 1:
                        pe.wait_ge(acts, A0.n + A("sa0", c))
                    both(psA, lw_w[d][:], low[0][:, 1:T + 1]).then_inc(pes, 1)
                    both(psB, lw_w[2 + d][:], low[1][:, 1:T + 1]).then_inc(pes, 1)
                pe.wait_ge(dves, V0.n + V("q1", c))
                both(psC, k.head_ones[:], tmp[0][:]).then_inc(pes, 1)


def rwkv_scan(nc, k, ops, vals, end_decay, y, yb=None):
    PAIRS = T // P
    UNITS = RW_TILES * PAIRS
    with ExitStack() as ctx:
        sb = lambda name, shape, dt=F32: ctx.enter_context(nc.sbuf_tensor(name, shape, dt))
        sem = lambda name: ctx.enter_context(nc.semaphore(name))
        dirs, slots = range(2), range(2)
        opt = [[sb(f"opt{s}{d}", [P, 4, P]) for d in dirs] for s in slots]
        byhead = [[sb(f"byhead{s}{d}", [P, 4, P]) for d in dirs] for s in slots]
        vc = [[sb(f"vc{s}{d}", [P, P]) for d in dirs] for s in slots]
        ended = [[sb(f"ended{s}{d}", [P, 2]) for d in dirs] for s in slots]
        r_kept = [sb(f"r_kept{s}", [P, 2, P]) for s in slots]
        end_kept = [sb(f"end_kept{s}", [P, 2, 2]) for s in slots]
        vt = [sb(f"vt{s}", [P, 2, P]) for s in slots]
        bk = [sb(f"bk{s}", [P, 2, 2, 2, P]) for s in slots]
        xa = [sb(f"xa{s}", [P, 2, 2, 2, HEAD]) for s in slots]
        kj = [sb(f"kj{s}", [P, 2, 4, P]) for s in slots]
        bj = [sb(f"bj{s}", [P, 2, 4, P]) for s in slots]
        X5 = [sb(f"X_5{s}", [P, 4, P]) for s in slots]
        yo = [sb(f"yo{s}", [P, 2, P]) for s in slots]
        U = lambda name: sb(name, [P, 4, P])
        E0, X0, X1, X2, X3, X4 = (U(f"X_{n}") for n in "e01234")
        D0, N1, N2, D1, E1, D2, E2, D3, Z1, Z2, T3, T4 = (U(f"N_{n}") for n in range(12))
        ua = sb("ua", [P, 2, 2, 2, HEAD])
        ya = sb("ya", [P, 2, 2, 2, HEAD])
        mt = sb("mt", [P, 2, 2, P])
        rt = [[sb(f"rt{d}{c}", [P, P]) for c in range(2)] for d in dirs]
        st = [[sb(f"st{d}{n}", [P, P]) for n in range(2)] for d in dirs]
        pb = [ctx.enter_context(nc.psum_tensor(f"pb{n}", [P, HALF], F32)) for n in range(8)]
        loaded = [sem(f"unit_loaded{s}") for s in slots]
        slot_free = [sem(f"slot_free{s}") for s in slots]
        y_stored = [sem(f"y_stored{s}") for s in slots]
        yo_free = sem("yo_free")
        yb_zeroed = sem("yb_zeroed")
        zeroed, cleared, passed = sem("zeroed"), sem("cleared"), sem("s_passed")
        kept, x0_made = sem("kept_r"), sem("x0_made")
        front_act, front_dve, front_pe = sem("front_act"), sem("front_dve"), sem("front_pe")
        start_act, start_dve, start_pe = sem("start_act"), sem("start_dve"), sem("start_pe")
        rest_act, rest_dve, rest_pe = sem("rest_act"), sem("rest_dve"), sem("rest_pe")
        SA = Steps("ta0 tv0 b00 b01 ta1 tv1 b10 b11")
        SV = Steps("kj0 kj1 bj0 bj1 e0")
        SP = Steps("tm0 tm1 kj0 kj1 bj0 bj1")
        FA = Steps("d1 e1 d2 e2 d3 z1 t3 z2 t4 xv")
        FV = Steps("d0 n1 n2 x1 x2 x3 x4 x5")
        FP = Steps("dt d1 e1 d2 e2 x1 d3 x2 x3 z1 t3 x4 z2 t4 xv x5")
        RA = Steps("ua0 ua1 ya0 ya1")
        RV = Steps("mt rt00 rt01 rt10 rt11 mid0 mid1 y0 y1 end0 end1")
        RP = Steps("ua mt yr rt mid0 mid1 end0 end1 y0 y1")
        by_unit = lambda ps, d: ps[:, d * 2 * P:(d + 1) * 2 * P].rearrange("p (h k e) -> p h k e", h=2, k=2)
        quad = lambda ps: ps[:].rearrange("p (u n) -> p u n", u=4)
        four = lambda m: m.unsqueeze(1).to_broadcast([P, 4, P])
        block = ctx.enter_context(nc.Block())

        def rounds(eng, start, body):
            start(0, 0)
            body(0, 0, True, False, True)
            with eng.Fori(0, UNITS // 2 - 1) as j:
                body(1, j * 2 + 1, True, True, True)
                body(0, j * 2 + 2, True, True, True)
            body(1, UNITS - 1, True, True, False)
            body(0, UNITS, False, True, False)

        @block.sync
        def _(sp):
            with sp.Fori(0, RW_TILES) as c:
                with sp.Fori(0, PAIRS // 2) as j:
                    for s in slots:
                        chan = sp.snap(c * P)
                        t0 = (sp.snap(j * (2 * P) + s * P), sp.snap(j * (-2 * P) + (PAIRS - 1 - s) * P))
                        ch0 = (sp.snap(j * 4 + s * 2), sp.snap(j * -4 + (PAIRS - 1 - s) * 2))
                        sp.wait_ge(slot_free[s], c * (PAIRS // 2) + j + 1)
                        for d in dirs:
                            tok = bass.ds(t0[d], P)
                            src = row(ops[d], chan, P)[:, :, tok]
                            sp.dma_start(opt[s][d][:], src).then_inc(loaded[s], 16)
                            for h in range(2):
                                rows = slice(h * HEAD, (h + 1) * HEAD)
                                sp.dma_start(byhead[s][d][rows, 2 * h:2 * h + 2, :],
                                             row(ops[d, h * HEAD:], chan, HEAD)[:, 0:2, tok]).then_inc(loaded[s], 16)
                            sp.dma_start(vc[s][d][:], row(vals, chan, P)[:, tok]).then_inc(loaded[s], 16)
                            sp.dma_start(ended[s][d][:],
                                         row(end_decay[d], chan, P)[:, bass.ds(ch0[d], 2)]).then_inc(loaded[s], 16)

        @block.gpsimd
        def _(pool):
            for s in slots:
                for d in dirs:
                    pool.memset(byhead[s][d][:], 0.0)
            for d in dirs:
                for c in range(2):
                    last = pool.memset(rt[d][c][:], 0.0)
            last.then_inc(zeroed, 1)
            pool.wait_ge(zeroed, 1)
            for s in slots:
                pool.sem_inc(slot_free[s], 1)
            pool.sem_inc(yo_free, 2)

            def front(s, i, nth):
                pool.wait_ge(loaded[s], nth * 160 + 160)
                pool.sem_inc(passed, 1)
                for d in dirs:
                    pool.tensor_copy(r_kept[s][:, d, :], opt[s][d][:, 1, :])
                    last = pool.tensor_copy(end_kept[s][:, d, :], ended[s][d][:])
                last.then_inc(kept, 1)
                pool.wait_ge(kept, i + 1)
                pool.wait_ge(start_pe, SP("bj1", i))
                pool.sem_inc(slot_free[s], 1)
                pool.wait_ge(start_dve, SV("e0", i))
                pool.tensor_tensor(X0[:], E0[:], four(k.ident[:]), ALU.add).then_inc(x0_made, 1)

            def store(s, i, c, j, nth):
                pool.wait_ge(rest_dve, RV("end1", i))
                for d in dirs:
                    t0 = j * (2 * P) + s * P if d == 0 else j * (-2 * P) + (PAIRS - 1 - s) * P
                    pool.dma_start(row(y[d], t0, P)[:, bass.ds(c * P, P)], yo[s][:, d, :]).then_inc(y_stored[s], 16)
                pool.wait_ge(y_stored[s], nth * 32 + 32)
                pool.sem_inc(yo_free, 1)

            front(0, 0, 0)
            with pool.Fori(0, RW_TILES - 1) as c:
                with pool.Fori(0, PAIRS // 2) as j:
                    n = c * (PAIRS // 2) + j
                    front(1, n * 2 + 1, n)
                    store(0, n * 2, c, j, n)
                    front(0, n * 2 + 2, n + 1)
                    store(1, n * 2 + 1, c, j, n)
            c, n0 = RW_TILES - 1, (RW_TILES - 1) * (PAIRS // 2)
            with pool.Fori(0, PAIRS // 2 - 1) as j:
                n = j + n0
                front(1, n * 2 + 1, n)
                store(0, n * 2, c, j, n)
                front(0, n * 2 + 2, n + 1)
                store(1, n * 2 + 1, c, j, n)
            j = PAIRS // 2 - 1
            front(1, UNITS - 1, n0 + j)
            store(0, UNITS - 2, c, j, n0 + j)
            store(1, UNITS - 1, c, j, n0 + j)

        @block.scalar
        def _(act):
            if yb is not None:
                act.dma_start(yb.rearrange("(n p) d -> p n d", p=P),
                              k.zeros[:].unsqueeze(1).to_broadcast([P, ROWS // P, D])).then_inc(yb_zeroed, 16)

            def transposes(d, s, i):
                line = Line(act, start_act, SA, i)
                line.at = d * SA.n // 2
                ps = quad(pb[7 - 2 * d])
                act.wait_ge(start_pe, SP(f"tm{d}", i))
                line(f"ta{d}", nc.scalar.copy(xa[s][:, d, :, 1, :], ps[:, 0, :].rearrange("p (h e) -> p h e", h=2)))
                line(f"tv{d}", nc.scalar.copy(vt[s][:, d, :], ps[:, 3, :]))
                for c in range(2):
                    line(f"b{d}{c}", nc.scalar.activation(bk[s][:, d, c, :, :], ps[:, 1:3, :], ACT.Copy,
                                                          scale=k.chunk_col[:, c:c + 1]))

            def start(s, i):
                for d in dirs:
                    transposes(d, s, i)

            def body(s, i, front, rest, more):
                line = Line(act, front_act, FA, i)
                after = Line(act, rest_act, RA, i - 1)

                def copied(name, out, ps):
                    act.wait_ge(front_pe, FP(name, i))
                    line(name, nc.scalar.copy(out[:], quad(ps)))

                if rest:
                    act.wait_ge(rest_pe, RP("ua", i - 1))
                    for d in dirs:
                        after(f"ua{d}", nc.scalar.copy(ua[:, d, :, :, :].rearrange("p k h e -> p h k e"),
                                                       by_unit(pb[6], d)))
                if front:
                    copied("d1", D1, pb[4])
                    copied("e1", E1, pb[2])
                if rest:
                    act.wait_ge(rest_pe, RP("yr", i - 1))
                    for d in dirs:
                        after(f"ya{d}", nc.scalar.copy(ya[:, d, :, :, :].rearrange("p k h e -> p h k e"),
                                                       by_unit(pb[5], d)))
                if front:
                    for name, out, n in (("d2", D2, 0), ("e2", E2, 1), ("d3", D3, 4), ("z1", Z1, 1), ("t3", T3, 3)):
                        copied(name, out, pb[n])
                if more:
                    transposes(0, 1 - s, i + 1)
                if front:
                    copied("z2", Z2, pb[2])
                    copied("t4", T4, pb[0])
                    act.wait_ge(front_pe, FP("xv", i))
                    line("xv", nc.scalar.copy(xa[s][:, :, :, 0, :],
                                              pb[3][:, 0:4 * HEAD].rearrange("p (d h e) -> p d h e", d=2, h=2)))
                if more:
                    transposes(1, 1 - s, i + 1)

            rounds(act, start, body)
            if yb is not None:
                act.wait_ge(yb_zeroed, 16)

        @block.vector
        def _(dve):
            def masked(out, ps, mask):
                return nc.vector.tensor_tensor(out, ps, mask, ALU.mult)

            def chunk_matrix(at, s, i):
                line = Line(dve, start_dve, SV, i)
                line.at = at
                nm, t, n, d = (("kj0", kj, 6, 0), ("kj1", kj, 4, 1), ("bj0", bj, 2, 0), ("bj1", bj, 7, 1))[at]
                dve.wait_ge(start_pe, SP(nm, i))
                line(nm, masked(t[s][:, d, :, :], quad(pb[n]), k.causal[:, d, :, :]))
                if nm == "bj1":
                    e_all = bj[s][:].rearrange("p d (h k) i -> p d h k i", k=2)[:, :, :, 0, :]
                    line("e0", masked(E0[:].rearrange("p (d h) i -> p d h i", d=2), e_all,
                                      k.near[:, 0, :].unsqueeze(1).unsqueeze(1).to_broadcast([P, 2, 2, P])))

            def start(s, i):
                for at in range(4):
                    chunk_matrix(at, s, i)

            def body(s, i, front, rest, more):
                line, r = Line(dve, front_dve, FV, i), 1 - s
                after = Line(dve, rest_dve, RV, i - 1)

                def added(name, out, ps, x):
                    dve.wait_ge(front_pe, FP(name, i))
                    line(name, nc.vector.tensor_tensor(out[:], quad(ps), x[:], ALU.add))

                def moved(name, ps, n):
                    for d in dirs:
                        c = n if d == 0 else 1 - n
                        after(f"{name}{d}", nc.vector.scalar_tensor_tensor(
                            out=st[d][1 - n][:], in0=ps[:, d * P:(d + 1) * P], scalar=end_kept[r][:, d, c:c + 1],
                            in1=k.head_ones[:], op0=ALU.mult, op1=ALU.mult))

                if front:
                    dve.wait_ge(front_pe, FP("dt", i))
                    for n, (nm, out) in enumerate((("d0", D0), ("n1", N1), ("n2", N2))):
                        line(nm, masked(out[:], quad(pb[3]), four(k.near[:, n, :])))
                if rest:
                    dve.wait_ge(rest_pe, RP("mt", i - 1))
                    after("mt", masked(mt[:].rearrange("p d c n -> p (d c) n"), quad(pb[7]), four(k.head_ones[:])))
                if front:
                    dve.wait_ge(x0_made, i + 1)
                    added("x1", X1, pb[3], X0)
                if rest:
                    dve.wait_ge(rest_pe, RP("rt", i - 1))
                    dve.wait_ge(kept, i)
                    for d in dirs:
                        for c in range(2):
                            cols = slice(c * CHUNK, (c + 1) * CHUNK)
                            after(f"rt{d}{c}", nc.vector.tensor_tensor(
                                rt[d][c][:, cols], pb[6][:, d * P + c * CHUNK:d * P + (c + 1) * CHUNK],
                                r_kept[r][:, d, cols], ALU.add))
                if front:
                    added("x2", X2, pb[2], X1)
                if rest:
                    dve.wait_ge(rest_pe, RP("mid1", i - 1))
                    moved("mid", pb[7], 0)
                if front:
                    added("x3", X3, pb[0], X2)
                if rest:
                    dve.wait_ge(rest_pe, RP("y1", i - 1))
                    dve.wait_ge(rest_act, RA("ya1", i - 1))
                    dve.wait_ge(yo_free, i)
                    for d in dirs:
                        after(f"y{d}", nc.vector.tensor_tensor(
                            yo[r][:, d, :], pb[6][:, d * P:(d + 1) * P],
                            ya[:, d, 0, :, :].rearrange("p h e -> p (h e)"), ALU.add))
                    moved("end", pb[5], 1)
                if front:
                    added("x4", X4, pb[4], X3)
                if more:
                    chunk_matrix(0, 1 - s, i + 1)
                if front:
                    added("x5", X5[s], pb[1], X4)
                if more:
                    for at in (1, 2, 3):
                        chunk_matrix(at, 1 - s, i + 1)

            for d in dirs:
                nc.vector.memset(st[d][0][:], 0.0).then_inc(cleared, 1)
            rounds(dve, start, body)

        @block.tensor
        def _(pe):
            mm = lambda out, lhsT, rhs, start=True, stop=True: nc.tensor.matmul(
                out, lhsT, rhs, start=start, stop=stop)
            flat = lambda t: t.rearrange("p h e -> p (h e)")
            of = lambda t: (lambda u: t[:, u, :])

            def each(ps, lhsT, rhs, width=P):
                for u in range(4):
                    last = mm(pb[ps][:, u * width:(u + 1) * width], lhsT(u), rhs(u))
                return last

            def turned(ps, src):
                for u in range(4):
                    last = nc.tensor.transpose(pb[ps][:, u * P:(u + 1) * P], src(u), k.ident[:])
                return last

            sp = lambda instruction: instruction.then_inc(start_pe, 1)

            def transposes(d, s):
                for n, src in enumerate((opt[s][d][:, 0, :], opt[s][d][:, 2, :], opt[s][d][:, 3, :], vc[s][d][:])):
                    last = nc.tensor.transpose(pb[7 - 2 * d][:, n * P:(n + 1) * P], src, k.ident[:])
                sp(last)

            def chunk_matrix(at, s):
                ps, n, d = ((6, 3, 0), (4, 3, 1), (2, 2, 0), (7, 2, 1))[at]
                sp(mm(pb[ps][:], opt[s][d][:, n, :], byhead[s][d][:].rearrange("p m i -> p (m i)")))

            def body(s, i, front, rest, more):
                r = 1 - s
                fa = lambda name: pe.wait_ge(front_act, FA(name, i))
                fv = lambda name: pe.wait_ge(front_dve, FV(name, i))
                ra = lambda name: pe.wait_ge(rest_act, RA(name, i - 1))
                rv = lambda name: pe.wait_ge(rest_dve, RV(name, i - 1))
                fp = lambda instruction: instruction.then_inc(front_pe, 1)
                rp = lambda instruction: instruction.then_inc(rest_pe, 1)

                def state(ps, n):
                    for d in dirs:
                        c = n if d == 0 else 1 - n
                        out = pb[ps][:, d * P:(d + 1) * P]
                        mm(out, bk[r][:, d, c, 0, :], flat(ua[:, d, 0, :, :]), True, False)
                        mm(out, bk[r][:, d, c, 1, :], vt[r][:, d, :], False, False)
                        mm(out, k.ident[:], st[d][n][:], False, False)
                        rp(mm(out, mt[:, d, c, :], st[d][n][:], False, True))

                if rest:
                    pe.wait_ge(front_act, FA("xv", i - 1))
                    pe.wait_ge(front_dve, FV("x5", i - 1))
                    if front:
                        pe.wait_ge(start_dve, SV("kj0", i))
                    rp(each(6, of(X5[r]), lambda u: xa[r][:, u // 2, u % 2, :, :].rearrange("p k e -> p (k e)")))
                if front:
                    pe.wait_ge(start_dve, SV("bj1", i))
                    if not rest:
                        pe.wait_ge(start_act, SA("b11", i))
                    fp(turned(3, lambda u: bj[s][:, u // 2, 2 * (u % 2), :]))
                if rest:
                    ra("ua1")
                    if front:
                        pe.wait_ge(start_act, SA("b11", i))
                    for d in dirs:
                        last = mm(pb[7][:, d * 2 * P:(d + 1) * 2 * P], flat(ua[:, d, 1, :, :]), bk[r][:, d, :, 0, :])
                    rp(last)
                    for u in range(4):
                        d, h = u // 2, u % 2
                        mm(pb[5][:, u * P:(u + 1) * P], bj[r][:, d, 2 * h + 1, :], ua[:, d, :, h, :], True, False)
                        last = mm(pb[5][:, u * P:u * P + HEAD], kj[r][:, d, 2 * h + 1, :],
                                  vt[r][:, d, h * HEAD:(h + 1) * HEAD], False, True)
                    rp(last)
                if front:
                    fv("d0")
                    pe.wait_ge(start_dve, SV("e0", i))
                    fp(each(4, of(E0), of(D0)))
                    fp(each(2, of(D0), of(E0)))
                if rest:
                    ra("ya1")
                    for d in dirs:
                        last = nc.tensor.transpose(pb[6][:, d * P:(d + 1) * P], flat(ya[:, d, 1, :, :]), k.ident[:])
                    rp(last)
                if front:
                    fa("e1")
                    fv("n2")
                    pe.wait_ge(x0_made, i + 1)
                    fp(each(0, of(E1), of(D1)))
                    fp(each(1, of(D1), of(E1)))
                    fp(each(3, of(D1), of(X0)))
                if rest:
                    rv("mt")
                    if not front:
                        rv("rt11")
                    state(7, 0)
                if front:
                    fa("e2")
                    fp(each(4, of(E2), of(D2)))
                    fv("x1")
                    fp(each(2, of(D2), of(X1)))
                if rest:
                    rv("mid1")
                    state(5, 1)
                if front:
                    fa("d3")
                    fv("x2")
                    fp(each(0, of(D3), of(X2)))
                if rest:
                    for d in dirs:
                        out = pb[6][:, d * P:(d + 1) * P]
                        mm(out, rt[d][d][:], st[d][0][:], True, False)
                        rp(mm(out, rt[d][1 - d][:], st[d][1][:], False, True))
                if front:
                    fv("x3")
                    fp(each(1, of(N1), of(X3)))
                    fp(turned(3, of(X3)))
                if more:
                    pe.wait_ge(loaded[1 - s], nth(1 - s, i + 1) * 160 + 160)
                    transposes(0, 1 - s)
                if front:
                    fa("t3")
                    fp(each(4, of(T3), of(Z1)))
                if more:
                    if rest:
                        rv("end1")
                    transposes(1, 1 - s)
                if front:
                    fv("x4")
                    fp(each(2, of(N2), of(X4)))
                    fp(turned(0, of(X4)))
                    fp(each(3, lambda u: kj[s][:, u // 2, 2 * (u % 2), :],
                            lambda u: vt[s][:, u // 2, (u % 2) * HEAD:(u % 2 + 1) * HEAD], HEAD))
                if more:
                    chunk_matrix(0, 1 - s)
                if front:
                    fa("t4")
                    fp(each(1, of(T4), of(Z2)))
                if more:
                    chunk_matrix(1, 1 - s)
                    chunk_matrix(2, 1 - s)
                    pe.wait_ge(start_act, SA("b01", i + 1))
                    chunk_matrix(3, 1 - s)

            def start(s, i):
                pe.wait_ge(loaded[s], 160)
                for d in dirs:
                    transposes(d, s)
                for at in range(3):
                    chunk_matrix(at, s)
                pe.wait_ge(start_act, SA("b01", i))
                chunk_matrix(3, s)

            pe.wait_ge(zeroed, 1)
            pe.wait_ge(cleared, 2)
            start(0, 0)
            nth = lambda s, i: 0
            body(0, 0, True, False, True)
            with pe.Fori(0, UNITS // 2 - 1) as j:
                nth = lambda s, i: j + 1
                body(1, j * 2 + 1, True, True, True)
                body(0, j * 2 + 2, True, True, True)
            body(1, UNITS - 1, True, True, False)
            body(0, UNITS, False, True, False)


E_DA = C_DA // DA_HEADS
QK = E_DA // 2


def differential_attention(nc, k, zT, q_gain, k_gain, lq1, lk1, lq2, lk2, sub_gain, oT):
    QT = NT
    with ExitStack() as ctx:
        sb = lambda name, shape, dt=F32: ctx.enter_context(nc.sbuf_tensor(name, shape, dt))
        sem = lambda name: ctx.enter_context(nc.semaphore(name))
        maps = range(2)
        zq, zk, zv = (sb(f"a{n}", [P, T]) for n in ("zq", "zk", "zv"))
        sq = sb("asq", [P, T])
        inv = sb("ainv", [P, T])
        qm = [sb(f"qm{m}", [P, T]) for m in maps]
        kn = sb("kn", [P, T])
        vt = sb("avt", [P, NT, E_DA])
        gains = sb("gains", [P, 3])
        lam_in = sb("lam_in", [P, 4, QK])
        lam = sb("lam", [P, 8])
        far = sb("far", [P, 2 * T - P], I32)
        dist = sb("dist", [P, 2 * T - P])
        slope = sb("slope", [P, 2 * T - P])
        sc = [sb(f"sc{m}", [P, T]) for m in maps]
        pr = [sb(f"pr{m}", [P, T]) for m in maps]
        at = sb("at", [P, T])
        aT = [sb(f"aT{s}", [P, NT, P]) for s in range(2)]
        stats = sb("astats", [P, QT, 11])
        col = lambda t, i, n=1: stats[:, t, i:i + n]
        MAX, NEG, SUM, INV, FACTOR, ROOT, SCALE = 0, 2, 4, 6, 8, 9, 10
        carrier = sb("carrier", [P, 1])
        o_sb = sb("o_sb", [P, E_DA])
        o_sq = sb("o_sq", [P, E_DA])
        oc = sb("oc", [P, T])
        ps = [ctx.enter_context(nc.psum_tensor(f"sp{m}", [P, T], F32)) for m in maps]
        tp = ctx.enter_context(nc.psum_tensor("atp", [P, T], F32))
        op = ctx.enter_context(nc.psum_tensor("aop", [P, HALF], F32))
        ot = ctx.enter_context(nc.psum_tensor("aot", [P, HALF], F32))
        par, zl, made = sem("apar"), sem("azl"), sem("amade")
        acts, dves, pes, kept = sem("a_acts"), sem("a_dves"), sem("a_pes"), sem("a_kept")
        A0 = Steps("e0 e1 gq")
        V0 = Steps("p0 p1 fcopy fneg dist lamd lamn")
        ROUNDS = QT + 3

        def names(*parts):
            return " ".join(f"{n}_{i - back}" for i in range(ROUNDS) for back, text in parts
                            if 0 <= i - back < QT for n in text.split())

        A = Steps("slope sqq rq sqk rk v0 v1 " + names((3, "osq ort"), (0, "ex0 ex1"), (1, "at0 at1"), (3, "oT")))
        V = Steps("iq q0 q1 ik kn " + names((3, "oc"), (1, "rs f a1"), (3, "orc on"), (0, "s0 n0 s1 n1")))
        M = Steps("nq nk v " + names((0, "s0 s1"), (1, "at"), (3, "oT"), (2, "o")))
        block = ctx.enter_context(nc.Block())

        @block.sync
        def _(sp):
            with nc.allow_non_contiguous_dma(reason="gains as columns"):
                for m in maps:
                    rows = slice(m * QK, (m + 1) * QK)
                    sp.dma_start(gains[rows, 0:1], q_gain.rearrange("(p o) -> p o", o=1)).then_inc(par, 16)
                    sp.dma_start(gains[rows, 1:2], k_gain.rearrange("(p o) -> p o", o=1)).then_inc(par, 16)
                sp.dma_start(gains[:, 2:3], sub_gain.rearrange("(p o) -> p o", o=1)).then_inc(par, 16)
            for i, v in enumerate((lq1, lk1, lq2, lk2)):
                sp.dma_start(lam_in[:, i, :], v.rearrange("(o n) -> o n", o=1).to_broadcast([P, QK])).then_inc(par, 16)
            with sp.Fori(0, DA_HEADS) as h:
                first = sp.snap(h * P)
                sp.wait_ge(kept, h * 16)
                for i, t in enumerate((zq, zk, zv)):
                    base = RW_COLS + i * C_DA
                    sp.dma_start(t[:], row(zT[base:base + C_DA], first, P)).then_inc(zl, 16)

        @block.gpsimd
        def _(pool):
            pool.memset(qm[0][:], 0.0)
            pool.memset(qm[1][:], 0.0)
            pool.iota(far[:], [[1, 2 * T - P]], base=-(T - P), channel_multiplier=-1).then_inc(made, 1)
            with pool.Fori(0, DA_HEADS) as h:
                pool.wait_ge(acts, A0.n + A(f"oT_{QT - 1}", h))
                pool.dma_start(row(oT, h * P + C_RW, P), oc[:]).then_inc(kept, 16)
            pool.wait_ge(kept, 16 * DA_HEADS)

        @block.vector
        def _(dve):
            line = Line(dve, dves, V0)
            dve.wait_ge(par, 16 * 9)
            for m in maps:
                line(f"p{m}", nc.vector.tensor_tensor_reduce(
                    lam_in[:, 2 * m, :], lam_in[:, 2 * m, :], lam_in[:, 2 * m + 1, :], 1.0, 0.0,
                    ALU.mult, ALU.add, lam[:, m:m + 1]))
            dve.wait_ge(made, 1)
            line("fcopy", nc.vector.tensor_copy(dist[:], far[:]))
            line("fneg", nc.vector.tensor_scalar(slope[:], dist[:], -1.0, None, ALU.mult))
            line("dist", nc.vector.tensor_tensor(dist[:], dist[:], slope[:], ALU.min))
            dve.wait_ge(acts, A0("e1"))
            line("lamd", nc.vector.tensor_tensor(lam[:, 4:5], lam[:, 3:4], lam[:, 2:3], ALU.subtract))
            line("lamn", nc.vector.tensor_scalar(lam[:, 5:6], lam[:, 4:5], -LAMBDA_INIT, None, ALU.add))
            with dve.Fori(0, DA_HEADS) as h:
                line = Line(dve, dves, V, h, V0.n)
                dve.wait_ge(acts, A0.n + A("rq", h))
                line("iq", nc.vector.reciprocal(inv[:], inv[:]))
                for m in maps:
                    rows = slice(m * QK, (m + 1) * QK)
                    line(f"q{m}", nc.vector.scalar_tensor_tensor(
                        out=qm[m][rows, :], in0=zq[rows, :], scalar=gains[rows, 0:1], in1=inv[rows, :],
                        op0=ALU.mult, op1=ALU.mult))
                dve.wait_ge(acts, A0.n + A("rk", h))
                line("ik", nc.vector.reciprocal(sq[:], sq[:]))
                line("kn", nc.vector.scalar_tensor_tensor(out=kn[:], in0=zk[:], scalar=gains[:, 1:2], in1=sq[:],
                                                          op0=ALU.mult, op1=ALU.mult))
                dve.wait_ge(acts, A0.n + A("v1", h))
                for i in range(ROUNDS):
                    t = i - 3
                    if 0 <= t:
                        dve.wait_ge(pes, M(f"o_{t}", h))
                        line(f"oc_{t}", nc.vector.tensor_scalar(o_sb[:], op[:, 0:E_DA], col(t, INV), None, ALU.mult))
                    t = i - 1
                    if 0 <= t < QT:
                        dve.wait_ge(acts, A0.n + A(f"ex1_{t}", h))
                        if t:
                            dve.wait_ge(pes, M(f"at_{t - 1}", h))
                        line(f"rs_{t}", nc.vector.reciprocal(col(t, INV, 2), col(t, SUM, 2)))
                        line(f"f_{t}", nc.vector.tensor_scalar(col(t, FACTOR), col(t, INV + 1), lam[:, 5:6],
                                                               col(t, SUM), ALU.mult, ALU.mult))
                        line(f"a1_{t}", nc.vector.scalar_tensor_tensor(out=at[:], in0=pr[1][:], scalar=col(t, FACTOR),
                                                                       in1=pr[0][:], op0=ALU.mult, op1=ALU.add))
                    t = i - 3
                    if 0 <= t:
                        dve.wait_ge(acts, A0.n + A(f"ort_{t}", h))
                        line(f"orc_{t}", nc.vector.reciprocal(col(t, SCALE), col(t, ROOT)))
                        line(f"on_{t}", nc.vector.tensor_scalar(o_sb[:], o_sb[:], col(t, SCALE), 1.0 - LAMBDA_INIT,
                                                                ALU.mult, ALU.mult))
                    t = i
                    if t < QT:
                        at0 = (T - P) - t * P
                        for m in maps:
                            dve.wait_ge(pes, M(f"s{m}_{t}", h))
                            nc.vector.memset(carrier[:], 0.0)
                            line(f"s{m}_{t}", nc.vector.tensor_tensor_reduce(
                                sc[m][:], ps[m][:], dist[:, at0:at0 + T], 1.0, -3.0e38, ALU.add, ALU.max,
                                col(t, MAX + m)))
                            line(f"n{m}_{t}", nc.vector.tensor_scalar(col(t, NEG + m), col(t, MAX + m), -1.0, None,
                                                                      ALU.mult))

        @block.scalar
        def _(act):
            line = Line(act, acts, A0)
            act.wait_ge(dves, V0("p1"))
            for m in maps:
                line(f"e{m}", nc.scalar.activation(lam[:, 2 + m:3 + m], lam[:, m:m + 1], ACT.Exp))
            line("gq", nc.scalar.mul(gains[:, 0:1], gains[:, 0:1], QK ** -0.5))
            with act.Fori(0, DA_HEADS) as h:
                line = Line(act, acts, A, h, A0.n)
                vdone = lambda name: V0.n + V(name, h)
                act.wait_ge(dves, V0.n + h * V.n)
                line("slope", nc.scalar.mul(dist[:], dist[:], 0.25))
                act.wait_ge(zl, h * 48 + 48)
                line("sqq", nc.scalar.activation(sq[:], zq[:], ACT.Square))
                act.wait_ge(pes, M("nq", h))
                line("rq", nc.scalar.activation(inv[:], ps[0][:], ACT.Sqrt, bias=k.eps[:, 0:1], scale=1.0 / QK))
                line("sqk", nc.scalar.activation(at[:], zk[:], ACT.Square))
                act.wait_ge(pes, M("nk", h))
                line("rk", nc.scalar.activation(sq[:], ps[1][:], ACT.Sqrt, bias=k.eps[:, 0:1], scale=1.0 / QK))
                act.wait_ge(pes, M("v", h))
                for n in range(2):
                    line(f"v{n}", nc.scalar.copy(vt[:].rearrange("p n e -> p (n e)")[:, n * HALF:(n + 1) * HALF],
                                                 tp[:, n * HALF:(n + 1) * HALF]))
                for i in range(ROUNDS):
                    t = i - 3
                    if 0 <= t:
                        act.wait_ge(dves, vdone(f"oc_{t}"))
                        line(f"osq_{t}", nc.scalar.activation(o_sq[:], o_sb[:], ACT.Square, accum_out=col(t, ROOT)))
                        line(f"ort_{t}", nc.scalar.activation(col(t, ROOT), col(t, ROOT), ACT.Sqrt,
                                                              bias=k.eps[:, 0:1], scale=1.0 / E_DA))
                    t = i
                    if t < QT:
                        for m in maps:
                            act.wait_ge(dves, vdone(f"n{m}_{t}"))
                            line(f"ex{m}_{t}", nc.scalar.activation(pr[m][:], sc[m][:], ACT.Exp, bias=col(t, NEG + m),
                                                                    accum_out=col(t, SUM + m)))
                    t = i - 1
                    if 0 <= t < QT:
                        act.wait_ge(pes, M(f"at_{t}", h))
                        for n in range(2):
                            line(f"at{n}_{t}", nc.scalar.copy(
                                aT[t % 2][:].rearrange("p n e -> p (n e)")[:, n * HALF:(n + 1) * HALF],
                                tp[:, n * HALF:(n + 1) * HALF]))
                    t = i - 3
                    if 0 <= t:
                        act.wait_ge(pes, M(f"oT_{t}", h))
                        act.wait_ge(kept, h * 16)
                        line(f"oT_{t}", nc.scalar.mul(oc[:, t * P:(t + 1) * P], ot[:, 0:P], gains[:, 2:3]))

        @block.tensor
        def _(pe):
            with pe.Fori(0, DA_HEADS) as h:
                adone = lambda name: A0.n + A(name, h)
                vdone = lambda name: V0.n + V(name, h)

                def both(out, lhsT, rhs):
                    for n in range(2):
                        last = nc.tensor.matmul(out[:, n * HALF:(n + 1) * HALF], lhsT,
                                                rhs[:, n * HALF:(n + 1) * HALF], start=True, stop=True)
                    last.then_inc(pes, 1)

                pe.wait_ge(acts, adone("sqq"))
                both(ps[0], k.head_ones[:], sq)
                pe.wait_ge(acts, adone("sqk"))
                both(ps[1], k.head_ones[:], at)
                for n in range(NT):
                    last = nc.tensor.transpose(tp[:, n * P:(n + 1) * P], zv[:, n * P:(n + 1) * P], k.ident[:])
                last.then_inc(pes, 1)
                pe.wait_ge(dves, vdone("kn"))
                for i in range(ROUNDS):
                    t = i
                    if t < QT:
                        for m in maps:
                            if t:
                                pe.wait_ge(dves, vdone(f"s{m}_{t - 1}"))
                            both(ps[m], qm[m][:, t * P:(t + 1) * P], kn)
                    t = i - 1
                    if 0 <= t < QT:
                        if t:
                            pe.wait_ge(acts, adone(f"at1_{t - 1}"))
                        pe.wait_ge(dves, vdone(f"a1_{t}"))
                        for n in range(NT):
                            last = nc.tensor.transpose(tp[:, n * P:(n + 1) * P], at[:, n * P:(n + 1) * P], k.ident[:])
                        last.then_inc(pes, 1)
                    t = i - 3
                    if 0 <= t:
                        if t:
                            pe.wait_ge(acts, adone(f"oT_{t - 1}"))
                        pe.wait_ge(dves, vdone(f"on_{t}"))
                        nc.tensor.transpose(ot[:, 0:P], o_sb[:], k.ident[:]).then_inc(pes, 1)
                    t = i - 2
                    if 0 <= t < QT:
                        pe.wait_ge(acts, adone(f"at1_{t}"))
                        for n in range(NT):
                            last = nc.tensor.matmul(op[:, 0:E_DA], aT[t % 2][:, n, :], vt[:, n, :],
                                                    start=(n == 0), stop=(n == NT - 1))
                        last.then_inc(pes, 1)


def finish_rwkv(nc, k, y, bonus, gate_in, g2, ln_g, ln_b, oT):
    with ExitStack() as ctx:
        sb = lambda name, shape, dt=F32: ctx.enter_context(nc.sbuf_tensor(name, shape, dt))
        sem = lambda name: ctx.enter_context(nc.semaphore(name))
        slots = range(2)
        yf = [sb(f"yf{s}", [P, NT, P]) for s in slots]
        yb = [sb(f"yb{s}", [P, NT, P]) for s in slots]
        yc = sb("ycent", [P, NT, P])
        bv = [sb(f"bvt{s}", [P, T]) for s in slots]
        g2s = sb("g2s", [P, C_RW])
        gin = sb("gins", [P, T])
        gains = sb("lngains", [P, 2, RW_TILES])
        stat = sb("gnstat", [P, 3, NT * 2])
        oc = [sb(f"orw{s}", [P, T]) for s in slots]
        tp = [ctx.enter_context(nc.psum_tensor(f"gtp{s}", [P, T], F32)) for s in slots]
        gp = [ctx.enter_context(nc.psum_tensor(f"ggp{s}", [P, T], F32)) for s in slots]
        once, y_loaded = sem("once"), [sem(f"y_in{s}") for s in slots]
        o_stored = [sem(f"o_out{s}") for s in slots]
        acts, dves, pes = sem("g_acts"), sem("g_dves"), sem("g_pes")
        A = Steps("root0 root1")
        V = Steps(" ".join(f"sum{s} mean{s} meand{s} cent{s} sq{s} var{s} inv{s} norm{s} aff{s} bon{s} gate{s}" for s in slots))
        M = Steps("gate0 turn0 gate1 turn1")
        LOOPS = RW_TILES // 2
        block = ctx.enter_context(nc.Block())

        @block.sync
        def _(sp):
            with nc.allow_non_contiguous_dma(reason="gains as columns"):
                sp.dma_start(gains[:, 0, :], ln_g.rearrange("(n p) -> p n", p=P)).then_inc(once, 16)
                sp.dma_start(gains[:, 1, :], ln_b.rearrange("(n p) -> p n", p=P)).then_inc(once, 16)
            sp.dma_start(g2s[:], g2).then_inc(once, 16)
            sp.dma_start(gin[:], gate_in).then_inc(once, 16)
            for c in range(RW_TILES):
                s = c % 2
                if c >= 2:
                    sp.wait_ge(dves, V(f"gate{s}", c // 2 - 1))
                chan = slice(c * P, (c + 1) * P)
                for d, t in ((0, yf), (1, yb)):
                    sp.dma_start(t[s][:], y[d][:, chan].rearrange("(n p) c -> p n c", p=P)).then_inc(y_loaded[s], 16)
                sp.dma_start(bv[s][:], bonus[chan, :]).then_inc(y_loaded[s], 16)

        @block.gpsimd
        def _(pool):
            for c in range(RW_TILES):
                s = c % 2
                pool.wait_ge(dves, V(f"gate{s}", c // 2))
                pool.dma_start(oT[c * P:(c + 1) * P, :], oc[s][:]).then_inc(o_stored[s], 16)
            for s in slots:
                pool.wait_ge(o_stored[s], 16 * LOOPS)

        @block.scalar
        def _(act):
            with act.Fori(0, LOOPS) as j:
                line = Line(act, acts, A, j)
                for s in slots:
                    act.wait_ge(dves, V(f"var{s}", j))
                    line(f"root{s}", nc.scalar.activation(stat[:, 2, :], stat[:, 1, :], ACT.Sqrt,
                                                          bias=k.eps[:, 2:3], scale=1.0 / HEAD))

        @block.vector
        def _(dve):
            dve.wait_ge(once, 64)
            with dve.Fori(0, LOOPS) as j:
                line = Line(dve, dves, V, j)
                for s in slots:
                    heads = lambda t: t[:].rearrange("p n (h e) -> p (n h) e", e=HEAD)
                    wide = lambda i: stat[:, i, :].unsqueeze(2).to_broadcast([P, NT * 2, HEAD])
                    col = lambda i: gains[:, i, bass.ds(j * 2 + s, 1)]
                    flat = lambda t: t[:].rearrange("p n c -> p (n c)")
                    dve.wait_ge(y_loaded[s], j * 48 + 48)
                    line(f"sum{s}", nc.vector.tensor_tensor(flat(yf[s]), flat(yf[s]), flat(yb[s]), ALU.add))
                    line(f"mean{s}", nc.vector.tensor_reduce(stat[:, 0, :], heads(yf[s]), AX.X, ALU.add))
                    line(f"meand{s}", nc.vector.tensor_scalar(stat[:, 0, :], stat[:, 0, :], 1.0 / HEAD, None, ALU.mult))
                    line(f"cent{s}", nc.vector.tensor_tensor(heads(yc), heads(yf[s]), wide(0), ALU.subtract))
                    line(f"sq{s}", nc.vector.tensor_tensor(flat(yb[s]), flat(yc), flat(yc), ALU.mult))
                    line(f"var{s}", nc.vector.tensor_reduce(stat[:, 1, :], heads(yb[s]), AX.X, ALU.add))
                    dve.wait_ge(acts, A(f"root{s}", j))
                    line(f"inv{s}", nc.vector.reciprocal(stat[:, 2, :], stat[:, 2, :]))
                    line(f"norm{s}", nc.vector.tensor_tensor(heads(yf[s]), heads(yc), wide(2), ALU.mult))
                    dve.wait_ge(pes, M(f"turn{s}", j))
                    dve.wait_ge(o_stored[s], j * 16)
                    line(f"aff{s}", nc.vector.tensor_scalar(oc[s][:], tp[s][:], col(0), col(1), ALU.mult, ALU.add))
                    line(f"bon{s}", nc.vector.tensor_tensor(oc[s][:], oc[s][:], bv[s][:], ALU.add))
                    line(f"gate{s}", nc.vector.tensor_tensor(oc[s][:], oc[s][:], gp[s][:], ALU.mult))

        @block.tensor
        def _(pe):
            pe.wait_ge(once, 64)
            for c in range(RW_TILES):
                s, j = c % 2, c // 2
                if j:
                    pe.wait_ge(dves, V(f"gate{s}", j - 1))
                for h in range(2):
                    last = nc.tensor.matmul(gp[s][:, h * HALF:(h + 1) * HALF], g2s[:, c * P:(c + 1) * P],
                                            gin[:, h * HALF:(h + 1) * HALF], start=True, stop=True)
                last.then_inc(pes, 1)
                pe.wait_ge(dves, V(f"norm{s}", j))
                for n in range(NT):
                    last = nc.tensor.transpose(tp[s][:, n * P:(n + 1) * P], yf[s][:, n, :], k.ident[:])
                last.then_inc(pes, 1)


def mix_out_and_route(nc, k, x, oT, w_out, ffn_gain, w_router, b_router, h1, m, chosen, gates):
    with ExitStack() as ctx:
        sb = lambda name, shape, dt=F32: ctx.enter_context(nc.sbuf_tensor(name, shape, dt))
        sem = lambda name: ctx.enter_context(nc.semaphore(name))
        slots = range(2)
        wo = sb("wo", [P, ND, D])
        wr = sb("wr", [P, ND, EXPERTS])
        br = sb("br", [P, EXPERTS])
        gb = sb("gb", [P, D])
        expert = sb("expert", [P, EXPERTS], I32)
        expertf = sb("expertf", [P, EXPERTS])
        ot = [sb(f"ot{s}", [P, ND, P]) for s in slots]
        xt = [sb(f"xin{s}", [P, D]) for s in slots]
        ht = [sb(f"ht{s}", [P, D]) for s in slots]
        mt = [sb(f"mtok{s}", [P, D]) for s in slots]
        mT = [sb(f"mT{s}", [P, ND, P]) for s in slots]
        carrier = sb("rcarrier", [P, 1])
        sq = sb("hsq", [P, D])
        st = [sb(f"hst{s}", [P, 2]) for s in slots]
        lg = [sb(f"lg{s}", [P, EXPERTS]) for s in slots]
        top = [sb(f"top{s}", [P, 8]) for s in slots]
        ix = [sb(f"ix{s}", [P, 8], U32) for s in slots]
        ixf = [sb(f"ixf{s}", [P, 8]) for s in slots]
        gt = [sb(f"gt{s}", [P, 4]) for s in slots]
        hp = [ctx.enter_context(nc.psum_tensor(f"hp{s}", [P, D], F32)) for s in slots]
        tp = ctx.enter_context(nc.psum_tensor("mtp", [P, D], F32))
        lp = [ctx.enter_context(nc.psum_tensor(f"lp{s}", [P, HALF], F32)) for s in slots]
        once, made = sem("r_once"), sem("r_made")
        loaded = [sem(f"r_loaded{s}") for s in slots]
        stored = [sem(f"r_stored{s}") for s in slots]
        acts, dves, pes = sem("r_acts"), sem("r_dves"), sem("r_pes")
        V0 = Steps("expertf")
        A = Steps(" ".join(f"sq{s} root{s} mTa{s} mTb{s} exp{s}" for s in slots))
        V = Steps(" ".join(f"h{s} inv{s} m{s} logit{s} max{s} idx{s} idf{s} neg{s} hot0{s} hot1{s} hot2{s} hot3{s} "
                           f"inve{s} gate{s}" for s in slots))
        M = Steps(" ".join(f"h{s} turn{s} logit{s}" for s in slots))
        LOOPS = NT // 2
        block = ctx.enter_context(nc.Block())
        oT_v = oT.rearrange("(n p) t -> p n t", p=P)

        @block.sync
        def _(sp):
            sp.dma_start(wr[:], w_router.rearrange("(n p) e -> p n e", p=P)).then_inc(once, 16)
            sp.dma_start(br[:], b_router.rearrange("(o e) -> o e", o=1).to_broadcast([P, EXPERTS])).then_inc(once, 16)
            sp.dma_start(gb[:], ffn_gain.rearrange("(o e) -> o e", o=1).to_broadcast([P, D])).then_inc(once, 16)
            sp.dma_start(wo[:], w_out.rearrange("(n p) e -> p n e", p=P)).then_inc(once, 16)
            with sp.Fori(0, LOOPS) as j:
                for s in slots:
                    first = sp.snap(j * 2 * P + s * P)
                    sp.wait_ge(stored[s], j * 32)
                    sp.dma_start(ot[s][:], oT_v[:, :, bass.ds(first, P)]).then_inc(loaded[s], 16)
                    sp.dma_start(xt[s][:], row(x, first, P)).then_inc(loaded[s], 16)

        @block.gpsimd
        def _(pool):
            pool.iota(expert[:], [[1, EXPERTS]], base=0, channel_multiplier=0).then_inc(made, 1)
            with pool.Fori(0, LOOPS) as j:
                for s in slots:
                    first = j * 2 * P + s * P
                    pool.wait_ge(dves, V0.n + V(f"m{s}", j))
                    pool.dma_start(row(h1, first, P), ht[s][:]).then_inc(stored[s], 16)
                    pool.dma_start(row(m, first, P), mt[s][:]).then_inc(stored[s], 16)
            for s in slots:
                pool.wait_ge(stored[s], 32 * LOOPS)

        @block.scalar
        def _(act):
            with act.Fori(0, LOOPS) as j:
                line = Line(act, acts, A, j)
                vdone = lambda name: V0.n + V(name, j)
                for s in slots:
                    act.wait_ge(dves, vdone(f"h{s}"))
                    line(f"sq{s}", nc.scalar.activation(sq[:], ht[s][:], ACT.Square, accum_out=st[s][:, 0:1]))
                    line(f"root{s}", nc.scalar.activation(st[s][:, 1:2], st[s][:, 0:1], ACT.Sqrt,
                                                          bias=k.eps[:, 0:1], scale=1.0 / D))
                    act.wait_ge(pes, M(f"turn{s}", j))
                    for n in range(2):
                        line(f"mT{'ab'[n]}{s}", nc.scalar.copy(
                            mT[s][:].rearrange("p n t -> p (n t)")[:, n * HALF:(n + 1) * HALF],
                            tp[:, n * HALF:(n + 1) * HALF]))
                    act.wait_ge(dves, vdone(f"neg{s}"))
                    line(f"exp{s}", nc.scalar.activation(gt[s][:], top[s][:, 0:4], ACT.Exp, bias=ixf[s][:, 7:8],
                                                         accum_out=ixf[s][:, 6:7]))

        @block.vector
        def _(dve):
            line = Line(dve, dves, V0)
            dve.wait_ge(made, 1)
            line("expertf", nc.vector.tensor_copy(expertf[:], expert[:]))
            dve.wait_ge(once, 64)
            with dve.Fori(0, LOOPS) as j:
                line = Line(dve, dves, V, j, V0.n)
                for s in slots:
                    tile = bass.ds(j * 2 + s, 1)
                    dve.wait_ge(pes, M(f"h{s}", j))
                    dve.wait_ge(loaded[s], j * 32 + 32)
                    line(f"h{s}", nc.vector.tensor_tensor(ht[s][:], hp[s][:], xt[s][:], ALU.add))
                    dve.wait_ge(acts, A(f"root{s}", j))
                    line(f"inv{s}", nc.vector.reciprocal(st[s][:, 0:1], st[s][:, 1:2]))
                    line(f"m{s}", nc.vector.scalar_tensor_tensor(out=mt[s][:], in0=ht[s][:], scalar=st[s][:, 0:1],
                                                                 in1=gb[:], op0=ALU.mult, op1=ALU.mult))
                    dve.wait_ge(pes, M(f"logit{s}", j))
                    line(f"logit{s}", nc.vector.tensor_tensor(lg[s][:], lp[s][:, 0:EXPERTS], br[:], ALU.add))
                    nc.vector.memset(carrier[:], 0.0)
                    line(f"max{s}", nc.vector.max(top[s][:], lg[s][:]))
                    nc.vector.memset(carrier[:], 0.0)
                    line(f"idx{s}", nc.vector.max_index(ix[s][:], top[s][:], lg[s][:]))
                    line(f"idf{s}", nc.vector.tensor_copy(ixf[s][:], ix[s][:]))
                    line(f"neg{s}", nc.vector.tensor_scalar(ixf[s][:, 7:8], top[s][:, 0:1], -1.0, None, ALU.mult))
                    for q in range(TOP_K):
                        line(f"hot{q}{s}", nc.vector.tensor_scalar(
                            chosen[:, tile, q, :].rearrange("p a e -> p (a e)"), expertf[:], ixf[s][:, q:q + 1],
                            None, ALU.is_equal))
                    dve.wait_ge(acts, A(f"exp{s}", j))
                    line(f"inve{s}", nc.vector.reciprocal(ixf[s][:, 6:7], ixf[s][:, 6:7]))
                    line(f"gate{s}", nc.vector.tensor_scalar(
                        gates[:, tile, :].rearrange("p a q -> p (a q)"), gt[s][:], ixf[s][:, 6:7], None, ALU.mult))

        @block.tensor
        def _(pe):
            pe.wait_ge(once, 64)
            with pe.Fori(0, LOOPS) as j:
                for s in slots:
                    pe.wait_ge(loaded[s], j * 32 + 32)
                    for h in range(2):
                        for n in range(ND):
                            last = nc.tensor.matmul(hp[s][:, h * HALF:(h + 1) * HALF], ot[s][:, n, :],
                                                    wo[:, n, h * HALF:(h + 1) * HALF],
                                                    start=(n == 0), stop=(n == ND - 1))
                    last.then_inc(pes, 1)
                    pe.wait_ge(dves, V0.n + V(f"m{s}", j))
                    for n in range(ND):
                        last = nc.tensor.transpose(tp[:, n * P:(n + 1) * P], mt[s][:, n * P:(n + 1) * P], k.ident[:])
                    last.then_inc(pes, 1)
                    pe.wait_ge(acts, A(f"mTb{s}", j))
                    for n in range(ND):
                        last = nc.tensor.matmul(lp[s][:, 0:EXPERTS], mT[s][:, n, :], wr[:, n, :],
                                                start=(n == 0), stop=(n == ND - 1))
                    last.then_inc(pes, 1)


def place_rows(nc, k, chosen, row_of, table, row_token):
    with ExitStack() as ctx:
        sb = lambda name, shape, dt=F32: ctx.enter_context(nc.sbuf_tensor(name, shape, dt))
        sem = lambda name: ctx.enter_context(nc.semaphore(name))
        mask = sb("pmask", [P, NT, EXPERTS])
        m1 = sb("pmask1", [P, NT, EXPERTS])
        cnt = sb("pcnt", [P, EXPERTS])
        nb = sb("pnb", [P, EXPERTS])
        ge = sb("pge", [P, EXPERTS])
        incl = sb("pincl", [P, EXPERTS])
        start = sb("pstart", [P, EXPERTS])
        rank = sb("prank", [P, NT, EXPERTS])
        prod = sb("pprod", [P, NT, TOP_K, EXPERTS])
        dest = sb("pdest", [P, NT * TOP_K])
        token = sb("ptoken", [P, NT], I32)
        zero = sb("pzero", [P, ROWS // P], I32)
        rp = ctx.enter_context(nc.psum_tensor("rp", [P, HALF], F32))
        cp = ctx.enter_context(nc.psum_tensor("cp", [P, HALF], F32))
        dves, pes, made, zeroed, scattered = (sem(f"p_{n}") for n in "dves pes made zeroed scattered".split())
        V = Steps("m0 m1 m cnt one " + " ".join(f"ge{n} nb{n}" for n in range(1, T // P)) +
                  " incl first tab0 tab1 start rank prod dest cast")
        block = ctx.enter_context(nc.Block())

        @block.vector
        def _(dve):
            line = Line(dve, dves, V)
            tt = lambda o, a, b, op: nc.vector.tensor_tensor(o, a, b, op)
            line("m0", tt(mask[:], chosen[:, :, 0, :], chosen[:, :, 1, :], ALU.add))
            line("m1", tt(m1[:], chosen[:, :, 2, :], chosen[:, :, 3, :], ALU.add))
            line("m", tt(mask[:], mask[:], m1[:], ALU.add))
            dve.wait_ge(pes, 1)
            line("cnt", nc.vector.tensor_copy(cnt[:], cp[:, 0:EXPERTS]))
            line("one", nc.vector.memset(nb[:], 1.0))
            for n in range(1, T // P):
                line(f"ge{n}", nc.vector.tensor_scalar(ge[:], cnt[:], float(n * P), None, ALU.is_gt))
                line(f"nb{n}", tt(nb[:], nb[:], ge[:], ALU.add))
            line("incl", nc.vector.tensor_tensor_scan(incl[:], k.ones[:, 0:EXPERTS], nb[:], 0.0, ALU.mult, ALU.add))
            line("first", tt(start[:], incl[:], nb[:], ALU.subtract))
            line("tab0", nc.vector.tensor_copy(table[:, 0, :], start[:]))
            line("tab1", nc.vector.tensor_copy(table[:, 1, :], nb[:]))
            line("start", nc.vector.tensor_scalar(start[:], start[:], float(P), None, ALU.mult))
            dve.wait_ge(pes, 2)
            line("rank", tt(rank[:], rp[:, 0:NT * EXPERTS].rearrange("p (t e) -> p t e", e=EXPERTS),
                            start[:].unsqueeze(1).to_broadcast([P, NT, EXPERTS]), ALU.add))
            line("prod", tt(prod[:], chosen[:], rank[:].unsqueeze(2).to_broadcast([P, NT, TOP_K, EXPERTS]), ALU.mult))
            line("dest", nc.vector.tensor_reduce(dest[:], prod[:].rearrange("p t q e -> p (t q) e"), AX.X, ALU.add))
            line("cast", nc.vector.tensor_copy(row_of[:], dest[:]))

        @block.tensor
        def _(pe):
            pe.wait_ge(dves, V("m"))
            for t in range(NT):
                last = nc.tensor.matmul(cp[:, 0:EXPERTS], k.ones[:], mask[:, t, :], start=(t == 0), stop=(t == NT - 1))
            last.then_inc(pes, 1)
            for t in range(NT):
                out = rp[:, t * EXPERTS:(t + 1) * EXPERTS]
                for u in range(t):
                    nc.tensor.matmul(out, k.ones[:], mask[:, u, :], start=(u == 0), stop=False)
                last = nc.tensor.matmul(out, k.before[:], mask[:, t, :], start=(t == 0), stop=True)
            last.then_inc(pes, 1)

        @block.gpsimd
        def _(pool):
            pool.memset(zero[:], 0).then_inc(made, 1)
            pool.iota(token[:], [[P, NT]], base=0, channel_multiplier=1).then_inc(made, 1)
            pool.wait_ge(made, 2)
            pool.dma_start(row_token.rearrange("(p n) o -> p (n o)", p=P), zero[:]).then_inc(zeroed, 16)
            pool.wait_ge(zeroed, 16)
            pool.wait_ge(dves, V("cast"))
            for t in range(NT):
                for q in range(TOP_K):
                    i = t * TOP_K + q
                    pool.indirect_dma_start(row_token, bass.IndirectOffsetOnAxis(ap=row_of[:, i:i + 1], axis=0),
                                            token[:, t:t + 1], None).then_inc(scattered, 16)
            pool.wait_ge(scattered, 16 * NT * TOP_K)


LIMIT, ALPHA = 7.0, 1.702
PARTS = 3


def split_biases(nc, b1, b2, biases):
    F = 2 * D_FF + D
    with ExitStack() as ctx:
        sb = lambda name, shape, dt=F32: ctx.enter_context(nc.sbuf_tensor(name, shape, dt))
        rest = sb("brest", [EXPERTS, F])
        part = [sb(f"bpart{i}", [EXPERTS, F], BF16) for i in range(PARTS)]
        loaded, split, stored = (ctx.enter_context(nc.semaphore(f"b_{n}")) for n in ("loaded", "split", "stored"))
        V = Steps("part0 rest1 part1 rest2 part2")
        block = ctx.enter_context(nc.Block())

        @block.sync
        def _(sp):
            sp.dma_start(rest[:, 0:2 * D_FF], b1).then_inc(loaded, 16)
            sp.dma_start(rest[:, 2 * D_FF:F], b2).then_inc(loaded, 16)
            for i in range(PARTS):
                sp.wait_ge(split, V(f"part{i}"))
                sp.dma_start(biases[:, i, :], part[i][:]).then_inc(stored, 16)
            sp.wait_ge(stored, 16 * PARTS)

        @block.vector
        def _(dve):
            line = Line(dve, split, V)
            dve.wait_ge(loaded, 32)
            for i in range(PARTS):
                if i:
                    line(f"rest{i}", nc.vector.tensor_tensor(rest[:], rest[:], part[i - 1][:], ALU.subtract))
                line(f"part{i}", nc.vector.tensor_copy(part[i][:], rest[:]))


def expert_rows(nc, k, m, row_token, table, w1, w2, biases, yb):
    SLOTS = 6
    order = (0, 2, 1, 3)
    Q = ND // 2
    with ExitStack() as ctx:
        sb = lambda name, shape, dt=F32: ctx.enter_context(nc.sbuf_tensor(name, shape, dt))
        sem = lambda name: ctx.enter_context(nc.semaphore(name))
        w = [sb(f"wslot{c}", [P, ND, HALF]) for c in range(SLOTS)]
        bias = [sb(f"bslot{c}", [PARTS, HALF], BF16) for c in range(SLOTS)]
        ones = sb("bones", [PARTS, P], BF16)
        idx = sb("gidx", [P, 1], U32)
        xg = sb("xg", [P, D])
        xT = sb("xT", [P, ND, P])
        glu = [sb(f"glu{h}", [P, HALF]) for h in range(2)]
        lin = [sb(f"lin{h}", [P, HALF]) for h in range(2)]
        sig = [sb(f"sig{h}", [P, HALF]) for h in range(2)]
        act_t = sb("actt", [P, D_FF])
        aT = sb("aTt", [P, ND, P])
        yo = sb("yo", [P, D])
        tp = [ctx.enter_context(nc.psum_tensor(f"etp{h}", [P, HALF], F32)) for h in range(2)]
        hc = [ctx.enter_context(nc.psum_tensor(f"hc{c}", [P, HALF], F32)) for c in range(SLOTS)]
        w_loaded = [sem(f"w_in{c}") for c in range(SLOTS)]
        used = [sem(f"used{c}") for c in range(SLOTS)]
        idx_loaded, gathered, y_stored, passed = sem("idx_in"), sem("gathered"), sem("y_out"), sem("e_passed")
        x_turned = sem("x_turned")
        act_turned = sem("act_turned")
        x_low, x_high = sem("x_low"), sem("x_high")
        act_copied = sem("act_copied")
        sigmoid_done, ones_made = sem("sigmoid_done"), sem("ones_made")
        y_low, y_high, passed_act = sem("y_low"), sem("y_high"), sem("act_passed")
        dves = sem("e_dves")
        V = Steps("glu0 lin0 mul0 act0 glu1 lin1 mul1 act1")
        flat = lambda t: t.rearrange("p n t -> p (n t)")
        block = ctx.enter_context(nc.Block())

        def blocks(eng, body):
            with eng.Fori(0, EXPERTS) as e:
                first = eng.value_load(table[0:1, 0, bass.ds(e, 1)], min_val=0, max_val=BLOCKS - 1)
                count = eng.value_load(table[0:1, 1, bass.ds(e, 1)], min_val=1, max_val=T // P)
                with eng.Fori(0, count) as b:
                    body(first + b, e)

        @block.sync
        def _(sp):
            def load(c, e):
                src, chunk = (w1, order[c]) if c < 4 else (w2, c - 4)
                cols = slice(chunk * HALF, (chunk + 1) * HALF)
                sp.dma_start(w[c][:], row(src, e).rearrange("o (n p) f -> p (o n) f", p=P)[:, :, cols]
                             ).then_inc(w_loaded[c], 16)
                bcols = slice(cols.start + (0 if c < 4 else 2 * D_FF), cols.stop + (0 if c < 4 else 2 * D_FF))
                sp.dma_start(bias[c][:], row(biases, e).rearrange("o s f -> (o s) f")[:, bcols]
                             ).then_inc(w_loaded[c], 16)

            for c in range(SLOTS):
                load(c, 0)
            with sp.Fori(1, EXPERTS) as e:
                first = sp.value_load(table[0:1, 0, bass.ds(e, 1)], min_val=0, max_val=BLOCKS - 1)
                for c in range(SLOTS):
                    sp.wait_ge(used[c], first)
                    load(c, e)

        @block.gpsimd
        def _(pool):
            def fetch(n):
                pool.dma_start(idx[:], row(row_token, n * P, P)).then_inc(idx_loaded, 16)
                pool.wait_ge(idx_loaded, n * 16 + 16)
                pool.sem_inc(passed, 1)
                pool.indirect_dma_start(xg[:], None, m, bass.IndirectOffsetOnAxis(ap=idx[:, 0:1], axis=0)
                                        ).then_inc(gathered, 16)

            def body(n, e):
                pool.wait_ge(x_turned, n * 2 + 2)
                fetch(n + 1)

            pool.memset(ones[:], 1.0).then_inc(ones_made, 1)
            fetch(0)
            blocks(pool, body)
            last = pool.value_load(table[0:1, 0, EXPERTS - 1:EXPERTS], min_val=0, max_val=BLOCKS - 1)
            more = pool.value_load(table[0:1, 1, EXPERTS - 1:EXPERTS], min_val=1, max_val=T // P)
            pool.wait_ge(gathered, (last + more) * 16 + 16)
            pool.sem_inc(passed, 1)

        @block.scalar
        def _(act):
            def copy_x(n):
                act.wait_ge(x_turned, n * 2 + 2)
                nc.scalar.copy(flat(xT[:, 0:Q, :]), tp[0][:]).then_inc(x_low, 1)

            def sigmoid(h, n):
                act.wait_ge(dves, V(f"glu{h}", n))
                nc.scalar.activation(sig[h][:], glu[h][:], ACT.Sigmoid, scale=ALPHA).then_inc(sigmoid_done, 1)

            def copy_act(h, n):
                act.wait_ge(act_turned, n * 2 + 1 + h)
                nc.scalar.copy(flat(aT[:, Q * h:Q * h + Q, :]), tp[h][:]).then_inc(act_copied, 1)

            def body(n, e):
                sigmoid(0, n)
                copy_act(0, n)
                sigmoid(1, n)
                copy_x(n + 1)
                copy_act(1, n)
                act.wait_ge(used[5], n + 1)
                nc.scalar.copy(yo[:, HALF:D], hc[5][:]).then_inc(y_high, 1)
                act.wait_ge(y_high, n + 1)
                act.wait_ge(y_low, n + 1)
                act.dma_start(row(yb, n * P, P), yo[:]).then_inc(y_stored, 16)
                act.wait_ge(y_stored, n * 16 + 16)
                act.sem_inc(passed_act, 1)

            copy_x(0)
            blocks(act, body)

        @block.vector
        def _(dve):
            def copy_x(n):
                dve.wait_ge(x_turned, n * 2 + 1)
                nc.vector.tensor_copy(flat(xT[:, Q:ND, :]), tp[1][:]).then_inc(x_high, 1)

            def body(n, e):
                line = Line(dve, dves, V, n)
                for h in range(2):
                    dve.wait_ge(used[2 * h], n + 1)
                    line(f"glu{h}", nc.vector.tensor_scalar(glu[h][:], hc[2 * h][:], LIMIT, None, ALU.min))
                    dve.wait_ge(used[2 * h + 1], n + 1)
                    line(f"lin{h}", nc.vector.tensor_scalar(lin[h][:], hc[2 * h + 1][:], LIMIT, -LIMIT,
                                                            ALU.min, ALU.max))
                    line(f"mul{h}", nc.vector.scalar_tensor_tensor(out=lin[h][:], in0=lin[h][:], scalar=1.0,
                                                                   in1=glu[h][:], op0=ALU.add, op1=ALU.mult))
                    dve.wait_ge(sigmoid_done, n * 2 + 1 + h)
                    line(f"act{h}", nc.vector.tensor_tensor(act_t[:, h * HALF:(h + 1) * HALF], lin[h][:], sig[h][:],
                                                            ALU.mult))
                copy_x(n + 1)
                dve.wait_ge(used[4], n + 1)
                nc.vector.tensor_copy(yo[:, 0:HALF], hc[4][:]).then_inc(y_low, 1)

            copy_x(0)
            blocks(dve, body)

        @block.tensor
        def _(pe):
            def turn(src, h):
                for q in range(Q):
                    last = nc.tensor.transpose(tp[h][:, q * P:(q + 1) * P],
                                               src[:, (Q * h + q) * P:(Q * h + q + 1) * P], k.ident[:])
                return last

            def turn_x(n):
                pe.wait_ge(gathered, n * 16 + 16)
                turn(xg, 1).then_inc(x_turned, 1)
                turn(xg, 0).then_inc(x_turned, 1)

            def bias_rows(c, e):
                pe.wait_ge(w_loaded[c], e * 32 + 32)
                nc.tensor.matmul(hc[c][:], ones[:], bias[c][:], start=True, stop=False)

            def part(c, lhsT, q):
                return nc.tensor.matmul(hc[c][:], lhsT[:, q, :], w[c][:, q, :], start=False, stop=(q == ND - 1))

            def product(c, lhsT, e):
                bias_rows(c, e)
                for q in range(ND):
                    last = part(c, lhsT, q)
                last.then_inc(used[c], 1)

            def body(n, e):
                pe.wait_ge(x_low, n + 1)
                pe.wait_ge(x_high, n + 1)
                for c in range(3):
                    product(c, xT, e)
                pe.wait_ge(dves, V("act0", n))
                turn(act_t, 0).then_inc(act_turned, 1)
                product(3, xT, e)
                pe.wait_ge(act_copied, n * 2 + 1)
                turn_x(n + 1)
                for c in (4, 5):
                    bias_rows(c, e)
                for q in range(Q - 1):
                    for c in (4, 5):
                        part(c, aT, q)
                pe.wait_ge(dves, V("act1", n))
                pe.wait_ge(x_high, n + 2)
                turn(act_t, 1).then_inc(act_turned, 1)
                for c in (4, 5):
                    part(c, aT, Q - 1)
                pe.wait_ge(act_copied, n * 2 + 2)
                for c in (4, 5):
                    for q in range(Q, ND):
                        last = part(c, aT, q)
                    last.then_inc(used[c], 1)

            pe.wait_ge(ones_made, 1)
            turn_x(0)
            blocks(pe, body)


def finish(nc, k, h1, yb, row_of, gates, p, w_ple, ple_gain, w_gate, out):
    NP = PLE // P
    with ExitStack() as ctx:
        sb = lambda name, shape, dt=F32: ctx.enter_context(nc.sbuf_tensor(name, shape, dt))
        sem = lambda name: ctx.enter_context(nc.semaphore(name))
        slots = range(2)
        wg = sb("wgate", [P, ND, D])
        wp = sb("wple", [P, NP, D])
        gb = sb("pgain", [P, D])
        ht = [sb(f"fh{s}", [P, D]) for s in slots]
        pt = [sb(f"fp{s}", [P, PLE]) for s in slots]
        rows = [[sb(f"frow{s}{q}", [P, D]) for q in range(TOP_K)] for s in slots]
        ix = [sb(f"fix{s}", [P, TOP_K], U32) for s in slots]
        hT = [sb(f"fhT{s}", [P, ND, P]) for s in slots]
        pT = [sb(f"fpT{s}", [P, NP, P]) for s in slots]
        sg = sb("fsig", [P, D])
        es = sb("fe", [P, D])
        sq = sb("fsq", [P, D])
        st = sb("fst", [P, 2])
        ot = [sb(f"fo{s}", [P, D]) for s in slots]
        tp = ctx.enter_context(nc.psum_tensor("ftp", [P, D], F32))
        pp = ctx.enter_context(nc.psum_tensor("fpp", [P, HALF], F32))
        ep = ctx.enter_context(nc.psum_tensor("fep", [P, D], F32))
        gp = ctx.enter_context(nc.psum_tensor("fgp", [P, D], F32))
        once, passed = sem("f_once"), sem("f_passed")
        loaded = [sem(f"f_loaded{s}") for s in slots]
        fetched = [sem(f"f_rows{s}") for s in slots]
        stored = [sem(f"f_stored{s}") for s in slots]
        acts, dves, pes = sem("f_acts"), sem("f_dves"), sem("f_pes")
        A = Steps(" ".join(f"pT{s} sq{s} root{s} ha{s} hb{s} sig{s}" for s in slots))
        V = Steps(" ".join(f"ix{s} " + " ".join(f"r{q}{s}" for q in range(TOP_K)) + f" inv{s} e{s} g{s} out{s}"
                           for s in slots))
        M = Steps(" ".join(f"pT{s} e{s} hT{s} g{s}" for s in slots))
        LOOPS = NT // 2
        block = ctx.enter_context(nc.Block())

        @block.sync
        def _(sp):
            sp.dma_start(wp[:], w_ple.rearrange("(n p) e -> p n e", p=P)).then_inc(once, 16)
            sp.dma_start(gb[:], ple_gain.rearrange("(o e) -> o e", o=1).to_broadcast([P, D])).then_inc(once, 16)
            sp.dma_start(wg[:], w_gate.rearrange("(n p) e -> p n e", p=P)).then_inc(once, 16)
            with sp.Fori(0, LOOPS) as j:
                for s in slots:
                    first = sp.snap(j * 2 * P + s * P)
                    sp.wait_ge(stored[s], j * 16)
                    sp.dma_start(ht[s][:], row(h1, first, P)).then_inc(loaded[s], 16)
                    sp.dma_start(pt[s][:], row(p, first, P)).then_inc(loaded[s], 16)

        @block.gpsimd
        def _(pool):
            with pool.Fori(0, LOOPS) as j:
                for s in slots:
                    pool.wait_ge(dves, V(f"ix{s}", j))
                    pool.sem_inc(passed, 1)
                    for q in range(TOP_K):
                        pool.indirect_dma_start(rows[s][q][:], None, yb,
                                                bass.IndirectOffsetOnAxis(ap=ix[s][:, q:q + 1], axis=0)
                                                ).then_inc(fetched[s], 16)

        @block.scalar
        def _(act):
            with act.Fori(0, LOOPS) as j:
                line = Line(act, acts, A, j)
                for s in slots:
                    act.wait_ge(pes, M(f"pT{s}", j))
                    line(f"pT{s}", nc.scalar.copy(pT[s][:].rearrange("p n t -> p (n t)"), pp[:, 0:PLE]))
                    act.wait_ge(pes, M(f"e{s}", j))
                    line(f"sq{s}", nc.scalar.activation(sq[:], ep[:], ACT.Square, accum_out=st[:, 0:1]))
                    line(f"root{s}", nc.scalar.activation(st[:, 0:1], st[:, 0:1], ACT.Sqrt, bias=k.eps[:, 0:1],
                                                          scale=1.0 / D))
                    act.wait_ge(pes, M(f"hT{s}", j))
                    for n in range(2):
                        line(f"h{'ab'[n]}{s}", nc.scalar.copy(
                            hT[s][:].rearrange("p n t -> p (n t)")[:, n * HALF:(n + 1) * HALF],
                            tp[:, n * HALF:(n + 1) * HALF]))
                    act.wait_ge(pes, M(f"g{s}", j))
                    line(f"sig{s}", nc.scalar.activation(sg[:], gp[:], ACT.Sigmoid))
                    act.wait_ge(dves, V(f"out{s}", j))
                    act.dma_start(row(out, j * 2 * P + s * P, P), ot[s][:]).then_inc(stored[s], 16)
            for s in slots:
                act.wait_ge(stored[s], 16 * LOOPS)

        @block.vector
        def _(dve):
            dve.wait_ge(once, 48)
            with dve.Fori(0, LOOPS) as j:
                line = Line(dve, dves, V, j)
                for s in slots:
                    dve.wait_ge(fetched[s], j * 64)
                    line(f"ix{s}", nc.vector.tensor_copy(ix[s][:], row_of[:, bass.ds((j * 2 + s) * TOP_K, TOP_K)]))
                    dve.wait_ge(loaded[s], j * 32 + 32)
                    dve.wait_ge(fetched[s], j * 64 + 64)
                    for q in range(TOP_K):
                        line(f"r{q}{s}", nc.vector.scalar_tensor_tensor(
                            out=ht[s][:], in0=rows[s][q][:],
                            scalar=gates[:, bass.ds(j * 2 + s, 1), q:q + 1].rearrange("p a q -> p (a q)"),
                            in1=ht[s][:], op0=ALU.mult, op1=ALU.add))
                    dve.wait_ge(acts, A(f"root{s}", j))
                    line(f"inv{s}", nc.vector.reciprocal(st[:, 1:2], st[:, 0:1]))
                    line(f"e{s}", nc.vector.scalar_tensor_tensor(out=es[:], in0=ep[:], scalar=st[:, 1:2], in1=gb[:],
                                                                 op0=ALU.mult, op1=ALU.mult))
                    dve.wait_ge(acts, A(f"sig{s}", j))
                    line(f"g{s}", nc.vector.tensor_tensor(es[:], es[:], sg[:], ALU.mult))
                    dve.wait_ge(stored[s], j * 16)
                    line(f"out{s}", nc.vector.tensor_tensor(ot[s][:], es[:], ht[s][:], ALU.add))

        @block.tensor
        def _(pe):
            pe.wait_ge(once, 48)
            with pe.Fori(0, LOOPS) as j:
                for s in slots:
                    pe.wait_ge(loaded[s], j * 32 + 32)
                    pe.wait_ge(dves, V.n * j if s == 0 else V("out0", j))
                    for n in range(NP):
                        last = nc.tensor.transpose(pp[:, n * P:(n + 1) * P], pt[s][:, n * P:(n + 1) * P], k.ident[:])
                    last.then_inc(pes, 1)
                    pe.wait_ge(acts, A(f"pT{s}", j))
                    for h in range(2):
                        for n in range(NP):
                            last = nc.tensor.matmul(ep[:, h * HALF:(h + 1) * HALF], pT[s][:, n, :],
                                                    wp[:, n, h * HALF:(h + 1) * HALF], start=(n == 0), stop=(n == NP - 1))
                    last.then_inc(pes, 1)
                    pe.wait_ge(dves, V(f"r{TOP_K - 1}{s}", j))
                    for n in range(ND):
                        last = nc.tensor.transpose(tp[:, n * P:(n + 1) * P], ht[s][:, n * P:(n + 1) * P], k.ident[:])
                    last.then_inc(pes, 1)
                    pe.wait_ge(acts, A(f"hb{s}", j))
                    for h in range(2):
                        for n in range(ND):
                            last = nc.tensor.matmul(gp[:, h * HALF:(h + 1) * HALF], hT[s][:, n, :],
                                                    wg[:, n, h * HALF:(h + 1) * HALF], start=(n == 0), stop=(n == ND - 1))
                    last.then_inc(pes, 1)


def build_layer(nc, x, p, norm_mix_g, w_in, rw_mu, rw_w0, rw_w2, rw_a0, rw_a2, rw_g2, rw_k_k, rw_k_a, rw_r_k,
                rw_ln_g, rw_ln_b, da_q_norm_g, da_k_norm_g, da_lq1, da_lk1, da_lq2, da_lk2, da_subln_g, w_out,
                norm_ffn_g, w_router, b_router, w1, b1, w2, b2, w_ple, ple_norm_g, w_ple_gate, out):
    scratch = lambda name, shape, dt=F32: nc.dram_tensor(name, shape, dt, kind="Internal").ap()
    zT = scratch("zT", [IN_COLS, T])
    ops = scratch("scan_ops", [2, C_RW, 4, T])
    vals = scratch("scan_vals", [C_RW, T])
    bonus = scratch("bonus", [C_RW, T])
    gate_in = scratch("gate_in", [P, T])
    end_decay = scratch("end_decay", [2, C_RW, NCH])
    y = scratch("scan_y", [2, T, C_RW])
    oT = scratch("mixed", [D, T])
    h1 = scratch("h1", [T, D])
    m = scratch("ffn_in", [T, D])
    row_token = scratch("row_token", [ROWS, 1], U32)
    yb = scratch("expert_out", [ROWS, D])
    biases = scratch("biases", [EXPERTS, PARTS, 2 * D_FF + D], BF16)
    flat = lambda ap: ap.rearrange("h n -> (h n)")
    x, p, out = x[0], p[0, 0], out[0]
    with ExitStack() as ctx:
        sb = lambda name, shape, dt=F32: ctx.enter_context(nc.sbuf_tensor(name, shape, dt))

        class k:
            ident, ones, head_ones, before = (sb(n, [P, P]) for n in ("ident", "ones", "head_ones", "before"))
            zeros = sb("zeros", [P, D])
            causal = sb("causal", [P, 2, 4, P])
            near = sb("near", [P, 3, P])
            chunk_col = sb("chunk_col", [P, 2])
            scan_keep = sb("scan_keep", [P, T])
            eps = sb("eps", [P, 3])

        chosen = sb("chosen", [P, NT, TOP_K, EXPERTS])
        gates = sb("gates", [P, NT, TOP_K])
        row_of = sb("row_of", [P, NT * TOP_K], U32)
        table = sb("table", [P, 2, EXPERTS], I32)
        constants(nc, k)
        split_biases(nc, b1[0], b2[0], biases)
        with nc.sbuf_tensor("uT", [P, ND, T], F32) as uT:
            normed_columns(nc, k, x, norm_mix_g[0], uT)
            project_in(nc, k, uT, w_in[0], zT)
        rwkv_prepare(nc, k, zT, rw_mu[0], rw_w0[0], rw_w2[0], rw_a0[0], rw_a2[0], rw_k_k[0], rw_k_a[0],
                     flat(rw_r_k[0]), ops, vals, bonus, gate_in, end_decay)
        rwkv_scan(nc, k, ops, vals, end_decay, y, yb)
        differential_attention(nc, k, zT, da_q_norm_g[0], da_k_norm_g[0], da_lq1[0], da_lk1[0], da_lq2[0],
                               da_lk2[0], da_subln_g[0], oT)
        finish_rwkv(nc, k, y, bonus, gate_in, rw_g2[0], flat(rw_ln_g[0]), flat(rw_ln_b[0]), oT)
        mix_out_and_route(nc, k, x, oT, w_out[0], norm_ffn_g[0], w_router[0], b_router[0], h1, m, chosen, gates)
        place_rows(nc, k, chosen, row_of, table, row_token)
        expert_rows(nc, k, m, row_token, table, w1[0], w2[0], biases, yb)
        finish(nc, k, h1, yb, row_of, gates, p, w_ple[0], ple_norm_g[0], w_ple_gate[0], out)


INPUTS = ("x p norm_mix_g w_in rw_mu rw_w0 rw_w2 rw_a0 rw_a2 rw_g2 rw_k_k rw_k_a rw_r_k rw_ln_g rw_ln_b "
          "da_q_norm_g da_k_norm_g da_lq1 da_lk1 da_lq2 da_lk2 da_subln_g w_out norm_ffn_g w_router b_router "
          "w1 b1 w2 b2 w_ple ple_norm_g w_ple_gate").split()


def kernel(**inputs):
    import numpy as np
    import concourse.bacc as bacc
    from concourse.bass_utils import run_bass_kernel_spmd

    nc = bacc.Bacc("TRN2", target_bir_lowering=False, num_devices=1)
    arrays, args = {}, []
    for name in INPUTS:
        a = np.ascontiguousarray(inputs[name])
        arrays[f"in_{name}"] = a
        args.append(nc.dram_tensor(f"in_{name}", a.shape, mybir.dt.from_np(a.dtype), kind="ExternalInput").ap())
    args.append(nc.dram_tensor("out_h", (1, T, D), F32, kind="ExternalOutput").ap())
    build_layer(nc, *args)
    r = run_bass_kernel_spmd(nc, [arrays], core_ids=[0])
    return r.results[0]["out_h"]
```

```python
import math
from contextlib import ExitStack

import concourse.bass as bass
from concourse import mybir
from concourse.alu_op_type import AluOpType as ALU

F32 = mybir.dt.float32
F32R = mybir.dt.float32r
BF16 = mybir.dt.bfloat16
U32 = mybir.dt.uint32
I32 = mybir.dt.int32
ACT = mybir.ActivationFunctionType
AX = mybir.AxisListType

P = 128
T, D = 1024, 1024
NT = T // P
ND = D // P
HALF = 512
C_RW = D // 2
RW_TILES = C_RW // P
HEAD = 64
CHUNK = 64
NCH = T // CHUNK
LORA = 64
RW_COLS = 3 * C_RW + 4 * LORA + 128
C_DA = D - C_RW
DA_HEADS = 4
IN_COLS = RW_COLS + 3 * C_DA
IN_TILES = IN_COLS // P
EXPERTS, TOP_K, D_FF = 32, 4, D
PLE = 256
BLOCKS = (T * TOP_K + EXPERTS * P) // P
ROWS = (BLOCKS + T // P) * P
PARTS = 3
NORM_EPS = 1e-6
RW_GN_EPS = HEAD * 1e-5
LAMBDA_INIT = 0.8 - 0.6 * math.exp(0.0)
DECAY = math.exp(-0.5)


def row(ap, i, n=1):
    return ap[bass.ds(i, n)]


class Steps:

    def __init__(self, text):
        self.names = text.split()
        self.n = len(self.names)

    def __call__(self, name, i=0):
        return self.names.index(name) + 1 + i * self.n


class Line:

    def __init__(self, eng, sem, steps, i=0, base=0):
        self.eng, self.sem, self.steps, self.i, self.base, self.at = eng, sem, steps, i, base, 0

    def __call__(self, name, instruction):
        assert self.steps.names[self.at] == name, (name, self.steps.names[self.at])
        self.at += 1
        instruction.then_inc(self.sem, 1)
        self.eng.wait_ge(self.sem, self.steps(name, self.i) + self.base)


def constants(nc, k, b1, b2, biases):
    F = 2 * D_FF + D
    with ExitStack() as ctx:
        sb = lambda name, shape, dt=F32: ctx.enter_context(nc.sbuf_tensor(name, shape, dt))
        rest = sb("brest", [EXPERTS, F])
        part = [sb(f"bpart{i}", [EXPERTS, F], BF16) for i in range(PARTS)]
        made, loaded, split, stored = (ctx.enter_context(nc.semaphore(n)) for n in (
            "const_made", "b_loaded", "b_split", "b_stored"))
        V = Steps("part0 rest1 part1 rest2 part2")
        block = ctx.enter_context(nc.Block())

        @block.sync
        def _(sp):
            sp.dma_start(rest[:, 0:2 * D_FF], b1).then_inc(loaded, 16)
            sp.dma_start(rest[:, 2 * D_FF:F], b2).then_inc(loaded, 16)
            for i in range(PARTS):
                sp.wait_ge(split, V(f"part{i}"))
                sp.dma_start(biases[:, i, :], part[i][:]).then_inc(stored, 16)
            sp.wait_ge(stored, 16 * PARTS)

        @block.vector
        def _(dve):
            line = Line(dve, split, V)
            dve.wait_ge(loaded, 32)
            for i in range(PARTS):
                if i:
                    line(f"rest{i}", nc.vector.tensor_tensor(rest[:], rest[:], part[i - 1][:], ALU.subtract))
                line(f"part{i}", nc.vector.tensor_copy(part[i][:], rest[:]))

        @block.gpsimd
        def _(pool):
            n = 0

            def select(t, pattern, mult, base, op, fill):
                nonlocal n
                pool.wait_ge(made, n)
                pool.affine_select(out=t, in_=t, compare_op=op, fill=fill, base=base,
                                   pattern=pattern, channel_multiplier=mult).then_inc(made, 1)
                n += 1

            def fill(t, v):
                nonlocal n
                pool.memset(t, v).then_inc(made, 1)
                n += 1

            def blocks(t, size):
                v = t.rearrange("p (b s) -> p b s", s=size)
                m = P // size
                select(v, [[-size, m], [0, size]], 1, 0, ALU.is_ge, 0.0)
                select(v, [[size, m], [0, size]], -1, size - 1, ALU.is_ge, 0.0)

            fill(k.ident[:], 0.0)
            select(k.ident[:], [[-1, P]], 1, 0, ALU.not_equal, 1.0)
            fill(k.ones[:], 1.0)
            fill(k.zeros[:], 0.0)
            fill(k.head_ones[:], 1.0)
            blocks(k.head_ones[:], HEAD)
            fill(k.before[:], 1.0)
            select(k.before[:], [[1, P]], -1, 0, ALU.is_gt, 0.0)
            for d in range(2):
                s = 1 - 2 * d
                for kind, op in ((0, ALU.is_gt), (1, ALU.is_ge)):
                    fill(k.causal[:, d, kind, :], 1.0)
                    select(k.causal[:, d, kind, :], [[s, P]], -s, 0, op, 0.0)
                    blocks(k.causal[:, d, kind, :], CHUNK)
                    fill(k.causal[:, d, 2 + kind, :], 1.0)
                    select(k.causal[:, d, 2 + kind, :], [[s, P]], -s, 0, op, 0.0)
                    blocks(k.causal[:, d, 2 + kind, :], CHUNK)
            for level, size in enumerate((16, 32, 64)):
                fill(k.near[:, level, :], 1.0)
                blocks(k.near[:, level, :], size)
            for level in (2, 1):
                pool.wait_ge(made, n)
                pool.tensor_tensor(k.near[:, level, :], k.near[:, level, :], k.near[:, level - 1, :],
                                   ALU.subtract).then_inc(made, 1)
                n += 1
            fill(k.chunk_col[:], 1.0)
            v = k.chunk_col[:]
            select(v[:, 0:1], [[0, 1]], -1, CHUNK - 1, ALU.is_ge, 0.0)
            select(v[:, 1:2], [[0, 1]], 1, -CHUNK, ALU.is_ge, 0.0)
            fill(k.scan_keep[:], 1.0)
            v = k.scan_keep[:].rearrange("p (c s) -> p c s", s=CHUNK)
            select(v, [[0, NCH], [1, CHUNK]], 0, 0, ALU.not_equal, 0.0)
            fill(k.eps[:, 0:1], NORM_EPS)
            fill(k.eps[:, 1:2], 1e-12)
            fill(k.eps[:, 2:3], RW_GN_EPS)
            pool.wait_ge(made, n)


def normed_columns(nc, k, x, gain, u_high, u_rest):
    with ExitStack() as ctx:
        sb = lambda name, shape, dt=F32: ctx.enter_context(nc.sbuf_tensor(name, shape, dt))
        sem = lambda name: ctx.enter_context(nc.semaphore(name))
        xa = sb("xa", [P, NT, D])
        xn = [sb(f"xn{s}", [P, D]) for s in range(2)]
        sq = sb("sq", [P, D])
        stats = sb("xstats", [P, NT])
        gcol = sb("gcol", [P, ND])
        ut = [sb(f"ut{s}", [P, ND, P]) for s in range(2)]
        ps = [ctx.enter_context(nc.psum_tensor(f"tp{s}", [P, D], F32)) for s in range(2)]
        x_loaded = [sem(f"x_loaded{s}") for s in range(2)]
        gain_loaded = sem("gain_loaded")
        act_done, dve_done, transposed = sem("a_done"), sem("v_done"), sem("transposed")
        A0 = Steps("root")
        V0 = Steps(" ".join(f"sum{i}" for i in range(NT)) + " inv")
        A = Steps("high0 high1")
        V = Steps("xn0 xn1 out0 out1 rest0 rest1")
        block = ctx.enter_context(nc.Block())
        PAIRS = NT // 2

        @block.sync
        def _(sp):
            x_view = x.rearrange("(n p) d -> p n d", p=P)
            for s in range(2):
                tiles = slice(s * PAIRS, (s + 1) * PAIRS)
                sp.dma_start(xa[:, tiles, :], x_view[:, tiles, :]).then_inc(x_loaded[s], 16)
            with nc.allow_non_contiguous_dma(reason="gain columns"):
                sp.dma_start(gcol[:], gain.rearrange("(n p) -> p n", p=P)).then_inc(gain_loaded, 16)

        @block.scalar
        def _(act):
            line = Line(act, act_done, A0)
            act.wait_ge(dve_done, V0(f"sum{NT - 1}"))
            line("root", nc.scalar.activation(stats[:], stats[:], ACT.Sqrt, bias=k.eps[:, 0:1], scale=1.0 / D))
            with act.Fori(0, PAIRS) as j:
                line = Line(act, act_done, A, j, A0.n)
                for s in range(2):
                    act.wait_ge(dve_done, V0.n + V(f"out{s}", j))
                    line(f"high{s}", nc.scalar.copy(u_high[:, :, bass.ds(j * 2 * P + s * P, P)], ut[s][:]))

        @block.vector
        def _(dve):
            line = Line(dve, dve_done, V0)
            for i in range(NT):
                if i % PAIRS == 0:
                    dve.wait_ge(x_loaded[i // PAIRS], 16)
                line(f"sum{i}", nc.vector.tensor_tensor_reduce(sq[:], xa[:, i, :], xa[:, i, :], 1.0, 0.0,
                                                               ALU.mult, ALU.add, stats[:, i:i + 1]))
            dve.wait_ge(act_done, A0("root"))
            line("inv", nc.vector.reciprocal(stats[:], stats[:]))
            dve.wait_ge(gain_loaded, 16)
            with dve.Fori(0, PAIRS) as j:
                line = Line(dve, dve_done, V, j, V0.n)
                tile = lambda s: bass.ds(j * 2 + s, 1)
                tokens = lambda s: bass.ds(j * 2 * P + s * P, P)
                for s in range(2):
                    line(f"xn{s}", nc.vector.tensor_scalar(xn[s][:], xa[:, tile(s), :].rearrange("p a d -> p (a d)"),
                                                           stats[:, tile(s)], None, ALU.mult))
                for s in range(2):
                    dve.wait_ge(transposed, j * 2 + s + 1)
                    line(f"out{s}", nc.vector.tensor_tensor(
                        ut[s][:], ps[s][:].rearrange("p (n t) -> p n t", t=P),
                        gcol[:].unsqueeze(2).to_broadcast([P, ND, P]), ALU.mult))
                for s in range(2):
                    dve.wait_ge(act_done, A0.n + A(f"high{s}", j))
                    line(f"rest{s}", nc.vector.tensor_tensor(u_rest[:, :, tokens(s)], ut[s][:], u_high[:, :, tokens(s)],
                                                             ALU.subtract))

        @block.tensor
        def _(pe):
            with pe.Fori(0, PAIRS) as j:
                for s in range(2):
                    pe.wait_ge(dve_done, V0.n + V(f"xn{s}", j))
                    for n in range(ND):
                        last = nc.tensor.transpose(ps[s][:, n * P:(n + 1) * P], xn[s][:, n * P:(n + 1) * P],
                                                   k.ident[:])
                    last.then_inc(transposed, 1)


def project_in(nc, k, u_high, u_rest, w_in, zT):
    R = 3
    STEPS = IN_TILES // R
    with ExitStack() as ctx:
        sb = lambda name, shape, dt=F32: ctx.enter_context(nc.sbuf_tensor(name, shape, dt))
        sem = lambda name: ctx.enter_context(nc.semaphore(name))
        w = [sb(f"win{s}", [P, ND, P]) for s in range(R)]
        w_high = [sb(f"winh{s}", [P, ND, P], F32R) for s in range(R)]
        w_rest = [sb(f"winr{s}", [P, ND, P], F32R) for s in range(R)]
        z = [sb(f"z{s}", [P, T]) for s in range(R)]
        ps = [ctx.enter_context(nc.psum_tensor(f"zp{s}", [P, T], F32)) for s in range(R)]
        w_loaded = [sem(f"w_loaded{s}") for s in range(R)]
        z_stored = [sem(f"z_stored{s}") for s in range(R)]
        multiplied = [sem(f"multiplied{s}") for s in range(R)]
        copied = [sem(f"copied{s}") for s in range(R)]
        high_made = [sem(f"winh_made{s}") for s in range(R)]
        rest_made = [sem(f"winr_made{s}") for s in range(R)]
        block = ctx.enter_context(nc.Block())
        w_view = w_in.rearrange("(kt p) n -> p kt n", p=P)
        flat = lambda t: t[:].rearrange("p n m -> p (n m)")

        @block.sync
        def _(sp):
            for s in range(R):
                sp.dma_start(w[s][:], w_view[:, :, s * P:(s + 1) * P]).then_inc(w_loaded[s], 16)
            with sp.Fori(1, STEPS) as j:
                for s in range(R):
                    first = sp.snap(j * R * P + s * P)
                    sp.wait_ge(rest_made[s], j)
                    sp.dma_start(w[s][:], w_view[:, :, bass.ds(first, P)]).then_inc(w_loaded[s], 16)

        @block.gpsimd
        def _(pool):
            with pool.Fori(0, STEPS) as j:
                for s in range(R):
                    pool.wait_ge(copied[s], j * 2 + 2)
                    pool.dma_start(row(zT, j * R * P + s * P, P), z[s][:]).then_inc(z_stored[s], 16)
            for s in range(R):
                pool.wait_ge(z_stored[s], 16 * STEPS)

        @block.tensor
        def _(pe):
            with pe.Fori(0, STEPS) as j:
                for s in range(R):
                    pe.wait_ge(rest_made[s], j + 1)
                    for h in range(2):
                        half = slice(h * HALF, (h + 1) * HALF)
                        for kt in range(ND):
                            for n, (a, b) in enumerate(((w_high, u_high), (w_high, u_rest), (w_rest, u_high))):
                                last = nc.tensor.matmul(ps[s][:, half], a[s][:, kt, :], b[:, kt, half],
                                                        start=(kt == 0 and n == 0), stop=(kt == ND - 1 and n == 2))
                    last.then_inc(multiplied[s], 1)

        def copies(eng, copy, half, split):
            def copied_out(s, j):
                eng.wait_ge(multiplied[s], j + 1)
                cols = slice(half * HALF, (half + 1) * HALF)
                copy(z[s][:, cols], ps[s][:, cols]).then_inc(copied[s], 1)

            split(0, 0)
            split(1, 0)
            for s in range(R):
                split((s + 2) % R, (s + 2) // R)
                copied_out(s, 0)
            with eng.Fori(1, STEPS - 1) as j:
                for s in range(R):
                    split((s + 2) % R, j + (s + 2) // R)
                    eng.wait_ge(z_stored[s], j * 16)
                    copied_out(s, j)
            split(2, STEPS - 1)
            for s in range(R):
                eng.wait_ge(z_stored[s], (STEPS - 1) * 16)
                copied_out(s, STEPS - 1)

        @block.scalar
        def _(act):
            def split(s, j):
                act.wait_ge(w_loaded[s], j * 16 + 16)
                if not isinstance(j, int) or j:
                    act.wait_ge(multiplied[s], j)
                nc.scalar.copy(flat(w_high[s]), flat(w[s])).then_inc(high_made[s], 1)

            copies(act, nc.scalar.copy, 0, split)

        @block.vector
        def _(dve):
            def split(s, j):
                if not isinstance(j, int) or j:
                    dve.wait_ge(copied[s], j * 2)
                dve.wait_ge(high_made[s], j + 1)
                nc.vector.tensor_tensor(flat(w_rest[s]), flat(w[s]), flat(w_high[s]), ALU.subtract
                                        ).then_inc(rest_made[s], 1)

            copies(dve, nc.vector.tensor_copy, 1, split)


def rwkv_prepare(nc, k, zT, mu, w0, w2, a0, a2, k_k, k_a, r_k, ops, vals, bonus, gate_in, end_decay):
    with ExitStack() as ctx:
        sb = lambda name, shape, dt=F32: ctx.enter_context(nc.sbuf_tensor(name, shape, dt))
        sem = lambda name: ctx.enter_context(nc.semaphore(name))
        low = [sb(f"low{i}", [P, T + 2]) for i in range(3)]
        zin = [sb(f"zin{i}", [P, T + 2]) for i in range(3)]
        rkv = [sb(f"rkv{i}", [P, T]) for i in range(3)]
        mixc = sb("mixc", [P, 3, RW_COLS // P])
        par = sb("par", [P, 4, 5 + 3])
        parv = sb("parv", [P, 8, 4])
        lw_w = [sb(f"lora{i}", [P, P]) for i in range(4)]
        neighbours = [sb(f"nb{i}", [P, T]) for i in range(3)]
        tmp = [sb(f"tmp{i}", [P, T]) for i in range(3)]
        norm = sb("knorm", [P, 2 * NT])
        kk = sb("kk", [P, T])
        rate = [sb(f"rate{d}", [P, T]) for d in range(2)]
        soft = [sb(f"soft{d}", [P, T]) for d in range(2)]
        acc = [sb(f"accl{d}", [P, T]) for d in range(2)]
        exc = [sb(f"exc{d}", [P, T]) for d in range(2)]
        grow = [sb(f"grow{d}", [P, T]) for d in range(2)]
        shrink = [sb(f"shrink{d}", [P, T]) for d in range(2)]
        kdir = [sb(f"kdir{d}", [P, T]) for d in range(2)]
        ksum = sb("ksum", [P, T])
        res = [sb(f"res{d}", [P, 4, T]) for d in range(2)]
        dec = [sb(f"dec{d}", [P, NCH]) for d in range(2)]
        bon = sb("bon", [P, T])
        tot = sb("tot", [P, NCH])
        psA = ctx.enter_context(nc.psum_tensor("psA", [P, T], F32))
        psB = ctx.enter_context(nc.psum_tensor("psB", [P, T], F32))
        psC = ctx.enter_context(nc.psum_tensor("psC", [P, T], F32))
        psD = ctx.enter_context(nc.psum_tensor("psD", [P, T], F32))
        par_loaded, lora_loaded = sem("par_loaded"), sem("lora_loaded")
        low_loaded, z_loaded = sem("low_loaded"), sem("z_loaded")
        edge, acts, dves, pes = sem("edge"), sem("acts"), sem("dves"), sem("pes")
        stored = [sem(f"stored{d}") for d in range(2)]
        pools = sem("pools")
        kept, cut, passed = sem("kept"), sem("decay_cut"), sem("w_passed")
        low_stored = sem("low_stored")
        results_left = sem("results_left")

        V0 = Steps("one_minus half s0 m0 o0 s1 m1 o1 s2 m2 o2 omka")
        A0 = Steps("tanh sig")
        V = Steps("mk rk kkr sq mr rr scan0 exc0 scan1 tot1 exc1 inc1 m0 kd0 m1 kd1 kkinv wide mv rv kk "
                  "r0 k0 a0 q1 r1 k1 a1 b0 b1 bv")
        A = Steps("sw0 sa0 sw1 sa1 root ex0 in0 en0 dc0 ex1 in1 en1 dc1")
        M = Steps("w0 a0 norm w1 a1 kk bonus")
        G = Steps("sk sr sv kb q0 bb0 bb1")
        block = ctx.enter_context(nc.Block())
        mu_v = mu.rearrange("(n p) -> p n", p=P)

        @block.sync
        def _(sp):
            with nc.allow_non_contiguous_dma(reason="per-channel parameters as columns"):
                sp.dma_start(mixc[:, 0, :], mu_v).then_inc(par_loaded, 16)
                for d in range(2):
                    sp.dma_start(parv[:, 0 + d, :], w0[d].rearrange("(n p) -> p n", p=P)).then_inc(par_loaded, 16)
                    sp.dma_start(parv[:, 2 + d, :], a0[d].rearrange("(n p) -> p n", p=P)).then_inc(par_loaded, 16)
                for i, v in enumerate((k_k, k_a, r_k)):
                    sp.dma_start(parv[:, 4 + i, :], v.rearrange("(n p) -> p n", p=P)).then_inc(par_loaded, 16)
            sp.wait_ge(edge, 2)
            for i in range(3):
                n = 3 * RW_TILES + i
                sp.dma_start(low[i][:, 1:T + 1], zT[n * P:(n + 1) * P, :]).then_inc(low_loaded, 16)
            for i in range(3):
                sp.dma_start(zin[i][:, 1:T + 1], zT[i * C_RW:i * C_RW + P, :]).then_inc(z_loaded, 16)

            def store(c, here):
                for d in range(2):
                    sp.wait_ge(dves, V(f"b{d}", c) + V0.n)
                    sp.dma_start(row(ops[d], here, P), res[d][:]).then_inc(stored[d], 16)
                    sp.wait_ge(cut, c * 2 + 2)
                    sp.dma_start(row(end_decay[d], here, P), dec[d][:]).then_inc(stored[d], 16)
                sp.dma_start(row(vals, here, P), rkv[2][:]).then_inc(kept, 16)
                sp.wait_ge(dves, V("bv", c) + V0.n)
                sp.dma_start(row(bonus, here, P), bon[:]).then_inc(kept, 16)
                for s in stored + [kept]:
                    sp.wait_ge(s, c * 32 + 32)
                sp.sem_inc(results_left, 1)

            sp.sem_inc(results_left, 1)
            with sp.Fori(0, RW_TILES - 1) as c:
                here, first = sp.snap(c * P), sp.snap(c * P + P)
                sources = [row(zT[i * C_RW:(i + 1) * C_RW], first, P) for i in range(3)]
                sp.wait_ge(dves, V("rv", c) + V0.n)
                for i in range(3):
                    sp.dma_start(zin[i][:, 1:T + 1], sources[i]).then_inc(z_loaded, 16)
                store(c, here)
            store(RW_TILES - 1, (RW_TILES - 1) * P)

        @block.gpsimd
        def _(pool):
            for t in low + zin:
                pool.memset(t[:, 0:1], 0.0)
                last = pool.memset(t[:, T + 1:T + 2], 0.0)
            last.then_inc(edge, 1)
            for t in lw_w:
                last = pool.memset(t[:], 0.0)
            last.then_inc(edge, 1)
            pool.wait_ge(acts, A0("sig"))
            pool.dma_start(gate_in, low[2][:, 1:T + 1]).then_inc(low_stored, 16)
            pool.wait_ge(low_stored, 16)
            with pool.Fori(0, RW_TILES) as c:
                line = Line(pool, pools, G, c)
                tt = lambda out, x, y, op: pool.tensor_tensor(out, x, y, op)
                pool.wait_ge(z_loaded, c * 48 + 48)
                pool.sem_inc(passed, 1)
                for x, i in (("k", 1), ("r", 0), ("v", 2)):
                    line(f"s{x}", tt(neighbours[i][:], zin[i][:, 0:T], zin[i][:, 2:T + 2], ALU.add))
                pool.wait_ge(dves, V("kd1", c) + V0.n)
                pool.sem_inc(passed, 1)
                line("kb", tt(ksum[:], kdir[0][:], kdir[1][:], ALU.add))
                line("q0", tt(ksum[:], ksum[:], rkv[0][:], ALU.mult))
                pool.wait_ge(dves, V("kk", c) + V0.n)
                pool.sem_inc(passed, 1)
                for d in range(2):
                    line(f"bb{d}", tt(rate[d][:], kk[:], rate[d][:], ALU.mult))
                for d in range(2):
                    pool.wait_ge(acts, A(f"dc{d}", c) + A0.n)
                    pool.sem_inc(passed, 1)
                    last = (NCH - 1) * (1 - d)
                    pool.memset(dec[d][:, last:last + 1], 0.0).then_inc(cut, 1)

        def shift(line, names, src, out, scr, n):
            line(names[0], nc.vector.tensor_tensor(scr[:], src[:, 0:T], src[:, 2:T + 2], ALU.add))
            line(names[1], nc.vector.tensor_scalar(scr[:], scr[:], mixc[:, 2, n], None, ALU.mult))
            line(names[2], nc.vector.scalar_tensor_tensor(out=out, in0=src[:, 1:T + 1], scalar=mixc[:, 1, n],
                                                          in1=scr[:], op0=ALU.mult, op1=ALU.add))

        @block.vector
        def _(dve):
            line = Line(dve, dves, V0)
            dve.wait_ge(par_loaded, 16 * 8)
            line("one_minus", nc.vector.tensor_scalar(mixc[:, 1, :], mixc[:, 0, :], -1.0, 1.0, ALU.mult, ALU.add))
            line("half", nc.vector.tensor_scalar(mixc[:, 2, :], mixc[:, 0, :], 0.5, None, ALU.mult))
            dve.wait_ge(low_loaded, 48)
            for i in range(3):
                n = 3 * RW_TILES + i
                shift(line, (f"s{i}", f"m{i}", f"o{i}"), low[i], low[i][:, 1:T + 1], tmp[0], slice(n, n + 1))
            line("omka", nc.vector.tensor_scalar(parv[:, 7, :], parv[:, 5, :], -1.0, 1.0, ALU.mult, ALU.add))
            with dve.Fori(0, RW_TILES) as c:
                line = Line(dve, dves, V, c, V0.n)
                mul = lambda out, x, y: nc.vector.tensor_tensor(out, x, y, ALU.mult)
                col = lambda j: parv[:, j, bass.ds(c, 1)]
                r, ky, v = rkv

                def shifted(x, i):
                    n = bass.ds(c + i * RW_TILES, 1)
                    dve.wait_ge(pools, G(f"s{x}", c))
                    line(f"m{x}", nc.vector.tensor_scalar(neighbours[i][:], neighbours[i][:], mixc[:, 2, n], None,
                                                          ALU.mult))
                    line(f"r{x}", nc.vector.scalar_tensor_tensor(out=rkv[i][:], in0=zin[i][:, 1:T + 1],
                                                                 scalar=mixc[:, 1, n], in1=neighbours[i][:],
                                                                 op0=ALU.mult, op1=ALU.add))

                shifted("k", 1)
                line("kkr", nc.vector.tensor_scalar(tmp[1][:], ky[:], col(4), None, ALU.mult))
                line("sq", mul(tmp[2][:], tmp[1][:], tmp[1][:]))
                shifted("r", 0)
                chunks = lambda t: t[:].rearrange("p (c s) -> p c s", s=CHUNK)
                for d in range(2):
                    dve.wait_ge(acts, A0.n + A(f"sw{d}", c))
                    line(f"scan{d}", nc.vector.tensor_tensor_scan(acc[d][:], k.scan_keep[:], soft[d][:], 0.0,
                                                                  ALU.mult, ALU.add))
                    if d == 0:
                        line("exc0", nc.vector.tensor_tensor(exc[0][:], acc[0][:], soft[0][:], ALU.subtract))
                    else:
                        line("tot1", nc.vector.tensor_copy(tot[:], chunks(acc[1])[:, :, CHUNK - 1]))
                        line("exc1", nc.vector.tensor_tensor(chunks(exc[1]),
                                                             tot[:].unsqueeze(2).to_broadcast([P, NCH, CHUNK]),
                                                             chunks(acc[1]), ALU.subtract))
                        line("inc1", nc.vector.tensor_tensor(acc[1][:], exc[1][:], soft[1][:], ALU.add))
                for d in range(2):
                    dve.wait_ge(acts, A0.n + A(f"sa{d}", c))
                    line(f"m{d}", nc.vector.tensor_scalar(tmp[0][:], rate[d][:], col(5), col(7), ALU.mult, ALU.add))
                    line(f"kd{d}", mul(kdir[d][:], tmp[0][:], ky[:]))
                dve.wait_ge(acts, A0.n + A("root", c))
                line("kkinv", nc.vector.reciprocal(norm[:], norm[:]))
                line("wide", nc.vector.tensor_copy(tmp[2][:].rearrange("p (n e) -> p n e", e=HEAD),
                                                   norm[:].unsqueeze(2).to_broadcast([P, 2 * NT, HEAD])))
                dve.wait_ge(results_left, c + 1)
                shifted("v", 2)
                dve.wait_ge(pes, M("kk", c))
                line("kk", mul(kk[:], tmp[1][:], psC[:]))
                for d in range(2):
                    dve.wait_ge(acts, A0.n + A(f"dc{d}", c))
                    line(f"r{d}", mul(res[d][:, 1, :], r[:], grow[d][:]))
                    line(f"k{d}", mul(res[d][:, 3, :], kdir[d][:], shrink[d][:]))
                    line(f"a{d}", nc.vector.scalar_tensor_tensor(out=res[d][:, 0, :], in0=exc[d][:], scalar=-1.0,
                                                                 in1=kk[:], op0=ALU.mult, op1=ALU.mult))
                    if d == 0:
                        dve.wait_ge(pools, G("q0", c))
                        line("q1", nc.vector.tensor_scalar(ksum[:], ksum[:], col(6), 0.5, ALU.mult, ALU.mult))
                for d in range(2):
                    dve.wait_ge(pools, G(f"bb{d}", c))
                    line(f"b{d}", mul(res[d][:, 2, :], rate[d][:], shrink[d][:]))
                dve.wait_ge(pes, M("bonus", c))
                line("bv", mul(bon[:], psD[:], v[:]))

        @block.scalar
        def _(act):
            line = Line(act, acts, A0)
            act.wait_ge(dves, V0("omka"))
            line("tanh", nc.scalar.activation(low[0][:, 1:T + 1], low[0][:, 1:T + 1], ACT.Tanh))
            line("sig", nc.scalar.activation(low[2][:, 1:T + 1], low[2][:, 1:T + 1], ACT.Sigmoid))
            with act.Fori(0, RW_TILES) as c:
                act.wait_ge(edge, 2)
                for d in range(2):
                    half = slice(d * LORA, (d + 1) * LORA)
                    act.dma_start(lw_w[d][half, :], w2[d][:, bass.ds(c * P, P)]).then_inc(lora_loaded, 16)
                    act.dma_start(lw_w[2 + d][half, :], a2[d][:, bass.ds(c * P, P)]).then_inc(lora_loaded, 16)
                line = Line(act, acts, A, c, A0.n)
                vdone = lambda name: V0.n + V(name, c)
                col = lambda j: parv[:, j, bass.ds(c, 1)]
                for d in range(2):
                    act.wait_ge(pes, M(f"w{d}", c))
                    act.wait_ge(dves, V0.n + c * V.n)
                    line(f"sw{d}", nc.scalar.activation(soft[d][:], psA[:], ACT.Sigmoid, bias=col(d)))
                    act.wait_ge(pes, M(f"a{d}", c))
                    line(f"sa{d}", nc.scalar.activation(rate[d][:], psB[:], ACT.Sigmoid, bias=col(2 + d)))
                act.wait_ge(pes, M("norm", c))
                line("root", nc.scalar.activation(norm[:], psC[:, 0:2 * NT], ACT.Sqrt, bias=k.eps[:, 1:2]))
                for d in range(2):
                    act.wait_ge(dves, vdone("exc0" if d == 0 else "inc1"))
                    act.wait_ge(results_left, c + 1)
                    line(f"ex{d}", nc.scalar.activation(exc[d][:], exc[d][:], ACT.Exp, scale=-DECAY))
                    line(f"in{d}", nc.scalar.activation(grow[d][:], acc[d][:], ACT.Exp, scale=-DECAY))
                    line(f"en{d}", nc.scalar.activation(shrink[d][:], acc[d][:], ACT.Exp, scale=DECAY))
                    end = CHUNK - 1 if d == 0 else 0
                    line(f"dc{d}", nc.scalar.activation(
                        dec[d][:], acc[d][:].rearrange("p (c s) -> p c s", s=CHUNK)[:, :, end], ACT.Exp,
                        scale=-DECAY))

        @block.tensor
        def _(pe):
            def both(ps, lhsT, rhs):
                for h in range(2):
                    last = nc.tensor.matmul(ps[:, h * HALF:(h + 1) * HALF], lhsT, rhs[:, h * HALF:(h + 1) * HALF],
                                            start=True, stop=True)
                last.then_inc(pes, 1)

            with pe.Fori(0, RW_TILES) as c:
                pe.wait_ge(lora_loaded, c * 64 + 64)
                pe.wait_ge(acts, A0.n + c * A.n)
                both(psA, lw_w[0][:], low[0][:, 1:T + 1])
                both(psB, lw_w[2][:], low[1][:, 1:T + 1])
                pe.wait_ge(dves, V0.n + V("sq", c))
                for n in range(NT):
                    last = nc.tensor.matmul(psC[:, 2 * n:2 * n + 2], tmp[2][:, n * P:(n + 1) * P], k.chunk_col[:],
                                            start=True, stop=True)
                last.then_inc(pes, 1)
                pe.wait_ge(acts, A0.n + A("sa0", c))
                both(psA, lw_w[1][:], low[0][:, 1:T + 1])
                both(psB, lw_w[3][:], low[1][:, 1:T + 1])
                pe.wait_ge(dves, V0.n + V("wide", c))
                for n in range(NT):
                    last = nc.tensor.matmul(psC[:, n * P:(n + 1) * P], tmp[2][:, n * P:(n + 1) * P], k.ident[:],
                                            start=True, stop=True)
                last.then_inc(pes, 1)
                pe.wait_ge(dves, V0.n + V("q1", c))
                both(psD, k.head_ones[:], ksum[:])


def rwkv_scan(nc, k, ops, vals, end_decay, y, yb):
    PAIRS = T // P
    UNITS = RW_TILES * PAIRS
    with ExitStack() as ctx:
        sb = lambda name, shape, dt=F32: ctx.enter_context(nc.sbuf_tensor(name, shape, dt))
        sem = lambda name: ctx.enter_context(nc.semaphore(name))
        dirs, slots = range(2), range(2)
        opt = [[sb(f"opt{s}{d}", [P, 4, P]) for d in dirs] for s in slots]
        byhead = [[sb(f"byhead{s}{d}", [P, 4, P]) for d in dirs] for s in slots]
        vc = [[sb(f"vc{s}{d}", [P, P]) for d in dirs] for s in slots]
        ended = [[sb(f"ended{s}{d}", [P, 2]) for d in dirs] for s in slots]
        r_kept = [sb(f"r_kept{s}", [P, 2, P]) for s in slots]
        end_kept = [sb(f"end_kept{s}", [P, 2, 2]) for s in slots]
        vt = [sb(f"vt{s}", [P, 2, P]) for s in slots]
        bk = [sb(f"bk{s}", [P, 2, 2, 2, P]) for s in slots]
        xa = [sb(f"xa{s}", [P, 2, 2, 2, HEAD]) for s in slots]
        kj = [sb(f"kj{s}", [P, 2, 4, P]) for s in slots]
        bj = [sb(f"bj{s}", [P, 2, 4, P]) for s in slots]
        X5 = [sb(f"X_5{s}", [P, 4, P]) for s in slots]
        yo = [sb(f"yo{s}", [P, 2, P]) for s in slots]
        U = lambda name: sb(name, [P, 4, P])
        E0, X0, X1, X2, X3, X4 = (U(f"X_{n}") for n in "e01234")
        D0, N1, N2, D1, E1, D2, E2, D3, Z1, Z2, T3, T4 = (U(f"N_{n}") for n in range(12))
        ua = sb("ua", [P, 2, 2, 2, HEAD])
        ya = sb("ya", [P, 2, 2, 2, HEAD])
        mt = sb("mt", [P, 2, 2, P])
        mt1 = sb("mt1", [P, 4, P])
        rt = [[sb(f"rt{d}{c}", [P, P]) for c in range(2)] for d in dirs]
        st = [[sb(f"st{d}{n}", [P, P]) for n in range(2)] for d in dirs]
        pb = [ctx.enter_context(nc.psum_tensor(f"pb{n}", [P, HALF], F32)) for n in range(8)]
        loaded = [sem(f"unit_loaded{s}") for s in slots]
        slot_free = [sem(f"slot_free{s}") for s in slots]
        y_stored = [sem(f"y_stored{s}") for s in slots]
        yo_free = sem("yo_free")
        yb_zeroed = sem("yb_zeroed")
        zeroed, cleared, passed = sem("zeroed"), sem("cleared"), sem("s_passed")
        mt1_made = sem("mt1_made")
        kept, x0_made = sem("kept_r"), sem("x0_made")
        front_act, front_dve, front_pe = sem("front_act"), sem("front_dve"), sem("front_pe")
        start_act, start_dve, start_pe = sem("start_act"), sem("start_dve"), sem("start_pe")
        rest_act, rest_dve, rest_pe = sem("rest_act"), sem("rest_dve"), sem("rest_pe")
        SA = Steps("ta0 tv0 b00 b01 ta1 tv1 b10 b11")
        SV = Steps("kj0 kj1 bj0 bj1 e0")
        SP = Steps("tm0 tm1 kj0 kj1 bj0 bj1")
        FA = Steps("d1 e1 d2 e2 d3 z1 t3 xv z2 t4")
        FV = Steps("d0 n1 n2 x1 x2 x3 x4 x5")
        FP = Steps("dt d1 e1 d2 e2 x1 d3 x2 x3 z1 t3 x4 xv z2 t4 x5")
        RA = Steps("ua0 ua1 ya0 ya1")
        RV = Steps("mt rt00 rt01 rt10 rt11 mid0 mid1 y0 y1 end0 end1")
        RP = Steps("ua mt yr rt mid0 mid1 end0 end1 y0 y1")
        by_unit = lambda ps, d: ps[:, d * 2 * P:(d + 1) * 2 * P].rearrange("p (h k e) -> p h k e", h=2, k=2)
        quad = lambda ps: ps[:].rearrange("p (u n) -> p u n", u=4)
        four = lambda m: m.unsqueeze(1).to_broadcast([P, 4, P])
        block = ctx.enter_context(nc.Block())

        def rounds(eng, start, body):
            start(0, 0)
            body(0, 0, True, False, True)
            with eng.Fori(0, UNITS // 2 - 1) as j:
                body(1, j * 2 + 1, True, True, True)
                body(0, j * 2 + 2, True, True, True)
            body(1, UNITS - 1, True, True, False)
            body(0, UNITS, False, True, False)

        @block.sync
        def _(sp):
            with sp.Fori(0, RW_TILES) as c:
                with sp.Fori(0, PAIRS // 2) as j:
                    for s in slots:
                        chan = sp.snap(c * P)
                        t0 = (sp.snap(j * (2 * P) + s * P), sp.snap(j * (-2 * P) + (PAIRS - 1 - s) * P))
                        ch0 = (sp.snap(j * 4 + s * 2), sp.snap(j * -4 + (PAIRS - 1 - s) * 2))
                        sp.wait_ge(slot_free[s], c * (PAIRS // 2) + j + 1)
                        for d in dirs:
                            tok = bass.ds(t0[d], P)
                            src = row(ops[d], chan, P)[:, :, tok]
                            sp.dma_start(opt[s][d][:], src).then_inc(loaded[s], 16)
                            for h in range(2):
                                rows = slice(h * HEAD, (h + 1) * HEAD)
                                sp.dma_start(byhead[s][d][rows, 2 * h:2 * h + 2, :],
                                             row(ops[d, h * HEAD:], chan, HEAD)[:, 0:2, tok]).then_inc(loaded[s], 16)
                            sp.dma_start(vc[s][d][:], row(vals, chan, P)[:, tok]).then_inc(loaded[s], 16)
                            sp.dma_start(ended[s][d][:],
                                         row(end_decay[d], chan, P)[:, bass.ds(ch0[d], 2)]).then_inc(loaded[s], 16)

        @block.gpsimd
        def _(pool):
            for s in slots:
                for d in dirs:
                    pool.memset(byhead[s][d][:], 0.0)
            for d in dirs:
                for c in range(2):
                    last = pool.memset(rt[d][c][:], 0.0)
            last.then_inc(zeroed, 1)
            pool.wait_ge(zeroed, 1)
            for s in slots:
                pool.sem_inc(slot_free[s], 1)
            pool.sem_inc(yo_free, 2)

            def front(s, i, nth):
                pool.wait_ge(loaded[s], nth * 160 + 160)
                pool.sem_inc(passed, 1)
                for d in dirs:
                    pool.tensor_copy(r_kept[s][:, d, :], opt[s][d][:, 1, :])
                    last = pool.tensor_copy(end_kept[s][:, d, :], ended[s][d][:])
                last.then_inc(kept, 1)
                pool.wait_ge(kept, i + 1)
                pool.wait_ge(start_pe, SP("bj1", i))
                pool.sem_inc(slot_free[s], 1)
                pool.wait_ge(start_dve, SV("e0", i))
                pool.tensor_tensor(X0[:], E0[:], four(k.ident[:]), ALU.add).then_inc(x0_made, 1)

            def store(s, i, c, j, nth):
                pool.wait_ge(rest_dve, RV("mt", i))
                pool.tensor_tensor(mt1[:], mt[:].rearrange("p d c n -> p (d c) n"), four(k.ident[:]), ALU.add
                                   ).then_inc(mt1_made, 1)
                pool.wait_ge(rest_dve, RV("end1", i))
                for d in dirs:
                    t0 = j * (2 * P) + s * P if d == 0 else j * (-2 * P) + (PAIRS - 1 - s) * P
                    pool.dma_start(row(y[d], t0, P)[:, bass.ds(c * P, P)], yo[s][:, d, :]).then_inc(y_stored[s], 16)
                pool.wait_ge(y_stored[s], nth * 32 + 32)
                pool.sem_inc(yo_free, 1)

            front(0, 0, 0)
            with pool.Fori(0, RW_TILES - 1) as c:
                with pool.Fori(0, PAIRS // 2) as j:
                    n = c * (PAIRS // 2) + j
                    front(1, n * 2 + 1, n)
                    store(0, n * 2, c, j, n)
                    front(0, n * 2 + 2, n + 1)
                    store(1, n * 2 + 1, c, j, n)
            c, n0 = RW_TILES - 1, (RW_TILES - 1) * (PAIRS // 2)
            with pool.Fori(0, PAIRS // 2 - 1) as j:
                n = j + n0
                front(1, n * 2 + 1, n)
                store(0, n * 2, c, j, n)
                front(0, n * 2 + 2, n + 1)
                store(1, n * 2 + 1, c, j, n)
            j = PAIRS // 2 - 1
            front(1, UNITS - 1, n0 + j)
            store(0, UNITS - 2, c, j, n0 + j)
            store(1, UNITS - 1, c, j, n0 + j)

        @block.scalar
        def _(act):
            def zero_rows(first, blocks):
                act.dma_start(row(yb, first, blocks * P).rearrange("(n p) d -> p n d", p=P),
                              k.zeros[:].unsqueeze(1).to_broadcast([P, blocks, D])).then_inc(yb_zeroed, 16)

            def transposes(d, s, i):
                line = Line(act, start_act, SA, i)
                line.at = d * SA.n // 2
                ps = quad(pb[7 - 2 * d])
                act.wait_ge(start_pe, SP(f"tm{d}", i))
                line(f"ta{d}", nc.scalar.copy(xa[s][:, d, :, 1, :], ps[:, 0, :].rearrange("p (h e) -> p h e", h=2)))
                line(f"tv{d}", nc.scalar.copy(vt[s][:, d, :], ps[:, 3, :]))
                for c in range(2):
                    line(f"b{d}{c}", nc.scalar.activation(bk[s][:, d, c, :, :], ps[:, 1:3, :], ACT.Copy,
                                                          scale=k.chunk_col[:, c:c + 1]))

            def start(s, i):
                for d in dirs:
                    transposes(d, s, i)

            def body(s, i, front, rest, more):
                line = Line(act, front_act, FA, i)
                after = Line(act, rest_act, RA, i - 1)

                def copied(name, out, ps):
                    act.wait_ge(front_pe, FP(name, i))
                    line(name, nc.scalar.copy(out[:], quad(ps)))

                if rest:
                    act.wait_ge(rest_pe, RP("ua", i - 1))
                    for d in dirs:
                        after(f"ua{d}", nc.scalar.copy(ua[:, d, :, :, :].rearrange("p k h e -> p h k e"),
                                                       by_unit(pb[6], d)))
                if front:
                    copied("d1", D1, pb[4])
                    copied("e1", E1, pb[2])
                if rest:
                    act.wait_ge(rest_pe, RP("yr", i - 1))
                    for d in dirs:
                        after(f"ya{d}", nc.scalar.copy(ya[:, d, :, :, :].rearrange("p k h e -> p h k e"),
                                                       by_unit(pb[5], d)))
                if front:
                    for name, out, n in (("d2", D2, 0), ("e2", E2, 1), ("d3", D3, 4), ("z1", Z1, 1), ("t3", T3, 3)):
                        copied(name, out, pb[n])
                if more:
                    transposes(0, 1 - s, i + 1)
                if front:
                    act.wait_ge(front_pe, FP("xv", i))
                    line("xv", nc.scalar.copy(xa[s][:, :, :, 0, :],
                                              pb[3][:, 0:4 * HEAD].rearrange("p (d h e) -> p d h e", d=2, h=2)))
                    copied("z2", Z2, pb[2])
                    copied("t4", T4, pb[0])
                if more:
                    transposes(1, 1 - s, i + 1)

            LOOPS = UNITS // 2 - 1
            per_loop = ROWS // P // LOOPS
            start(0, 0)
            body(0, 0, True, False, True)
            with act.Fori(0, LOOPS) as j:
                zero_rows(j * per_loop * P, per_loop)
                body(1, j * 2 + 1, True, True, True)
                body(0, j * 2 + 2, True, True, True)
            zero_rows(LOOPS * per_loop * P, ROWS // P - LOOPS * per_loop)
            body(1, UNITS - 1, True, True, False)
            body(0, UNITS, False, True, False)
            act.wait_ge(yb_zeroed, 16 * (LOOPS + 1))

        @block.vector
        def _(dve):
            def masked(out, ps, mask):
                return nc.vector.tensor_tensor(out, ps, mask, ALU.mult)

            def chunk_matrix(at, s, i):
                line = Line(dve, start_dve, SV, i)
                line.at = at
                nm, t, n, d = (("kj0", kj, 6, 0), ("kj1", kj, 4, 1), ("bj0", bj, 2, 0), ("bj1", bj, 7, 1))[at]
                dve.wait_ge(start_pe, SP(nm, i))
                line(nm, masked(t[s][:, d, :, :], quad(pb[n]), k.causal[:, d, :, :]))
                if nm == "bj1":
                    e_all = bj[s][:].rearrange("p d (h k) i -> p d h k i", k=2)[:, :, :, 0, :]
                    line("e0", masked(E0[:].rearrange("p (d h) i -> p d h i", d=2), e_all,
                                      k.near[:, 0, :].unsqueeze(1).unsqueeze(1).to_broadcast([P, 2, 2, P])))

            def start(s, i):
                for at in range(4):
                    chunk_matrix(at, s, i)

            def body(s, i, front, rest, more):
                line, r = Line(dve, front_dve, FV, i), 1 - s
                after = Line(dve, rest_dve, RV, i - 1)

                def added(name, out, ps, x):
                    dve.wait_ge(front_pe, FP(name, i))
                    line(name, nc.vector.tensor_tensor(out[:], quad(ps), x[:], ALU.add))

                def moved(name, ps, n):
                    for d in dirs:
                        c = n if d == 0 else 1 - n
                        after(f"{name}{d}", nc.vector.scalar_tensor_tensor(
                            out=st[d][1 - n][:], in0=ps[:, d * P:(d + 1) * P], scalar=end_kept[r][:, d, c:c + 1],
                            in1=k.head_ones[:], op0=ALU.mult, op1=ALU.mult))

                if front:
                    dve.wait_ge(front_pe, FP("dt", i))
                    for n, (nm, out) in enumerate((("d0", D0), ("n1", N1), ("n2", N2))):
                        line(nm, masked(out[:], quad(pb[3]), four(k.near[:, n, :])))
                if rest:
                    dve.wait_ge(rest_pe, RP("mt", i - 1))
                    after("mt", masked(mt[:].rearrange("p d c n -> p (d c) n"), quad(pb[7]), four(k.head_ones[:])))
                if front:
                    dve.wait_ge(x0_made, i + 1)
                    added("x1", X1, pb[3], X0)
                if rest:
                    dve.wait_ge(rest_pe, RP("rt", i - 1))
                    dve.wait_ge(kept, i)
                    for d in dirs:
                        for c in range(2):
                            cols = slice(c * CHUNK, (c + 1) * CHUNK)
                            after(f"rt{d}{c}", nc.vector.tensor_tensor(
                                rt[d][c][:, cols], pb[6][:, d * P + c * CHUNK:d * P + (c + 1) * CHUNK],
                                r_kept[r][:, d, cols], ALU.add))
                if rest:
                    dve.wait_ge(rest_pe, RP("mid1", i - 1))
                    moved("mid", pb[7], 0)
                if front:
                    added("x2", X2, pb[2], X1)
                if front:
                    added("x3", X3, pb[0], X2)
                if rest:
                    dve.wait_ge(rest_pe, RP("y1", i - 1))
                    dve.wait_ge(rest_act, RA("ya1", i - 1))
                    dve.wait_ge(yo_free, i)
                    for d in dirs:
                        after(f"y{d}", nc.vector.tensor_tensor(
                            yo[r][:, d, :], pb[6][:, d * P:(d + 1) * P],
                            ya[:, d, 0, :, :].rearrange("p h e -> p (h e)"), ALU.add))
                    moved("end", pb[5], 1)
                if front:
                    added("x4", X4, pb[4], X3)
                if more:
                    chunk_matrix(0, 1 - s, i + 1)
                if front:
                    added("x5", X5[s], pb[1], X4)
                if more:
                    for at in (1, 2, 3):
                        chunk_matrix(at, 1 - s, i + 1)

            for d in dirs:
                nc.vector.memset(st[d][0][:], 0.0).then_inc(cleared, 1)
            rounds(dve, start, body)

        @block.tensor
        def _(pe):
            mm = lambda out, lhsT, rhs, start=True, stop=True: nc.tensor.matmul(
                out, lhsT, rhs, start=start, stop=stop)
            flat = lambda t: t.rearrange("p h e -> p (h e)")
            of = lambda t: (lambda u: t[:, u, :])

            def each(ps, lhsT, rhs, width=P):
                for u in range(4):
                    last = mm(pb[ps][:, u * width:(u + 1) * width], lhsT(u), rhs(u))
                return last

            def turned(ps, src):
                for u in range(4):
                    last = nc.tensor.transpose(pb[ps][:, u * P:(u + 1) * P], src(u), k.ident[:])
                return last

            sp = lambda instruction: instruction.then_inc(start_pe, 1)

            def transposes(d, s):
                for n, src in enumerate((opt[s][d][:, 0, :], opt[s][d][:, 2, :], opt[s][d][:, 3, :], vc[s][d][:])):
                    last = nc.tensor.transpose(pb[7 - 2 * d][:, n * P:(n + 1) * P], src, k.ident[:])
                sp(last)

            def chunk_matrix(at, s):
                ps, n, d = ((6, 3, 0), (4, 3, 1), (2, 2, 0), (7, 2, 1))[at]
                sp(mm(pb[ps][:], opt[s][d][:, n, :], byhead[s][d][:].rearrange("p m i -> p (m i)")))

            def body(s, i, front, rest, more):
                r = 1 - s
                fa = lambda name: pe.wait_ge(front_act, FA(name, i))
                fv = lambda name: pe.wait_ge(front_dve, FV(name, i))
                ra = lambda name: pe.wait_ge(rest_act, RA(name, i - 1))
                rv = lambda name: pe.wait_ge(rest_dve, RV(name, i - 1))
                fp = lambda instruction: instruction.then_inc(front_pe, 1)
                rp = lambda instruction: instruction.then_inc(rest_pe, 1)

                def state(ps, n):
                    for d in dirs:
                        c = n if d == 0 else 1 - n
                        out = pb[ps][:, d * P:(d + 1) * P]
                        mm(out, bk[r][:, d, c, 0, :], flat(ua[:, d, 0, :, :]), True, False)
                        mm(out, bk[r][:, d, c, 1, :], vt[r][:, d, :], False, False)
                        rp(mm(out, mt1[:, 2 * d + c, :], st[d][n][:], False, True))

                if rest:
                    pe.wait_ge(front_act, FA("t4", i - 1))
                    pe.wait_ge(front_dve, FV("x5", i - 1))
                    if front:
                        pe.wait_ge(start_dve, SV("kj0", i))
                    rp(each(6, of(X5[r]), lambda u: xa[r][:, u // 2, u % 2, :, :].rearrange("p k e -> p (k e)")))
                if front:
                    pe.wait_ge(start_dve, SV("bj1", i))
                    if not rest:
                        pe.wait_ge(start_act, SA("b11", i))
                    fp(turned(3, lambda u: bj[s][:, u // 2, 2 * (u % 2), :]))
                if rest:
                    ra("ua1")
                    if front:
                        pe.wait_ge(start_act, SA("b11", i))
                    for d in dirs:
                        last = mm(pb[7][:, d * 2 * P:(d + 1) * 2 * P], flat(ua[:, d, 1, :, :]), bk[r][:, d, :, 0, :])
                    rp(last)
                if front:
                    fv("d0")
                    pe.wait_ge(start_dve, SV("e0", i))
                    fp(each(4, of(E0), of(D0)))
                    fp(each(2, of(D0), of(E0)))
                if rest:
                    for u in range(4):
                        d, h = u // 2, u % 2
                        mm(pb[5][:, u * P:(u + 1) * P], bj[r][:, d, 2 * h + 1, :], ua[:, d, :, h, :], True, False)
                        last = mm(pb[5][:, u * P:u * P + HEAD], kj[r][:, d, 2 * h + 1, :],
                                  vt[r][:, d, h * HEAD:(h + 1) * HEAD], False, True)
                    rp(last)
                if front:
                    fa("e1")
                    fv("n2")
                    pe.wait_ge(x0_made, i + 1)
                    fp(each(0, of(E1), of(D1)))
                    fp(each(1, of(D1), of(E1)))
                    fp(each(3, of(D1), of(X0)))
                if rest:
                    ra("ya1")
                    for d in dirs:
                        last = nc.tensor.transpose(pb[6][:, d * P:(d + 1) * P], flat(ya[:, d, 1, :, :]), k.ident[:])
                    rp(last)
                    pe.wait_ge(mt1_made, i)
                    if not front:
                        rv("rt11")
                    state(7, 0)
                if front:
                    fa("e2")
                    fp(each(4, of(E2), of(D2)))
                    fv("x1")
                    fp(each(2, of(D2), of(X1)))
                if rest:
                    rv("mid1")
                    state(5, 1)
                if front:
                    fa("d3")
                    fv("x2")
                    fp(each(0, of(D3), of(X2)))
                if rest:
                    for d in dirs:
                        out = pb[6][:, d * P:(d + 1) * P]
                        mm(out, rt[d][d][:], st[d][0][:], True, False)
                        rp(mm(out, rt[d][1 - d][:], st[d][1][:], False, True))
                if front:
                    fv("x3")
                    fp(each(1, of(N1), of(X3)))
                    fp(turned(3, of(X3)))
                if more:
                    pe.wait_ge(loaded[1 - s], nth(1 - s, i + 1) * 160 + 160)
                    transposes(0, 1 - s)
                if front:
                    fa("t3")
                    fp(each(4, of(T3), of(Z1)))
                if more:
                    if rest:
                        rv("end1")
                    transposes(1, 1 - s)
                if front:
                    fp(each(3, lambda u: kj[s][:, u // 2, 2 * (u % 2), :],
                            lambda u: vt[s][:, u // 2, (u % 2) * HEAD:(u % 2 + 1) * HEAD], HEAD))
                    fv("x4")
                    fp(each(2, of(N2), of(X4)))
                    fp(turned(0, of(X4)))
                if more:
                    chunk_matrix(0, 1 - s)
                if front:
                    fa("t4")
                    fp(each(1, of(T4), of(Z2)))
                if more:
                    chunk_matrix(1, 1 - s)
                    chunk_matrix(2, 1 - s)
                    pe.wait_ge(start_act, SA("b01", i + 1))
                    chunk_matrix(3, 1 - s)

            def start(s, i):
                pe.wait_ge(loaded[s], 160)
                for d in dirs:
                    transposes(d, s)
                for at in range(3):
                    chunk_matrix(at, s)
                pe.wait_ge(start_act, SA("b01", i))
                chunk_matrix(3, s)

            pe.wait_ge(zeroed, 1)
            pe.wait_ge(cleared, 2)
            start(0, 0)
            nth = lambda s, i: 0
            body(0, 0, True, False, True)
            with pe.Fori(0, UNITS // 2 - 1) as j:
                nth = lambda s, i: j + 1
                body(1, j * 2 + 1, True, True, True)
                body(0, j * 2 + 2, True, True, True)
            body(1, UNITS - 1, True, True, False)
            body(0, UNITS, False, True, False)


E_DA = C_DA // DA_HEADS
QK = E_DA // 2


def differential_attention(nc, k, zT, q_gain, k_gain, lq1, lk1, lq2, lk2, sub_gain, oT):
    QT = NT
    with ExitStack() as ctx:
        sb = lambda name, shape, dt=F32: ctx.enter_context(nc.sbuf_tensor(name, shape, dt))
        sem = lambda name: ctx.enter_context(nc.semaphore(name))
        maps = range(2)
        zq, zk, zv = (sb(f"a{n}", [P, T]) for n in ("zq", "zk", "zv"))
        sq = sb("asq", [P, T])
        inv = sb("ainv", [P, 2, QT, 2])
        qm = [sb(f"qm{m}", [P, T]) for m in maps]
        kn = sb("kn", [P, T])
        vt = sb("avt", [P, NT, E_DA])
        gains = sb("gains", [P, 3])
        lam_in = sb("lam_in", [P, 4, QK])
        lam = sb("lam", [P, 8])
        far = sb("far", [P, 2 * T - P], I32)
        dist = sb("dist", [P, 2 * T - P])
        slope = sb("slope", [P, 2 * T - P])
        sc = [sb(f"sc{m}", [P, T]) for m in maps]
        pr = [sb(f"pr{m}", [P, T]) for m in maps]
        at = sb("at", [P, T])
        aT = [sb(f"aT{s}", [P, NT, P]) for s in range(2)]
        stats = sb("astats", [P, QT, 11])
        col = lambda t, i, n=1: stats[:, t, i:i + n]
        MAX, NEG, SUM, INV, FACTOR, ROOT, SCALE = 0, 2, 4, 6, 8, 9, 10
        carrier = sb("carrier", [P, 1])
        o_all = sb("o_all", [P, QT, E_DA])
        o_sq = sb("o_sq", [P, E_DA])
        oc = sb("oc", [P, T])
        ps = [ctx.enter_context(nc.psum_tensor(f"sp{m}", [P, T], F32)) for m in maps]
        tp = ctx.enter_context(nc.psum_tensor("atp", [P, T], F32))
        op = ctx.enter_context(nc.psum_tensor("aop", [P, HALF], F32))
        par, zl, made = sem("apar"), sem("azl"), sem("amade")
        acts, dves, pes, kept = sem("a_acts"), sem("a_dves"), sem("a_pes"), sem("a_kept")
        oc_free = sem("oc_free")
        A0 = Steps("e0 e1 gq go")
        V0 = Steps("p0 p1 fcopy fneg dist lamd lamn")
        ROUNDS = QT + 3

        def names(*parts):
            return " ".join(f"{n}_{i - back}" for i in range(ROUNDS) for back, text in parts
                            if 0 <= i - back < QT for n in text.split())

        A = Steps("rq rk bk v0 v1 slope " + names((3, "osq"), (0, "ex0 ex1"), (1, "at0 at1")) + " ort oT0 oT1")
        V = Steps("sqq sqk ir bq q0 q1 kn " + names((3, "oc"), (1, "rs f a1"), (0, "s0 n0 s1 n1")) + " orc on")
        M = Steps("nq nk v xq xk " + names((0, "s0 s1"), (1, "at"), (2, "o")) + " oT")
        narrow = lambda i: inv[:, i, :, :].rearrange("p t m -> p (t m)").unsqueeze(2).to_broadcast([P, 2 * QT, QK])
        wide = lambda i: sc[i][:].rearrange("p (n e) -> p n e", e=QK)
        block = ctx.enter_context(nc.Block())

        @block.sync
        def _(sp):
            with nc.allow_non_contiguous_dma(reason="gains as columns"):
                for m in maps:
                    rows = slice(m * QK, (m + 1) * QK)
                    sp.dma_start(gains[rows, 0:1], q_gain.rearrange("(p o) -> p o", o=1)).then_inc(par, 16)
                    sp.dma_start(gains[rows, 1:2], k_gain.rearrange("(p o) -> p o", o=1)).then_inc(par, 16)
                sp.dma_start(gains[:, 2:3], sub_gain.rearrange("(p o) -> p o", o=1)).then_inc(par, 16)
            for i, v in enumerate((lq1, lk1, lq2, lk2)):
                sp.dma_start(lam_in[:, i, :], v.rearrange("(o n) -> o n", o=1).to_broadcast([P, QK])).then_inc(par, 16)
            def load(h):
                first = sp.snap(h * P) if h is not None else 0
                return [row(zT[RW_COLS + i * C_DA:RW_COLS + (i + 1) * C_DA], first, P) for i in range(3)]

            for t, src in zip((zq, zk, zv), load(None)):
                sp.dma_start(t[:], src).then_inc(zl, 16)
            with sp.Fori(1, DA_HEADS) as h:
                sources = load(h)
                sp.wait_ge(dves, V("kn", h) + (V0.n - V.n))
                for t, src in zip((zq, zk, zv), sources):
                    sp.dma_start(t[:], src).then_inc(zl, 16)

        @block.gpsimd
        def _(pool):
            pool.memset(qm[0][:], 0.0)
            pool.memset(qm[1][:], 0.0)
            pool.iota(far[:], [[1, 2 * T - P]], base=-(T - P), channel_multiplier=-1).then_inc(made, 1)
            pool.sem_inc(oc_free, 1)
            with pool.Fori(0, DA_HEADS) as h:
                pool.wait_ge(acts, A0.n + A("oT1", h))
                pool.dma_start(row(oT, h * P + C_RW, P), oc[:]).then_inc(kept, 16)
                pool.wait_ge(kept, h * 16 + 16)
                pool.sem_inc(oc_free, 1)

        @block.vector
        def _(dve):
            line = Line(dve, dves, V0)
            dve.wait_ge(par, 16 * 9)
            for m in maps:
                line(f"p{m}", nc.vector.tensor_tensor_reduce(
                    lam_in[:, 2 * m, :], lam_in[:, 2 * m, :], lam_in[:, 2 * m + 1, :], 1.0, 0.0,
                    ALU.mult, ALU.add, lam[:, m:m + 1]))
            dve.wait_ge(made, 1)
            line("fcopy", nc.vector.tensor_copy(dist[:], far[:]))
            line("fneg", nc.vector.tensor_scalar(slope[:], dist[:], -1.0, None, ALU.mult))
            line("dist", nc.vector.tensor_tensor(dist[:], dist[:], slope[:], ALU.min))
            dve.wait_ge(acts, A0("e1"))
            line("lamd", nc.vector.tensor_tensor(lam[:, 4:5], lam[:, 3:4], lam[:, 2:3], ALU.subtract))
            line("lamn", nc.vector.tensor_scalar(lam[:, 5:6], lam[:, 4:5], -LAMBDA_INIT, None, ALU.add))
            with dve.Fori(0, DA_HEADS) as h:
                line = Line(dve, dves, V, h, V0.n)
                dve.wait_ge(zl, h * 48 + 48)
                line("sqq", nc.vector.tensor_tensor(sq[:], zq[:], zq[:], ALU.mult))
                line("sqk", nc.vector.tensor_tensor(at[:], zk[:], zk[:], ALU.mult))
                dve.wait_ge(acts, A0.n + A("rk", h))
                flat = lambda t: t[:].rearrange("p a t m -> p (a t m)")
                line("ir", nc.vector.reciprocal(flat(inv), flat(inv)))
                line("bq", nc.vector.tensor_copy(wide(0), narrow(0)))
                dve.wait_ge(pes, M("xq", h))
                for m in maps:
                    rows = slice(m * QK, (m + 1) * QK)
                    line(f"q{m}", nc.vector.scalar_tensor_tensor(
                        out=qm[m][rows, :], in0=zq[rows, :], scalar=gains[rows, 0:1], in1=ps[0][rows, :],
                        op0=ALU.mult, op1=ALU.mult))
                dve.wait_ge(pes, M("xk", h))
                line("kn", nc.vector.scalar_tensor_tensor(out=kn[:], in0=zk[:], scalar=gains[:, 1:2], in1=ps[1][:],
                                                          op0=ALU.mult, op1=ALU.mult))
                dve.wait_ge(acts, A0.n + A("slope", h))
                for i in range(ROUNDS):
                    t = i - 3
                    if 0 <= t:
                        dve.wait_ge(pes, M(f"o_{t}", h))
                        line(f"oc_{t}", nc.vector.tensor_scalar(o_all[:, t, :], op[:, 0:E_DA], col(t, INV), None, ALU.mult))
                    t = i - 1
                    if 0 <= t < QT:
                        dve.wait_ge(acts, A0.n + A(f"ex1_{t}", h))
                        if t:
                            dve.wait_ge(pes, M(f"at_{t - 1}", h))
                        line(f"rs_{t}", nc.vector.reciprocal(col(t, INV, 2), col(t, SUM, 2)))
                        line(f"f_{t}", nc.vector.tensor_scalar(col(t, FACTOR), col(t, INV + 1), lam[:, 5:6],
                                                               col(t, SUM), ALU.mult, ALU.mult))
                        line(f"a1_{t}", nc.vector.scalar_tensor_tensor(out=at[:], in0=pr[1][:], scalar=col(t, FACTOR),
                                                                       in1=pr[0][:], op0=ALU.mult, op1=ALU.add))
                    t = i
                    if t < QT:
                        at0 = (T - P) - t * P
                        for m in maps:
                            dve.wait_ge(pes, M(f"s{m}_{t}", h))
                            nc.vector.memset(carrier[:], 0.0)
                            line(f"s{m}_{t}", nc.vector.tensor_tensor_reduce(
                                sc[m][:], ps[m][:], dist[:, at0:at0 + T], 1.0, -3.0e38, ALU.add, ALU.max,
                                col(t, MAX + m)))
                            line(f"n{m}_{t}", nc.vector.tensor_scalar(col(t, NEG + m), col(t, MAX + m), -1.0, None,
                                                                      ALU.mult))
                dve.wait_ge(acts, A0.n + A("ort", h))
                line("orc", nc.vector.reciprocal(stats[:, :, SCALE], stats[:, :, ROOT]))
                line("on", nc.vector.tensor_tensor(o_all[:], o_all[:], stats[:, :, SCALE].unsqueeze(2).to_broadcast(
                    [P, QT, E_DA]), ALU.mult))

        @block.scalar
        def _(act):
            line = Line(act, acts, A0)
            act.wait_ge(dves, V0("p1"))
            for m in maps:
                line(f"e{m}", nc.scalar.activation(lam[:, 2 + m:3 + m], lam[:, m:m + 1], ACT.Exp))
            line("gq", nc.scalar.mul(gains[:, 0:1], gains[:, 0:1], QK ** -0.5))
            line("go", nc.scalar.mul(gains[:, 2:3], gains[:, 2:3], 1.0 - LAMBDA_INIT))
            with act.Fori(0, DA_HEADS) as h:
                line = Line(act, acts, A, h, A0.n)
                vdone = lambda name: V0.n + V(name, h)
                act.wait_ge(dves, V0.n + h * V.n)
                for i, n in enumerate("qk"):
                    act.wait_ge(pes, M(f"n{n}", h))
                    line(f"r{n}", nc.scalar.activation(inv[:, i, :, :].rearrange("p t m -> p (t m)"),
                                                       ps[i][:, 0:2 * QT], ACT.Sqrt, bias=k.eps[:, 0:1],
                                                       scale=1.0 / QK))
                act.wait_ge(dves, vdone("ir"))
                line("bk", nc.scalar.copy(wide(1), narrow(1)))
                act.wait_ge(pes, M("v", h))
                for n in range(2):
                    line(f"v{n}", nc.scalar.copy(vt[:].rearrange("p n e -> p (n e)")[:, n * HALF:(n + 1) * HALF],
                                                 tp[:, n * HALF:(n + 1) * HALF]))
                line("slope", nc.scalar.mul(dist[:], dist[:], 0.25))
                for i in range(ROUNDS):
                    t = i - 3
                    if 0 <= t:
                        act.wait_ge(dves, vdone(f"oc_{t}"))
                        line(f"osq_{t}", nc.scalar.activation(o_sq[:], o_all[:, t, :], ACT.Square,
                                                              accum_out=col(t, ROOT)))
                    t = i
                    if t < QT:
                        for m in maps:
                            act.wait_ge(dves, vdone(f"n{m}_{t}"))
                            line(f"ex{m}_{t}", nc.scalar.activation(pr[m][:], sc[m][:], ACT.Exp, bias=col(t, NEG + m),
                                                                    accum_out=col(t, SUM + m)))
                    t = i - 1
                    if 0 <= t < QT:
                        act.wait_ge(pes, M(f"at_{t}", h))
                        for n in range(2):
                            line(f"at{n}_{t}", nc.scalar.copy(
                                aT[t % 2][:].rearrange("p n e -> p (n e)")[:, n * HALF:(n + 1) * HALF],
                                tp[:, n * HALF:(n + 1) * HALF]))
                line("ort", nc.scalar.activation(stats[:, :, ROOT], stats[:, :, ROOT], ACT.Sqrt, bias=k.eps[:, 0:1],
                                                 scale=1.0 / E_DA))
                act.wait_ge(pes, M("oT", h))
                act.wait_ge(oc_free, h + 1)
                for n in range(2):
                    line(f"oT{n}", nc.scalar.mul(oc[:, n * HALF:(n + 1) * HALF], tp[:, n * HALF:(n + 1) * HALF],
                                                 gains[:, 2:3]))

        @block.tensor
        def _(pe):
            with pe.Fori(0, DA_HEADS) as h:
                adone = lambda name: A0.n + A(name, h)
                vdone = lambda name: V0.n + V(name, h)

                def both(out, lhsT, rhs):
                    for n in range(2):
                        last = nc.tensor.matmul(out[:, n * HALF:(n + 1) * HALF], lhsT,
                                                rhs[:, n * HALF:(n + 1) * HALF], start=True, stop=True)
                    last.then_inc(pes, 1)

                for i, (name, t) in enumerate((("sqq", sq), ("sqk", at))):
                    pe.wait_ge(dves, vdone(name))
                    for n in range(QT):
                        last = nc.tensor.matmul(ps[i][:, 2 * n:2 * n + 2], t[:, n * P:(n + 1) * P], k.chunk_col[:],
                                                start=True, stop=True)
                    last.then_inc(pes, 1)
                pe.wait_ge(acts, A0.n + h * A.n)
                for n in range(NT):
                    last = nc.tensor.transpose(tp[:, n * P:(n + 1) * P], zv[:, n * P:(n + 1) * P], k.ident[:])
                last.then_inc(pes, 1)
                for i in range(2):
                    pe.wait_ge(acts, adone("bk")) if i else pe.wait_ge(dves, vdone("bq"))
                    for n in range(QT):
                        last = nc.tensor.matmul(ps[i][:, n * P:(n + 1) * P],
                                                sc[i][:, n * P:(n + 1) * P], k.ident[:], start=True, stop=True)
                    last.then_inc(pes, 1)
                pe.wait_ge(dves, vdone("kn"))
                for i in range(ROUNDS):
                    t = i
                    if t < QT:
                        for m in maps:
                            if t:
                                pe.wait_ge(dves, vdone(f"s{m}_{t - 1}"))
                            both(ps[m], qm[m][:, t * P:(t + 1) * P], kn)
                    t = i - 1
                    if 0 <= t < QT:
                        if t:
                            pe.wait_ge(acts, adone(f"at1_{t - 1}"))
                        pe.wait_ge(dves, vdone(f"a1_{t}"))
                        for n in range(NT):
                            last = nc.tensor.transpose(tp[:, n * P:(n + 1) * P], at[:, n * P:(n + 1) * P], k.ident[:])
                        last.then_inc(pes, 1)
                    t = i - 2
                    if 0 <= t < QT:
                        pe.wait_ge(acts, adone(f"at1_{t}"))
                        if t:
                            pe.wait_ge(dves, vdone(f"oc_{t - 1}"))
                        for n in range(NT):
                            last = nc.tensor.matmul(op[:, 0:E_DA], aT[t % 2][:, n, :], vt[:, n, :],
                                                    start=(n == 0), stop=(n == NT - 1))
                        last.then_inc(pes, 1)
                pe.wait_ge(dves, vdone("on"))
                for t in range(QT):
                    last = nc.tensor.transpose(tp[:, t * P:(t + 1) * P], o_all[:, t, :], k.ident[:])
                last.then_inc(pes, 1)


def finish_rwkv(nc, k, y, bonus, gate_in, g2, ln_g, ln_b, oT, w_out, wo, wo_loaded):
    with ExitStack() as ctx:
        sb = lambda name, shape, dt=F32: ctx.enter_context(nc.sbuf_tensor(name, shape, dt))
        sem = lambda name: ctx.enter_context(nc.semaphore(name))
        slots = range(2)
        yf = [sb(f"yf{s}", [P, NT, P]) for s in slots]
        yb = [sb(f"yb{s}", [P, NT, P]) for s in slots]
        yc = sb("ycent", [P, NT, P])
        bv = [sb(f"bvt{s}", [P, T]) for s in slots]
        g2s = sb("g2s", [P, C_RW])
        gin = sb("gins", [P, T])
        gains = sb("lngains", [P, 2, RW_TILES])
        stat = sb("gnstat", [P, 3, NT * 2])
        oc = [sb(f"orw{s}", [P, T]) for s in slots]
        tp = [ctx.enter_context(nc.psum_tensor(f"gtp{s}", [P, T], F32)) for s in slots]
        gp = [ctx.enter_context(nc.psum_tensor(f"ggp{s}", [P, T], F32)) for s in slots]
        once, y_loaded = sem("once"), [sem(f"y_in{s}") for s in slots]
        o_stored = [sem(f"o_out{s}") for s in slots]
        oc_free = [sem(f"orw_free{s}") for s in slots]
        acts, dves, pes = sem("g_acts"), sem("g_dves"), sem("g_pes")
        A = Steps("root0 root1")
        V = Steps(" ".join(f"sum{s} mean{s} meand{s} cent{s} sq{s} var{s} inv{s} norm{s} aff{s} bon{s} gate{s}" for s in slots))
        M = Steps("gate0 turn0 gate1 turn1")
        LOOPS = RW_TILES // 2
        block = ctx.enter_context(nc.Block())

        @block.sync
        def _(sp):
            with nc.allow_non_contiguous_dma(reason="gains as columns"):
                sp.dma_start(gains[:, 0, :], ln_g.rearrange("(n p) -> p n", p=P)).then_inc(once, 16)
                sp.dma_start(gains[:, 1, :], ln_b.rearrange("(n p) -> p n", p=P)).then_inc(once, 16)
            sp.dma_start(g2s[:], g2).then_inc(once, 16)
            sp.dma_start(gin[:], gate_in).then_inc(once, 16)
            for c in range(RW_TILES):
                s = c % 2
                if c >= 2:
                    sp.wait_ge(dves, V(f"gate{s}", c // 2 - 1))
                chan = slice(c * P, (c + 1) * P)
                for d, t in ((0, yf), (1, yb)):
                    sp.dma_start(t[s][:], y[d][:, chan].rearrange("(n p) c -> p n c", p=P)).then_inc(y_loaded[s], 16)
                sp.dma_start(bv[s][:], bonus[chan, :]).then_inc(y_loaded[s], 16)

        @block.gpsimd
        def _(pool):
            for s in slots:
                pool.sem_inc(oc_free[s], 1)
            for c in range(RW_TILES):
                s = c % 2
                pool.wait_ge(dves, V(f"gate{s}", c // 2))
                pool.dma_start(oT[c * P:(c + 1) * P, :], oc[s][:]).then_inc(o_stored[s], 16)
                pool.wait_ge(o_stored[s], c // 2 * 16 + 16)
                pool.sem_inc(oc_free[s], 1)

        @block.scalar
        def _(act):
            with act.Fori(0, LOOPS) as j:
                line = Line(act, acts, A, j)
                for s in slots:
                    act.wait_ge(dves, V(f"var{s}", j))
                    line(f"root{s}", nc.scalar.activation(stat[:, 2, :], stat[:, 1, :], ACT.Sqrt,
                                                          bias=k.eps[:, 2:3], scale=1.0 / HEAD))
            act.dma_start(wo[:], w_out.rearrange("(n p) e -> p n e", p=P)).then_inc(wo_loaded, 16)

        @block.vector
        def _(dve):
            dve.wait_ge(once, 64)
            with dve.Fori(0, LOOPS) as j:
                line = Line(dve, dves, V, j)
                for s in slots:
                    heads = lambda t: t[:].rearrange("p n (h e) -> p (n h) e", e=HEAD)
                    wide = lambda i: stat[:, i, :].unsqueeze(2).to_broadcast([P, NT * 2, HEAD])
                    col = lambda i: gains[:, i, bass.ds(j * 2 + s, 1)]
                    flat = lambda t: t[:].rearrange("p n c -> p (n c)")
                    dve.wait_ge(y_loaded[s], j * 48 + 48)
                    line(f"sum{s}", nc.vector.tensor_tensor(flat(yf[s]), flat(yf[s]), flat(yb[s]), ALU.add))
                    line(f"mean{s}", nc.vector.tensor_reduce(stat[:, 0, :], heads(yf[s]), AX.X, ALU.add))
                    line(f"meand{s}", nc.vector.tensor_scalar(stat[:, 0, :], stat[:, 0, :], 1.0 / HEAD, None, ALU.mult))
                    line(f"cent{s}", nc.vector.tensor_tensor(heads(yc), heads(yf[s]), wide(0), ALU.subtract))
                    line(f"sq{s}", nc.vector.tensor_tensor(flat(yb[s]), flat(yc), flat(yc), ALU.mult))
                    line(f"var{s}", nc.vector.tensor_reduce(stat[:, 1, :], heads(yb[s]), AX.X, ALU.add))
                    dve.wait_ge(acts, A(f"root{s}", j))
                    line(f"inv{s}", nc.vector.reciprocal(stat[:, 2, :], stat[:, 2, :]))
                    line(f"norm{s}", nc.vector.tensor_tensor(heads(yf[s]), heads(yc), wide(2), ALU.mult))
                    dve.wait_ge(pes, M(f"turn{s}", j))
                    dve.wait_ge(oc_free[s], j + 1)
                    line(f"aff{s}", nc.vector.tensor_scalar(oc[s][:], tp[s][:], col(0), col(1), ALU.mult, ALU.add))
                    line(f"bon{s}", nc.vector.tensor_tensor(oc[s][:], oc[s][:], bv[s][:], ALU.add))
                    line(f"gate{s}", nc.vector.tensor_tensor(oc[s][:], oc[s][:], gp[s][:], ALU.mult))

        @block.tensor
        def _(pe):
            pe.wait_ge(once, 64)
            for c in range(RW_TILES):
                s, j = c % 2, c // 2
                if j:
                    pe.wait_ge(dves, V(f"gate{s}", j - 1))
                for h in range(2):
                    last = nc.tensor.matmul(gp[s][:, h * HALF:(h + 1) * HALF], g2s[:, c * P:(c + 1) * P],
                                            gin[:, h * HALF:(h + 1) * HALF], start=True, stop=True)
                last.then_inc(pes, 1)
                pe.wait_ge(dves, V(f"norm{s}", j))
                for n in range(NT):
                    last = nc.tensor.transpose(tp[s][:, n * P:(n + 1) * P], yf[s][:, n, :], k.ident[:])
                last.then_inc(pes, 1)


def mix_out_and_route(nc, k, x, oT, wo, wo_loaded, ffn_gain, w_router, b_router, h1, m, chosen, gates):
    with ExitStack() as ctx:
        sb = lambda name, shape, dt=F32: ctx.enter_context(nc.sbuf_tensor(name, shape, dt))
        sem = lambda name: ctx.enter_context(nc.semaphore(name))
        slots = range(2)
        wr = sb("wr", [P, ND, EXPERTS])
        br = sb("br", [P, EXPERTS])
        gb = sb("gb", [P, D])
        expert = sb("expert", [P, EXPERTS], I32)
        expertf = sb("expertf", [P, EXPERTS])
        ot = [sb(f"ot{s}", [P, ND, P]) for s in slots]
        xt = [sb(f"xin{s}", [P, D]) for s in slots]
        ht = [sb(f"ht{s}", [P, D]) for s in slots]
        mt = [sb(f"mtok{s}", [P, D]) for s in slots]
        mT = [sb(f"mT{s}", [P, ND, P]) for s in slots]
        carrier = sb("rcarrier", [P, 1])
        sq = sb("hsq", [P, D])
        st = [sb(f"hst{s}", [P, 2]) for s in slots]
        lg = [sb(f"lg{s}", [P, EXPERTS]) for s in slots]
        top = [sb(f"top{s}", [P, 8]) for s in slots]
        ix = [sb(f"ix{s}", [P, 8], U32) for s in slots]
        ixf = [sb(f"ixf{s}", [P, 8]) for s in slots]
        gt = [sb(f"gt{s}", [P, 4]) for s in slots]
        hp = [ctx.enter_context(nc.psum_tensor(f"hp{s}", [P, D], F32)) for s in slots]
        tp = ctx.enter_context(nc.psum_tensor("mtp", [P, D], F32))
        lp = [ctx.enter_context(nc.psum_tensor(f"lp{s}", [P, HALF], F32)) for s in slots]
        once, made = sem("r_once"), sem("r_made")
        loaded = [sem(f"r_loaded{s}") for s in slots]
        stored = [sem(f"r_stored{s}") for s in slots]
        slot_free = [sem(f"r_slot_free{s}") for s in slots]
        acts, dves, pes = sem("r_acts"), sem("r_dves"), sem("r_pes")
        V0 = Steps("expertf")
        A = Steps(" ".join(f"sq{s} root{s} mTa{s} mTb{s} exp{s}" for s in slots))
        V = Steps(" ".join(f"h{s} inv{s} m{s} logit{s} max{s} idx{s} idf{s} neg{s} hot0{s} hot1{s} hot2{s} hot3{s} "
                           f"inve{s} gate{s}" for s in slots))
        M = Steps(" ".join(f"turn{s} logit{s}" for s in slots))
        mixed = sem("r_mixed")
        LOOPS = NT // 2
        block = ctx.enter_context(nc.Block())
        oT_v = oT.rearrange("(n p) t -> p n t", p=P)

        @block.sync
        def _(sp):
            sp.dma_start(wr[:], w_router.rearrange("(n p) e -> p n e", p=P)).then_inc(once, 16)
            sp.dma_start(br[:], b_router.rearrange("(o e) -> o e", o=1).to_broadcast([P, EXPERTS])).then_inc(once, 16)
            sp.dma_start(gb[:], ffn_gain.rearrange("(o e) -> o e", o=1).to_broadcast([P, D])).then_inc(once, 16)
            with sp.Fori(0, LOOPS) as j:
                for s in slots:
                    first = sp.snap(j * 2 * P + s * P)
                    sp.wait_ge(slot_free[s], j + 1)
                    sp.dma_start(ot[s][:], oT_v[:, :, bass.ds(first, P)]).then_inc(loaded[s], 16)
                    sp.dma_start(xt[s][:], row(x, first, P)).then_inc(loaded[s], 16)

        @block.gpsimd
        def _(pool):
            for s in slots:
                pool.sem_inc(slot_free[s], 1)
            pool.iota(expert[:], [[1, EXPERTS]], base=0, channel_multiplier=0).then_inc(made, 1)
            with pool.Fori(0, LOOPS) as j:
                for s in slots:
                    first = j * 2 * P + s * P
                    pool.wait_ge(dves, V0.n + V(f"m{s}", j))
                    pool.dma_start(row(h1, first, P), ht[s][:]).then_inc(stored[s], 16)
                    pool.dma_start(row(m, first, P), mt[s][:]).then_inc(stored[s], 16)
                    pool.wait_ge(stored[s], j * 32 + 32)
                    pool.sem_inc(slot_free[s], 1)

        @block.scalar
        def _(act):
            with act.Fori(0, LOOPS) as j:
                line = Line(act, acts, A, j)
                vdone = lambda name: V0.n + V(name, j)
                for s in slots:
                    act.wait_ge(dves, vdone(f"h{s}"))
                    line(f"sq{s}", nc.scalar.activation(sq[:], ht[s][:], ACT.Square, accum_out=st[s][:, 0:1]))
                    line(f"root{s}", nc.scalar.activation(st[s][:, 1:2], st[s][:, 0:1], ACT.Sqrt,
                                                          bias=k.eps[:, 0:1], scale=1.0 / D))
                    act.wait_ge(pes, M(f"turn{s}", j))
                    for n in range(2):
                        line(f"mT{'ab'[n]}{s}", nc.scalar.copy(
                            mT[s][:].rearrange("p n t -> p (n t)")[:, n * HALF:(n + 1) * HALF],
                            tp[:, n * HALF:(n + 1) * HALF]))
                    act.wait_ge(dves, vdone(f"neg{s}"))
                    line(f"exp{s}", nc.scalar.activation(gt[s][:], top[s][:, 0:4], ACT.Exp, bias=ixf[s][:, 7:8],
                                                         accum_out=ixf[s][:, 6:7]))

        @block.vector
        def _(dve):
            line = Line(dve, dves, V0)
            dve.wait_ge(made, 1)
            line("expertf", nc.vector.tensor_copy(expertf[:], expert[:]))
            dve.wait_ge(once, 48)
            with dve.Fori(0, LOOPS) as j:
                line = Line(dve, dves, V, j, V0.n)
                for s in slots:
                    tile = bass.ds(j * 2 + s, 1)
                    dve.wait_ge(mixed, j * 2 + s + 1)
                    dve.wait_ge(loaded[s], j * 32 + 32)
                    line(f"h{s}", nc.vector.tensor_tensor(ht[s][:], hp[s][:], xt[s][:], ALU.add))
                    dve.wait_ge(acts, A(f"root{s}", j))
                    line(f"inv{s}", nc.vector.reciprocal(st[s][:, 0:1], st[s][:, 1:2]))
                    line(f"m{s}", nc.vector.scalar_tensor_tensor(out=mt[s][:], in0=ht[s][:], scalar=st[s][:, 0:1],
                                                                 in1=gb[:], op0=ALU.mult, op1=ALU.mult))
                    dve.wait_ge(pes, M(f"logit{s}", j))
                    line(f"logit{s}", nc.vector.tensor_tensor(lg[s][:], lp[s][:, 0:EXPERTS], br[:], ALU.add))
                    nc.vector.memset(carrier[:], 0.0)
                    line(f"max{s}", nc.vector.max(top[s][:], lg[s][:]))
                    nc.vector.memset(carrier[:], 0.0)
                    line(f"idx{s}", nc.vector.max_index(ix[s][:], top[s][:], lg[s][:]))
                    line(f"idf{s}", nc.vector.tensor_copy(ixf[s][:], ix[s][:]))
                    line(f"neg{s}", nc.vector.tensor_scalar(ixf[s][:, 7:8], top[s][:, 0:1], -1.0, None, ALU.mult))
                    for q in range(TOP_K):
                        line(f"hot{q}{s}", nc.vector.tensor_scalar(
                            chosen[:, tile, q, :].rearrange("p a e -> p (a e)"), expertf[:], ixf[s][:, q:q + 1],
                            None, ALU.is_equal))
                    dve.wait_ge(acts, A(f"exp{s}", j))
                    line(f"inve{s}", nc.vector.reciprocal(ixf[s][:, 6:7], ixf[s][:, 6:7]))
                    line(f"gate{s}", nc.vector.tensor_scalar(
                        gates[:, tile, :].rearrange("p a q -> p (a q)"), gt[s][:], ixf[s][:, 6:7], None, ALU.mult))

        @block.tensor
        def _(pe):
            pe.wait_ge(once, 48)
            pe.wait_ge(wo_loaded, 16)

            def mix(s, j):
                pe.wait_ge(loaded[s], j * 32 + 32)
                for h in range(2):
                    for n in range(ND):
                        last = nc.tensor.matmul(hp[s][:, h * HALF:(h + 1) * HALF], ot[s][:, n, :],
                                                wo[:, n, h * HALF:(h + 1) * HALF], start=(n == 0), stop=(n == ND - 1))
                last.then_inc(mixed, 1)

            def route(s, j):
                pe.wait_ge(dves, V0.n + V(f"m{s}", j))
                for n in range(ND):
                    last = nc.tensor.transpose(tp[:, n * P:(n + 1) * P], mt[s][:, n * P:(n + 1) * P], k.ident[:])
                last.then_inc(pes, 1)
                pe.wait_ge(acts, A(f"mTb{s}", j))
                for n in range(ND):
                    last = nc.tensor.matmul(lp[s][:, 0:EXPERTS], mT[s][:, n, :], wr[:, n, :],
                                            start=(n == 0), stop=(n == ND - 1))
                last.then_inc(pes, 1)

            mix(0, 0)
            with pe.Fori(0, LOOPS - 1) as j:
                mix(1, j)
                route(0, j)
                mix(0, j + 1)
                route(1, j)
            mix(1, LOOPS - 1)
            route(0, LOOPS - 1)
            route(1, LOOPS - 1)


def place_rows(nc, k, chosen, row_of, table, row_token):
    with ExitStack() as ctx:
        sb = lambda name, shape, dt=F32: ctx.enter_context(nc.sbuf_tensor(name, shape, dt))
        sem = lambda name: ctx.enter_context(nc.semaphore(name))
        mask = sb("pmask", [P, NT, EXPERTS])
        m1 = sb("pmask1", [P, NT, EXPERTS])
        cnt = sb("pcnt", [P, EXPERTS])
        nb = sb("pnb", [P, EXPERTS])
        ge = sb("pge", [P, EXPERTS])
        incl = sb("pincl", [P, EXPERTS])
        start = sb("pstart", [P, EXPERTS])
        rank = sb("prank", [P, NT, EXPERTS])
        prod = sb("pprod", [P, NT, TOP_K, EXPERTS])
        dest = sb("pdest", [P, NT * TOP_K])
        zero = sb("pzero", [P, ROWS // P], I32)
        rp = ctx.enter_context(nc.psum_tensor("rp", [P, HALF], F32))
        cp = ctx.enter_context(nc.psum_tensor("cp", [P, HALF], F32))
        dves, pes, made, zeroed = (sem(f"p_{n}") for n in "dves pes made zeroed".split())
        V = Steps("m0 m1 m cnt one " + " ".join(f"ge{n} nb{n}" for n in range(1, T // P)) +
                  " incl first tab0 tab1 tab2 none start rank prod dest cast")
        block = ctx.enter_context(nc.Block())

        @block.vector
        def _(dve):
            line = Line(dve, dves, V)
            tt = lambda o, a, b, op: nc.vector.tensor_tensor(o, a, b, op)
            line("m0", tt(mask[:], chosen[:, :, 0, :], chosen[:, :, 1, :], ALU.add))
            line("m1", tt(m1[:], chosen[:, :, 2, :], chosen[:, :, 3, :], ALU.add))
            line("m", tt(mask[:], mask[:], m1[:], ALU.add))
            dve.wait_ge(pes, 1)
            line("cnt", nc.vector.tensor_copy(cnt[:], cp[:, 0:EXPERTS]))
            line("one", nc.vector.memset(nb[:], 1.0))
            for n in range(1, T // P):
                line(f"ge{n}", nc.vector.tensor_scalar(ge[:], cnt[:], float(n * P), None, ALU.is_gt))
                line(f"nb{n}", tt(nb[:], nb[:], ge[:], ALU.add))
            line("incl", nc.vector.tensor_tensor_scan(incl[:], k.ones[:, 0:EXPERTS], nb[:], 0.0, ALU.mult, ALU.add))
            line("first", tt(start[:], incl[:], nb[:], ALU.subtract))
            line("tab0", nc.vector.tensor_copy(table[:, 0, :], start[:]))
            line("tab1", nc.vector.tensor_copy(table[:, 1, :], nb[:]))
            line("tab2", nc.vector.tensor_scalar(table[:, 2, :], nb[:], -1.0, None, ALU.add))
            line("none", nc.vector.memset(table[:, 2, EXPERTS - 1:EXPERTS], T // P))
            line("start", nc.vector.tensor_scalar(start[:], start[:], float(P), None, ALU.mult))
            dve.wait_ge(pes, 2)
            line("rank", tt(rank[:], rp[:, 0:NT * EXPERTS].rearrange("p (t e) -> p t e", e=EXPERTS),
                            start[:].unsqueeze(1).to_broadcast([P, NT, EXPERTS]), ALU.add))
            line("prod", tt(prod[:], chosen[:], rank[:].unsqueeze(2).to_broadcast([P, NT, TOP_K, EXPERTS]), ALU.mult))
            line("dest", nc.vector.tensor_reduce(dest[:], prod[:].rearrange("p t q e -> p (t q) e"), AX.X, ALU.add))
            line("cast", nc.vector.tensor_copy(row_of[:], dest[:]))

        @block.tensor
        def _(pe):
            pe.wait_ge(dves, V("m"))
            for t in range(NT):
                last = nc.tensor.matmul(cp[:, 0:EXPERTS], k.ones[:], mask[:, t, :], start=(t == 0), stop=(t == NT - 1))
            last.then_inc(pes, 1)
            for t in range(NT):
                out = rp[:, t * EXPERTS:(t + 1) * EXPERTS]
                for u in range(t):
                    nc.tensor.matmul(out, k.ones[:], mask[:, u, :], start=(u == 0), stop=False)
                last = nc.tensor.matmul(out, k.before[:], mask[:, t, :], start=(t == 0), stop=True)
            last.then_inc(pes, 1)

        @block.gpsimd
        def _(pool):
            pool.memset(zero[:], 0).then_inc(made, 1)
            pool.wait_ge(made, 1)
            pool.dma_start(row_token.rearrange("(p n) o -> p (n o)", p=P), zero[:]).then_inc(zeroed, 16)
            pool.wait_ge(zeroed, 16)


LIMIT, ALPHA = 7.0, 1.702


def expert_rows(nc, k, m, row_of, row_token, table, w1, w2, biases, yb):
    SLOTS, W1_SLOTS = 6, 4
    order = (0, 2, 1, 3)
    Q = ND // 2
    with ExitStack() as ctx:
        sb = lambda name, shape, dt=F32: ctx.enter_context(nc.sbuf_tensor(name, shape, dt))
        sem = lambda name: ctx.enter_context(nc.semaphore(name))
        w, w_rest = [], []
        for c in range(SLOTS):
            at = (nc.sbuf_base + 31) // 32 * 32
            w.append(sb(f"wslot{c}", [P, ND, HALF]))
            if c < W1_SLOTS:
                w_rest.append(nc.alloc_sbuf_tensor_at(f"wrest{c}", [P, ND, HALF], F32R, offset=at))
        bias = [sb(f"bslot{c}", [PARTS, HALF], BF16) for c in range(SLOTS)]
        ones = sb("bones", [PARTS, P], BF16)
        idx = sb("gidx", [P, 1], U32)
        token = sb("token", [P, NT], I32)
        xg = sb("xg", [P, D])
        w_high = [sb(f"whigh{c}", [P, ND, HALF], F32R) for c in range(W1_SLOTS)]
        x_parts = [sb(f"x{n}", [P, ND, P], F32R) for n in ("high", "rest")]
        glu = [sb(f"glu{h}", [P, HALF]) for h in range(2)]
        lin = [sb(f"lin{h}", [P, HALF]) for h in range(2)]
        sig = [sb(f"sig{h}", [P, HALF]) for h in range(2)]
        act_t = sb("actt", [P, D_FF])
        aT = sb("aTt", [P, ND, P])
        yo = sb("yo", [P, D])
        tp = [ctx.enter_context(nc.psum_tensor(f"etp{h}", [P, HALF], F32)) for h in range(2)]
        hc = [ctx.enter_context(nc.psum_tensor(f"hc{c}", [P, HALF], F32)) for c in range(SLOTS)]
        w_loaded = [sem(f"w_in{c}") for c in range(SLOTS)]
        used = [sem(f"used{c}") for c in range(SLOTS)]
        idx_loaded, gathered, y_stored, passed = sem("idx_in"), sem("gathered"), sem("y_out"), sem("e_passed")
        x_turned = sem("x_turned")
        act_turned = sem("act_turned")
        x_low, x_high = sem("x_low"), sem("x_high")
        act_copied = sem("act_copied")
        sigmoid_done, ones_made = sem("sigmoid_done"), sem("ones_made")
        y_low, y_high, passed_act = sem("y_low"), sem("y_high"), sem("act_passed")
        tokens_made, scattered = sem("tokens_made"), sem("scattered")
        dves, x_rest, high_made, rest_made = sem("e_dves"), sem("x_rest"), sem("high_made"), sem("rest_made")
        V = Steps("glu0 lin0 mul0 act0 glu1 lin1 mul1 act1")
        flat = lambda t: t.rearrange("p n t -> p (n t)")
        block = ctx.enter_context(nc.Block())

        def blocks(eng, body, split=False):
            register = lambda v: v.val if isinstance(v.val, bass.RegisterHandle) else v.val.handles[0]

            with eng.Fori(0, EXPERTS) as e:
                first = eng.value_load(table[0:1, 0, bass.ds(e, 1)], min_val=0, max_val=BLOCKS - 1)
                count = eng.value_load(table[0:1, 1, bass.ds(e, 1)], min_val=1, max_val=T // P)
                split_at = eng.value_load(table[0:1, 2, bass.ds(e, 1)], min_val=0, max_val=T // P) if split else None
                with eng.Fori(0, count) as b:
                    body(first + b, e, (lambda: eng.If_eq(register(b), register(split_at))) if split else None)

        @block.sync
        def _(sp):
            def load(c, e):
                src, chunk = (w1, order[c]) if c < 4 else (w2, c - 4)
                cols = slice(chunk * HALF, (chunk + 1) * HALF)
                sp.dma_start(w[c][:], row(src, e).rearrange("o (n p) f -> p (o n) f", p=P)[:, :, cols]
                             ).then_inc(w_loaded[c], 16)
                bcols = slice(cols.start + (0 if c < 4 else 2 * D_FF), cols.stop + (0 if c < 4 else 2 * D_FF))
                sp.dma_start(bias[c][:], row(biases, e).rearrange("o s f -> (o s) f")[:, bcols]
                             ).then_inc(w_loaded[c], 16)

            for c in range(SLOTS):
                load(c, 0)
            with sp.Fori(1, EXPERTS) as e:
                first = sp.value_load(table[0:1, 0, bass.ds(e, 1)], min_val=0, max_val=BLOCKS - 1)
                for c in range(SLOTS):
                    sp.wait_ge(used[c], first)
                    load(c, e)

        @block.gpsimd
        def _(pool):
            def fetch(n):
                pool.dma_start(idx[:], row(row_token, n * P, P)).then_inc(idx_loaded, 16)
                pool.wait_ge(idx_loaded, n * 16 + 16)
                pool.sem_inc(passed, 1)
                pool.indirect_dma_start(xg[:], None, m, bass.IndirectOffsetOnAxis(ap=idx[:, 0:1], axis=0)
                                        ).then_inc(gathered, 16)

            def body(n, e, last_block):
                pool.wait_ge(x_turned, n * 2 + 2)
                fetch(n + 1)

            pool.memset(ones[:], 1.0).then_inc(ones_made, 1)
            pool.iota(token[:], [[P, NT]], base=0, channel_multiplier=1).then_inc(tokens_made, 1)
            pool.wait_ge(tokens_made, 1)
            for t in range(NT):
                for q in range(TOP_K):
                    i = t * TOP_K + q
                    pool.indirect_dma_start(row_token, bass.IndirectOffsetOnAxis(ap=row_of[:, i:i + 1], axis=0),
                                            token[:, t:t + 1], None).then_inc(scattered, 16)
            pool.wait_ge(scattered, 16 * NT * TOP_K)
            fetch(0)
            blocks(pool, body)
            last = pool.value_load(table[0:1, 0, EXPERTS - 1:EXPERTS], min_val=0, max_val=BLOCKS - 1)
            more = pool.value_load(table[0:1, 1, EXPERTS - 1:EXPERTS], min_val=1, max_val=T // P)
            pool.wait_ge(gathered, (last + more) * 16 + 16)
            pool.sem_inc(passed, 1)

        @block.scalar
        def _(act):
            def copy_x(n):
                act.wait_ge(x_turned, n * 2 + 2)
                nc.scalar.copy(flat(x_parts[0][:, 0:Q, :]), tp[0][:]).then_inc(x_low, 1)

            def high(c, e):
                act.wait_ge(w_loaded[c], e * 32 + 32)
                nc.scalar.copy(flat(w_high[c]), flat(w[c])).then_inc(high_made, 1)

            def sigmoid(h, n):
                act.wait_ge(dves, V(f"glu{h}", n))
                nc.scalar.activation(sig[h][:], glu[h][:], ACT.Sigmoid, scale=ALPHA).then_inc(sigmoid_done, 1)

            def copy_act(h, n):
                act.wait_ge(act_turned, n * 2 + 1 + h)
                nc.scalar.copy(flat(aT[:, Q * h:Q * h + Q, :]), tp[h][:]).then_inc(act_copied, 1)

            def body(n, e, last_block):
                sigmoid(0, n)
                copy_act(0, n)
                sigmoid(1, n)
                with last_block():
                    high(0, e + 1)
                copy_x(n + 1)
                with last_block():
                    high(1, e + 1)
                copy_act(1, n)
                with last_block():
                    high(2, e + 1)
                    high(3, e + 1)
                act.wait_ge(used[5], n + 1)
                nc.scalar.copy(yo[:, HALF:D], hc[5][:]).then_inc(y_high, 1)
                act.wait_ge(y_high, n + 1)
                act.wait_ge(y_low, n + 1)
                act.dma_start(row(yb, n * P, P), yo[:]).then_inc(y_stored, 16)
                act.wait_ge(y_stored, n * 16 + 16)
                act.sem_inc(passed_act, 1)

            copy_x(0)
            for c in range(W1_SLOTS):
                high(c, 0)
            blocks(act, body, split=True)

        @block.vector
        def _(dve):
            def copy_x(n):
                dve.wait_ge(x_turned, n * 2 + 1)
                nc.vector.tensor_copy(flat(x_parts[0][:, Q:ND, :]), tp[1][:]).then_inc(x_high, 1)
                dve.wait_ge(x_high, n + 1)
                nc.vector.tensor_tensor(flat(x_parts[1][:, Q:ND, :]), tp[1][:], flat(x_parts[0][:, Q:ND, :]),
                                        ALU.subtract).then_inc(x_rest, 1)
                dve.wait_ge(x_low, n + 1)
                nc.vector.tensor_tensor(flat(x_parts[1][:, 0:Q, :]), tp[0][:], flat(x_parts[0][:, 0:Q, :]),
                                        ALU.subtract).then_inc(x_rest, 1)

            def rest(c, e):
                dve.wait_ge(high_made, e * W1_SLOTS + c + 1)
                nc.vector.tensor_tensor(flat(w_rest[c]), flat(w[c]), flat(w_high[c]), ALU.subtract
                                        ).then_inc(rest_made, 1)

            def body(n, e, last_block):
                line = Line(dve, dves, V, n)
                for h in range(2):
                    dve.wait_ge(used[2 * h], n + 1)
                    line(f"glu{h}", nc.vector.tensor_scalar(glu[h][:], hc[2 * h][:], LIMIT, None, ALU.min))
                    dve.wait_ge(used[2 * h + 1], n + 1)
                    line(f"lin{h}", nc.vector.tensor_scalar(lin[h][:], hc[2 * h + 1][:], LIMIT, -LIMIT,
                                                            ALU.min, ALU.max))
                    line(f"mul{h}", nc.vector.scalar_tensor_tensor(out=lin[h][:], in0=lin[h][:], scalar=1.0,
                                                                   in1=glu[h][:], op0=ALU.add, op1=ALU.mult))
                    dve.wait_ge(sigmoid_done, n * 2 + 1 + h)
                    line(f"act{h}", nc.vector.tensor_tensor(act_t[:, h * HALF:(h + 1) * HALF], lin[h][:], sig[h][:],
                                                            ALU.mult))
                copy_x(n + 1)
                with last_block():
                    for c in range(W1_SLOTS - 1):
                        rest(c, e + 1)
                dve.wait_ge(used[4], n + 1)
                nc.vector.tensor_copy(yo[:, 0:HALF], hc[4][:]).then_inc(y_low, 1)
                with last_block():
                    rest(W1_SLOTS - 1, e + 1)

            copy_x(0)
            for c in range(W1_SLOTS):
                rest(c, 0)
            blocks(dve, body, split=True)

        @block.tensor
        def _(pe):
            def turn(src, h):
                for q in range(Q):
                    last = nc.tensor.transpose(tp[h][:, q * P:(q + 1) * P],
                                               src[:, (Q * h + q) * P:(Q * h + q + 1) * P], k.ident[:])
                return last

            def turn_x(n):
                pe.wait_ge(gathered, n * 16 + 16)
                turn(xg, 1).then_inc(x_turned, 1)
                turn(xg, 0).then_inc(x_turned, 1)

            def bias_rows(c, e):
                pe.wait_ge(w_loaded[c], e * 32 + 32)
                nc.tensor.matmul(hc[c][:], ones[:], bias[c][:], start=True, stop=False)

            def part(c, lhsT, q):
                return nc.tensor.matmul(hc[c][:], lhsT[:, q, :], w[c][:, q, :], start=False, stop=(q == ND - 1))

            def product(c, e):
                pe.wait_ge(rest_made, e * W1_SLOTS + c + 1)
                nc.tensor.matmul(hc[c][:], ones[:], bias[c][:], start=True, stop=False)
                x_high_part, x_rest_part = x_parts
                for q in range(ND):
                    nc.tensor.matmul(hc[c][:], x_high_part[:, q, :], w_high[c][:, q, :], start=False, stop=False)
                    nc.tensor.matmul(hc[c][:], x_high_part[:, q, :], w_rest[c][:, q, :], start=False,
                                     stop=False)
                    last = nc.tensor.matmul(hc[c][:], x_rest_part[:, q, :], w_high[c][:, q, :], start=False,
                                            stop=(q == ND - 1))
                last.then_inc(used[c], 1)

            def body(n, e, last_block):
                pe.wait_ge(x_rest, n * 2 + 2)
                for c in range(3):
                    product(c, e)
                pe.wait_ge(dves, V("act0", n))
                turn(act_t, 0).then_inc(act_turned, 1)
                product(3, e)
                pe.wait_ge(act_copied, n * 2 + 1)
                turn_x(n + 1)
                for c in (4, 5):
                    bias_rows(c, e)
                for q in range(Q - 1):
                    for c in (4, 5):
                        part(c, aT, q)
                pe.wait_ge(dves, V("act1", n))
                pe.wait_ge(x_rest, n * 2 + 3)
                turn(act_t, 1).then_inc(act_turned, 1)
                for c in (4, 5):
                    part(c, aT, Q - 1)
                pe.wait_ge(act_copied, n * 2 + 2)
                for c in (4, 5):
                    for q in range(Q, ND):
                        last = part(c, aT, q)
                    last.then_inc(used[c], 1)

            pe.wait_ge(ones_made, 1)
            turn_x(0)
            blocks(pe, body)


def finish(nc, k, h1, yb, row_of, gates, p, w_ple, ple_gain, w_gate, out):
    NP = PLE // P
    with ExitStack() as ctx:
        sb = lambda name, shape, dt=F32: ctx.enter_context(nc.sbuf_tensor(name, shape, dt))
        sem = lambda name: ctx.enter_context(nc.semaphore(name))
        slots = range(2)
        wg = sb("wgate", [P, ND, D])
        wp = sb("wple", [P, NP, D])
        gb = sb("pgain", [P, D])
        ht = [sb(f"fh{s}", [P, D]) for s in slots]
        pt = [sb(f"fp{s}", [P, PLE]) for s in slots]
        rows = [[sb(f"frow{s}{q}", [P, D]) for q in range(TOP_K)] for s in slots]
        hT = [sb(f"fhT{s}", [P, ND, P]) for s in slots]
        pT = [sb(f"fpT{s}", [P, NP, P]) for s in slots]
        sg = [sb(f"fsig{s}", [P, D]) for s in slots]
        es = sb("fe", [P, D])
        sq = sb("fsq", [P, D])
        st = sb("fst", [P, 2])
        ot = [sb(f"fo{s}", [P, D]) for s in slots]
        tp = ctx.enter_context(nc.psum_tensor("ftp", [P, D], F32))
        pp = ctx.enter_context(nc.psum_tensor("fpp", [P, HALF], F32))
        ep = ctx.enter_context(nc.psum_tensor("fep", [P, D], F32))
        gp = ctx.enter_context(nc.psum_tensor("fgp", [P, D], F32))
        once, gate_loaded = sem("f_once"), sem("f_gate_loaded")
        loaded = [sem(f"f_loaded{s}") for s in slots]
        fetched = [sem(f"f_rows{s}") for s in slots]
        stored = [sem(f"f_stored{s}") for s in slots]
        slot_free = [sem(f"f_slot_free{s}") for s in slots]
        acts, dves, pes, added = sem("f_acts"), sem("f_dves"), sem("f_pes"), sem("f_added")
        A = Steps("pT ha hb sq root sig")
        V = Steps("inv e g out")
        R = Steps(" ".join(f"r{q}" for q in range(TOP_K)))
        M = Steps("pT hT e g")
        LOOPS = NT // 2
        block = ctx.enter_context(nc.Block())

        @block.sync
        def _(sp):
            sp.dma_start(wp[:], w_ple.rearrange("(n p) e -> p n e", p=P)).then_inc(once, 16)
            sp.dma_start(gb[:], ple_gain.rearrange("(o e) -> o e", o=1).to_broadcast([P, D])).then_inc(once, 16)
            with sp.Fori(0, LOOPS) as j:
                for s in slots:
                    first = sp.snap(j * 2 * P + s * P)
                    sp.wait_ge(slot_free[s], j + 1)
                    sp.dma_start(ht[s][:], row(h1, first, P)).then_inc(loaded[s], 16)
                    sp.dma_start(pt[s][:], row(p, first, P)).then_inc(loaded[s], 16)

        @block.gpsimd
        def _(pool):
            for s in slots:
                pool.sem_inc(slot_free[s], 1)
            for i in range(NT + 2):
                s = i % 2
                if i < NT:
                    if i >= 2:
                        pool.wait_ge(added, R(f"r{TOP_K - 1}", i - 2))
                    for q in range(TOP_K):
                        pool.indirect_dma_start(rows[s][q][:], None, yb, bass.IndirectOffsetOnAxis(
                            ap=row_of[:, i * TOP_K + q:i * TOP_K + q + 1], axis=0)).then_inc(fetched[s], 16)
                if i >= 2:
                    pool.wait_ge(dves, V("out", i - 2))
                    pool.dma_start(row(out, (i - 2) * P, P), ot[s][:]).then_inc(stored[s], 16)
                    pool.wait_ge(stored[s], (i // 2) * 16)
                    pool.sem_inc(slot_free[s], 1)

        @block.scalar
        def _(act):
            act.wait_ge(fetched[0], 16 * TOP_K)
            act.dma_start(wg[:], w_gate.rearrange("(n p) e -> p n e", p=P)).then_inc(gate_loaded, 16)
            with act.Fori(0, LOOPS) as j:
                for s in slots:
                    i = j * 2 + s
                    line = Line(act, acts, A, i)
                    act.wait_ge(pes, M("pT", i))
                    line("pT", nc.scalar.copy(pT[s][:].rearrange("p n t -> p (n t)"), pp[:, 0:PLE]))
                    act.wait_ge(pes, M("hT", i))
                    for n in range(2):
                        line(f"h{'ab'[n]}", nc.scalar.copy(
                            hT[s][:].rearrange("p n t -> p (n t)")[:, n * HALF:(n + 1) * HALF],
                            tp[:, n * HALF:(n + 1) * HALF]))
                    act.wait_ge(pes, M("e", i))
                    line("sq", nc.scalar.activation(sq[:], ep[:], ACT.Square, accum_out=st[:, 0:1]))
                    line("root", nc.scalar.activation(st[:, 0:1], st[:, 0:1], ACT.Sqrt, bias=k.eps[:, 0:1],
                                                      scale=1.0 / D))
                    act.wait_ge(pes, M("g", i))
                    line("sig", nc.scalar.activation(sg[s][:], gp[:], ACT.Sigmoid))

        @block.vector
        def _(dve):
            def add_rows(s, i, nth):
                line = Line(dve, added, R, i)
                dve.wait_ge(loaded[s], nth * 32 + 32)
                dve.wait_ge(fetched[s], nth * 64 + 64)
                for q in range(TOP_K):
                    line(f"r{q}", nc.vector.scalar_tensor_tensor(
                        out=ht[s][:], in0=rows[s][q][:],
                        scalar=gates[:, bass.ds(i, 1), q:q + 1].rearrange("p a q -> p (a q)"),
                        in1=ht[s][:], op0=ALU.mult, op1=ALU.add))

            def tile(s, i, nth, more):
                line = Line(dve, dves, V, i)
                dve.wait_ge(acts, A("root", i))
                line("inv", nc.vector.reciprocal(st[:, 1:2], st[:, 0:1]))
                line("e", nc.vector.scalar_tensor_tensor(out=es[:], in0=ep[:], scalar=st[:, 1:2], in1=gb[:],
                                                         op0=ALU.mult, op1=ALU.mult))
                if more:
                    add_rows(1 - s, i + 1, nth + s)
                dve.wait_ge(acts, A("sig", i))
                line("g", nc.vector.tensor_tensor(es[:], es[:], sg[s][:], ALU.mult))
                dve.wait_ge(loaded[s], nth * 32 + 32)
                line("out", nc.vector.tensor_tensor(ot[s][:], es[:], ht[s][:], ALU.add))

            dve.wait_ge(once, 32)
            add_rows(0, 0, 0)
            with dve.Fori(0, LOOPS - 1) as j:
                for s in slots:
                    tile(s, j * 2 + s, j, True)
            tile(0, NT - 2, LOOPS - 1, True)
            tile(1, NT - 1, LOOPS - 1, False)

        @block.tensor
        def _(pe):
            pe.wait_ge(once, 32)
            with pe.Fori(0, LOOPS) as j:
                for s in slots:
                    i = j * 2 + s
                    pe.wait_ge(loaded[s], j * 32 + 32)
                    for n in range(NP):
                        last = nc.tensor.transpose(pp[:, n * P:(n + 1) * P], pt[s][:, n * P:(n + 1) * P], k.ident[:])
                    last.then_inc(pes, 1)
                    pe.wait_ge(added, R(f"r{TOP_K - 1}", i))
                    for n in range(ND):
                        last = nc.tensor.transpose(tp[:, n * P:(n + 1) * P], ht[s][:, n * P:(n + 1) * P], k.ident[:])
                    last.then_inc(pes, 1)
                    pe.wait_ge(acts, A("pT", i))
                    for h in range(2):
                        for n in range(NP):
                            last = nc.tensor.matmul(ep[:, h * HALF:(h + 1) * HALF], pT[s][:, n, :],
                                                    wp[:, n, h * HALF:(h + 1) * HALF], start=(n == 0), stop=(n == NP - 1))
                    last.then_inc(pes, 1)
                    pe.wait_ge(acts, A("hb", i))
                    pe.wait_ge(gate_loaded, 16)
                    for h in range(2):
                        for n in range(ND):
                            last = nc.tensor.matmul(gp[:, h * HALF:(h + 1) * HALF], hT[s][:, n, :],
                                                    wg[:, n, h * HALF:(h + 1) * HALF], start=(n == 0), stop=(n == ND - 1))
                    last.then_inc(pes, 1)


def build_layer(nc, x, p, norm_mix_g, w_in, rw_mu, rw_w0, rw_w2, rw_a0, rw_a2, rw_g2, rw_k_k, rw_k_a, rw_r_k,
                rw_ln_g, rw_ln_b, da_q_norm_g, da_k_norm_g, da_lq1, da_lk1, da_lq2, da_lk2, da_subln_g, w_out,
                norm_ffn_g, w_router, b_router, w1, b1, w2, b2, w_ple, ple_norm_g, w_ple_gate, out):
    scratch = lambda name, shape, dt=F32: nc.dram_tensor(name, shape, dt, kind="Internal").ap()
    zT = scratch("zT", [IN_COLS, T])
    ops = scratch("scan_ops", [2, C_RW, 4, T])
    vals = scratch("scan_vals", [C_RW, T])
    bonus = scratch("bonus", [C_RW, T])
    gate_in = scratch("gate_in", [P, T])
    end_decay = scratch("end_decay", [2, C_RW, NCH])
    y = scratch("scan_y", [2, T, C_RW])
    oT = scratch("mixed", [D, T])
    h1 = scratch("h1", [T, D])
    m = scratch("ffn_in", [T, D])
    row_token = scratch("row_token", [ROWS, 1], U32)
    yb = scratch("expert_out", [ROWS, D])
    biases = scratch("biases", [EXPERTS, PARTS, 2 * D_FF + D], BF16)
    flat = lambda ap: ap.rearrange("h n -> (h n)")
    x, p, out = x[0], p[0, 0], out[0]
    with ExitStack() as ctx:
        sb = lambda name, shape, dt=F32: ctx.enter_context(nc.sbuf_tensor(name, shape, dt))

        class k:
            ident = sb("ident", [P, P])
            eps = sb("eps", [P, 3])

        gates = sb("gates", [P, NT, TOP_K])
        row_of = sb("row_of", [P, NT * TOP_K], U32)
        table = sb("table", [P, 3, EXPERTS], I32)
        with ExitStack() as early:
            sb = lambda name, shape, dt=F32: early.enter_context(nc.sbuf_tensor(name, shape, dt))
            k.ones, k.head_ones, k.before = (sb(n, [P, P]) for n in ("ones", "head_ones", "before"))
            k.zeros = sb("zeros", [P, D])
            k.causal = sb("causal", [P, 2, 4, P])
            k.near = sb("near", [P, 3, P])
            k.chunk_col = sb("chunk_col", [P, 2])
            k.scan_keep = sb("scan_keep", [P, T])
            chosen = sb("chosen", [P, NT, TOP_K, EXPERTS])
            constants(nc, k, b1[0], b2[0], biases)
            with nc.sbuf_tensor("u_high", [P, ND, T], F32R) as u_high, nc.sbuf_tensor("u_rest", [P, ND, T], F32R) as u_rest:
                normed_columns(nc, k, x, norm_mix_g[0], u_high, u_rest)
                project_in(nc, k, u_high, u_rest, w_in[0], zT)
            rwkv_prepare(nc, k, zT, rw_mu[0], rw_w0[0], rw_w2[0], rw_a0[0], rw_a2[0], rw_k_k[0], rw_k_a[0],
                         flat(rw_r_k[0]), ops, vals, bonus, gate_in, end_decay)
            rwkv_scan(nc, k, ops, vals, end_decay, y, yb)
            differential_attention(nc, k, zT, da_q_norm_g[0], da_k_norm_g[0], da_lq1[0], da_lk1[0], da_lq2[0],
                                   da_lk2[0], da_subln_g[0], oT)
            with nc.sbuf_tensor("wo", [P, ND, D], F32) as wo, nc.semaphore("wo_loaded") as wo_loaded:
                finish_rwkv(nc, k, y, bonus, gate_in, rw_g2[0], flat(rw_ln_g[0]), flat(rw_ln_b[0]), oT,
                            w_out[0], wo, wo_loaded)
                mix_out_and_route(nc, k, x, oT, wo, wo_loaded, norm_ffn_g[0], w_router[0], b_router[0], h1, m,
                                  chosen, gates)
            place_rows(nc, k, chosen, row_of, table, row_token)
        expert_rows(nc, k, m, row_of, row_token, table, w1[0], w2[0], biases, yb)
        finish(nc, k, h1, yb, row_of, gates, p, w_ple[0], ple_norm_g[0], w_ple_gate[0], out)


INPUTS = ("x p norm_mix_g w_in rw_mu rw_w0 rw_w2 rw_a0 rw_a2 rw_g2 rw_k_k rw_k_a rw_r_k rw_ln_g rw_ln_b "
          "da_q_norm_g da_k_norm_g da_lq1 da_lk1 da_lq2 da_lk2 da_subln_g w_out norm_ffn_g w_router b_router "
          "w1 b1 w2 b2 w_ple ple_norm_g w_ple_gate").split()


def kernel(**inputs):
    import numpy as np
    import concourse.bacc as bacc
    from concourse.bass_utils import run_bass_kernel_spmd

    nc = bacc.Bacc("TRN2", target_bir_lowering=False, num_devices=1)
    arrays, args = {}, []
    for name in INPUTS:
        a = np.ascontiguousarray(inputs[name])
        arrays[f"in_{name}"] = a
        args.append(nc.dram_tensor(f"in_{name}", a.shape, mybir.dt.from_np(a.dtype), kind="ExternalInput").ap())
    args.append(nc.dram_tensor("out_h", (1, T, D), F32, kind="ExternalOutput").ap())
    build_layer(nc, *args)
    r = run_bass_kernel_spmd(nc, [arrays], core_ids=[0])
    return r.results[0]["out_h"]
```
